# Optimizing a Trainium2 kernel written in Bass

```python
import math
import jax, jax.numpy as jnp
from jax import lax
import numpy as np

D_MODEL = 1024
BATCH = 1
SEQ = 256
DEPTH = 1

CHUNK = 64
GM_CHUNK = 128
GM_HEADS = 8
GM_WIDTH = D_MODEL
GM_HD = GM_WIDTH // GM_HEADS
HEAD_DIM = 64
N_Q_HEADS = D_MODEL // HEAD_DIM
N_KV_HEADS = 2
GQ = N_Q_HEADS // N_KV_HEADS
WINDOW = 128
WINDOW_CHUNKS = WINDOW // CHUNK
ROPE_THETA = 500000.0
ROT_DIM = HEAD_DIM // 4
Q_W = N_Q_HEADS * HEAD_DIM
KV_W = N_KV_HEADS * HEAD_DIM
OFF_U = 0
OFF_V = OFF_U + GM_WIDTH
OFF_Q = OFF_V + GM_WIDTH
OFF_K = OFF_Q + Q_W
OFF_VV = OFF_K + KV_W
OFF_GA = OFF_VV + KV_W
OFF_GB = OFF_GA + D_MODEL
IN_W = OFF_GB + D_MODEL
N_EXPERTS = 32
TOP_K = 4
D_FF = D_MODEL
SWIGLU_ALPHA = 1.702
SWIGLU_LIMIT = 7.0
MOE_BLOCK = 128
EPS = 1e-5

kernel_name = "hybrid_gmlp_swa_sink_moe_adaln"

def rms_norm(x, g):
    xf = x.astype(jnp.float32)
    y = xf * lax.rsqrt(jnp.mean(xf * xf, axis=-1, keepdims=True) + EPS)
    return (y * g.astype(jnp.float32)).astype(x.dtype)

def layer_norm(x, g, b):
    xf = x.astype(jnp.float32)
    mu = jnp.mean(xf, axis=-1, keepdims=True)
    var = jnp.mean(jnp.square(xf - mu), axis=-1, keepdims=True)
    y = (xf - mu) * lax.rsqrt(var + EPS)
    return (y * g.astype(jnp.float32) + b.astype(jnp.float32)).astype(x.dtype)

def partial_rope(t, cos, sin):
    half = ROT_DIM // 2
    t1 = t[..., :half]
    t2 = t[..., half:ROT_DIM]
    return jnp.concatenate([t1 * cos - t2 * sin, t2 * cos + t1 * sin, t[..., ROT_DIM:]], axis=-1)

def gmlp_spatial(u, v, ln_g, ln_b, w_s, b_s):
    b, s, _ = u.shape
    ng = s // GM_CHUNK
    vn = layer_norm(v, ln_g, ln_b)
    pos_chunk = jnp.arange(GM_CHUNK) // CHUNK
    mask = (pos_chunk[None, :] <= pos_chunk[:, None]).astype(w_s.dtype)
    vg = vn.reshape(b, ng, GM_CHUNK, GM_HEADS, GM_HD)
    f = jnp.einsum('hij,bnjhc->bnihc', w_s * mask[None], vg)
    f = f + b_s.T[None, None, :, :, None]
    return (u.reshape(b, ng, GM_CHUNK, GM_HEADS, GM_HD) * f).reshape(b, s, GM_WIDTH)

def shift_chunks(t, d):
    if d == 0:
        return t
    return jnp.concatenate([jnp.zeros_like(t[:, :d]), t[:, :-d]], axis=1)

def swa_sink_attention(q, k, v, sinks):
    b, s = q.shape[0], q.shape[1]
    nc = s // CHUNK
    qc = q.reshape(b, nc, CHUNK, N_KV_HEADS, GQ, HEAD_DIM)
    kc = k.reshape(b, nc, CHUNK, N_KV_HEADS, HEAD_DIM)
    vc = v.reshape(b, nc, CHUNK, N_KV_HEADS, HEAD_DIM)
    shifts = [WINDOW_CHUNKS - 1 - m for m in range(WINDOW_CHUNKS)]
    kb = jnp.concatenate([shift_chunks(kc, d) for d in shifts], axis=2)
    vb = jnp.concatenate([shift_chunks(vc, d) for d in shifts], axis=2)
    scores = jnp.einsum('bnihgd,bnjhd->bnhgij', qc, kb).astype(jnp.float32)
    scores = scores * (1.0 / math.sqrt(HEAD_DIM))
    chunk_idx = jnp.arange(nc)[:, None]
    key_shift = jnp.repeat(jnp.array(shifts, dtype=jnp.int32), CHUNK)[None, :]
    valid = chunk_idx >= key_shift
    scores = jnp.where(valid[None, :, None, None, None, :], scores, -jnp.inf)
    sink = sinks.astype(jnp.float32).reshape(N_KV_HEADS, GQ)[None, None, :, :, None, None]
    sink = jnp.broadcast_to(sink, scores.shape[:-1] + (1,))
    p = jax.nn.softmax(jnp.concatenate([scores, sink], axis=-1), axis=-1)[..., :-1]
    o = jnp.einsum('bnhgij,bnjhd->bnihgd', p.astype(v.dtype), vb)
    return o.reshape(b, s, N_Q_HEADS * HEAD_DIM)

def moe_ffn(h, w_router, b_router, w_gate_up, b_gate_up, w_down, b_down):
    n, d = h.shape
    logits = (h @ w_router + b_router).astype(jnp.float32)
    top_v, top_e = lax.top_k(logits, TOP_K)
    gate = jax.nn.softmax(top_v, axis=-1)
    a = n * TOP_K
    flat_e = top_e.reshape(-1).astype(jnp.int32)
    flat_tok = jnp.arange(a, dtype=jnp.int32) // TOP_K
    flat_w = gate.reshape(-1)
    order = jnp.argsort(flat_e)
    se, stok, sw = flat_e[order], flat_tok[order], flat_w[order]
    counts = jnp.zeros((N_EXPERTS,), jnp.int32).at[flat_e].add(1)
    padded = (counts + MOE_BLOCK - 1) // MOE_BLOCK * MOE_BLOCK
    start = jnp.cumsum(counts) - counts
    pend = jnp.cumsum(padded)
    pstart = pend - padded
    dest = pstart[se] + jnp.arange(a, dtype=jnp.int32) - start[se]
    n_blocks = -(-a // MOE_BLOCK) + N_EXPERTS
    n_slots = n_blocks * MOE_BLOCK
    slot_tok = jnp.full((n_slots,), n, jnp.int32).at[dest].set(stok)
    slot_w = jnp.zeros((n_slots,), jnp.float32).at[dest].set(sw)
    block_e = jnp.searchsorted(pend, jnp.arange(n_blocks, dtype=jnp.int32) * MOE_BLOCK, side='right')
    block_e = jnp.minimum(block_e, N_EXPERTS - 1).astype(jnp.int32)
    h_pad = jnp.concatenate([h, jnp.zeros((1, d), h.dtype)], axis=0)
    xb = h_pad[slot_tok].reshape(n_blocks, MOE_BLOCK, d)

    def expert_block(args):
        xblk, e = args
        gu = xblk @ w_gate_up[e] + b_gate_up[e]
        g = jnp.minimum(gu[:, :D_FF], SWIGLU_LIMIT)
        u = jnp.clip(gu[:, D_FF:], -SWIGLU_LIMIT, SWIGLU_LIMIT)
        hid = g * jax.nn.sigmoid(SWIGLU_ALPHA * g) * (u + 1.0)
        return hid @ w_down[e] + b_down[e]

    yb = lax.map(expert_block, (xb, block_e)).reshape(n_slots, d)
    out = jnp.zeros((n + 1, d), yb.dtype).at[slot_tok].add(yb * slot_w[:, None].astype(yb.dtype))
    return out[:n].astype(h.dtype)

def setup_inputs(seed: int = 0) -> dict:
    key = jax.random.key(seed)
    ks = jax.random.split(key, 24)
    f32 = jnp.float32
    L, D = DEPTH, D_MODEL

    def nrm(k, shape, scale):
        return jax.random.normal(k, shape, f32) * scale

    x = jax.random.normal(ks[0], (BATCH, SEQ, D), f32)
    c = jax.random.normal(ks[1], (BATCH, D), f32)
    offset = jax.random.randint(ks[2], (BATCH, 1), 0, 4096, dtype=jnp.int32)
    positions = offset + jnp.arange(SEQ, dtype=jnp.int32)[None, :]
    return {
        "x": x,
        "c": c,
        "positions": positions,
        "w_ada": nrm(ks[3], (L, D, 6 * D), D ** -0.5),
        "b_ada": nrm(ks[4], (L, 6 * D), 0.02),
        "g_norm1": 1.0 + nrm(ks[5], (L, D), 0.05),
        "w_in": nrm(ks[6], (L, D, IN_W), D ** -0.5),
        "b_in": nrm(ks[7], (L, IN_W), 0.02),
        "ln_v_g": 1.0 + nrm(ks[8], (L, GM_WIDTH), 0.05),
        "ln_v_b": nrm(ks[9], (L, GM_WIDTH), 0.02),
        "w_spatial": nrm(ks[10], (L, GM_HEADS, GM_CHUNK, GM_CHUNK), 0.5 * GM_CHUNK ** -0.5),
        "b_spatial": 1.0 + nrm(ks[11], (L, GM_HEADS, GM_CHUNK), 0.05),
        "sinks": nrm(ks[12], (L, N_Q_HEADS), 1.0),
        "w_o_a": nrm(ks[13], (L, GM_WIDTH, D), GM_WIDTH ** -0.5),
        "w_o_b": nrm(ks[14], (L, Q_W, D), Q_W ** -0.5),
        "w_out": nrm(ks[15], (L, D, D), D ** -0.5),
        "g_norm2": 1.0 + nrm(ks[16], (L, D), 0.05),
        "w_router": nrm(ks[17], (L, D, N_EXPERTS), D ** -0.5),
        "b_router": nrm(ks[18], (L, N_EXPERTS), 0.01),
        "w_gate_up": nrm(ks[19], (L, N_EXPERTS, D, 2 * D_FF), D ** -0.5),
        "b_gate_up": nrm(ks[20], (L, N_EXPERTS, 2 * D_FF), 0.02),
        "w_down": nrm(ks[21], (L, N_EXPERTS, D_FF, D), D_FF ** -0.5),
        "b_down": nrm(ks[22], (L, N_EXPERTS, D), 0.02),
        "g_final": 1.0 + nrm(ks[23], (D,), 0.05),
    }

def reference(x, c, positions, w_ada, b_ada, g_norm1, w_in, b_in, ln_v_g, ln_v_b,
              w_spatial, b_spatial, sinks, w_o_a, w_o_b, w_out, g_norm2, w_router,
              b_router, w_gate_up, b_gate_up, w_down, b_down, g_final):
    b, s, d = x.shape
    inv_freq = ROPE_THETA ** (-jnp.arange(0, ROT_DIM, 2, dtype=jnp.float32) / ROT_DIM)
    ang = positions.astype(jnp.float32)[..., None] * inv_freq
    cos = jnp.cos(ang)[:, :, None, :].astype(x.dtype)
    sin = jnp.sin(ang)[:, :, None, :].astype(x.dtype)
    c_act = jax.nn.silu(c)

    for l in range(DEPTH):
        mod = c_act @ w_ada[l] + b_ada[l]
        sh1, sc1, gt1, sh2, sc2, gt2 = [m[:, None, :] for m in jnp.split(mod, 6, axis=-1)]

        h = rms_norm(x, g_norm1[l]) * (1.0 + sc1) + sh1
        z = h @ w_in[l] + b_in[l]
        uv = jax.nn.gelu(z[..., OFF_U:OFF_Q], approximate=False)
        ya = gmlp_spatial(uv[..., :GM_WIDTH], uv[..., GM_WIDTH:], ln_v_g[l], ln_v_b[l],
                          w_spatial[l], b_spatial[l])
        q = z[..., OFF_Q:OFF_K].reshape(b, s, N_Q_HEADS, HEAD_DIM)
        k = z[..., OFF_K:OFF_VV].reshape(b, s, N_KV_HEADS, HEAD_DIM)
        vv = z[..., OFF_VV:OFF_GA].reshape(b, s, N_KV_HEADS, HEAD_DIM)
        yb = swa_sink_attention(partial_rope(q, cos, sin), partial_rope(k, cos, sin), vv, sinks[l])
        gate_a = jax.nn.sigmoid(z[..., OFF_GA:OFF_GB])
        gate_b = jax.nn.sigmoid(z[..., OFF_GB:IN_W])
        merged = gate_a * (ya @ w_o_a[l]) + gate_b * (yb @ w_o_b[l])
        x = x + gt1 * (merged @ w_out[l])

        h2 = rms_norm(x, g_norm2[l]) * (1.0 + sc2) + sh2
        y2 = moe_ffn(h2.reshape(b * s, d), w_router[l], b_router[l], w_gate_up[l],
                     b_gate_up[l], w_down[l], b_down[l]).reshape(b, s, d)
        x = x + gt2 * y2

    return rms_norm(x, g_final)


_drawn_inputs = setup_inputs


def setup_inputs(seed=0):
    import zlib

    import numpy as np

    out = dict(_drawn_inputs(seed))
    spreads = {}
    factors = {'ln_v_g': 2.93,
     'ln_v_b': 5.54,
     'sinks': 4.646,
     'b_router': 2.68,
     'b_gate_up': 6.557,
     'b_down': 8.0}
    for name, (base, spread) in spreads.items():
        noise = np.random.default_rng([zlib.crc32(name.encode()), seed]).standard_normal(out[name].shape)
        drawn = base * np.exp(spread * noise) if base else spread * noise
        out[name] = __import__('jax').numpy.asarray(drawn.astype(out[name].dtype))
    for name, factor in factors.items():
        out[name] = (out[name] * factor).astype(out[name].dtype)
    return out
```

```python
from contextlib import ExitStack
import math

import numpy as np
import concourse.bass as bass
from concourse import mybir

F32 = mybir.dt.float32
I32 = mybir.dt.int32
ALU = mybir.AluOpType
ACT = mybir.ActivationFunctionType
AX = mybir.AxisListType

P = 128
D = 1024
S = 256
TILES = S // P
KC = D // P
COLS = 512
H = 8
CH = 64
NCH = S // CH
NQ = 16
NKV = 2
HALF = 8
THETA = 500000.0
IN_W = 5376
E = 32
TOPK = 4
FF = 1024
ALPHA = 1.702
LIMIT = 7.0
EPS = 1e-5
BM = 32
NQT = P // BM
QW = D // NQT
GMAX = 64
BIG = 12582912.0

EVENTS = ("acc_init", "ada_added", "ada_made", "angle_ready", "c_act_ready", "cmp_ready", "comb_done",
          "consts", "counters", "counts_ready", "crep_ready", "down_done", "ex_ready", "exp_done",
          "gT_ready", "g_ready", "gates_ready", "gt_done", "gu_done", "h2_ready", "hidT_ready",
          "hid_ready", "hot_ready", "ht_done", "mask_ready", "merged_ready", "modT_done", "mod_col_ready",
          "negm_ready", "negtop_ready", "next_ready", "now_ready", "out_ready", "p_norm", "pool_steps",
          "prod_ready", "rope_ready", "s_done", "sel_ready", "selg_ready", "sig_done", "sig_ready",
          "slots_ready", "ssq_ready", "std_ready", "table_ready", "trig_ready", "u_gelu", "u_ready",
          "v_gelu", "var_ready", "vec_steps", "vn_ready", "vp_ready", "ws_masked", "x2_ready", "xT_ready",
          "xe_ready", "xg_done", "xn_ready", "xt_done", "y2_ready", "y_ready")


def bass_hybrid_layer(nc, x, c, positions, w_ada, b_ada, g_norm1, w_in, b_in, ln_v_g, ln_v_b,
                      w_spatial, b_spatial, sinks, w_o_a, w_o_b, w_out, g_norm2, w_router,
                      b_router, w_gate_up, b_gate_up, w_down, b_down, g_final, out):
    RING = 3
    items = []
    for j in range(4):
        items.append((f"ada{j}", w_ada[0, :, j * COLS:(j + 1) * COLS], None))
    OFF_V, OFF_Q, OFF_K, OFF_GA, OFF_GB = 1024, 2048, 3072, 3328, 4352
    for name, off, w in [("v0", OFF_V, 512), ("v1", OFF_V + 512, 512), ("u0", 0, 512), ("u1", 512, 512),
                         ("q0", OFF_Q, 512), ("q1", OFF_Q + 512, 512), ("kv", OFF_K, 256),
                         ("ga0", OFF_GA, 512), ("ga1", OFF_GA + 512, 512),
                         ("gb0", OFF_GB, 512), ("gb1", OFF_GB + 512, 512)]:
        items.append((name, w_in[0, :, off:off + w], b_in[0:1, off:off + w]))
    for name, w in [("oa", w_o_a), ("ob", w_o_b)]:
        for j in range(2):
            items.append((f"{name}{j}", w[0, :, j * COLS:(j + 1) * COLS], None))
    for j in range(4, 12):
        items.append((f"ada{j}", w_ada[0, :, j * COLS:(j + 1) * COLS], None))
    for j in range(2):
        items.append((f"out{j}", w_out[0, :, j * COLS:(j + 1) * COLS], None))
    names = [n for n, _, _ in items]
    biased = [n for n, _, b in items if b is not None]

    def ring_slot(name):
        n = names.index(name)
        return n % RING, 16 * (n // RING + 1)

    z_order = [f"xT{t}{h}" for t in range(TILES) for h in range(2)]
    for n in ["v0", "v1", "u0", "u1", "q0", "q1", "kv"]:
        z_order += [f"{n}t{t}" for t in range(TILES)]
        if n == "u1":
            z_order += [f"f{t}{h}" for t in range(TILES) for h in range(2)]
    for n in ["ga0", "ga1", "gb0", "gb1", "oa0", "oa1", "ob0", "ob1"]:
        z_order += [f"{n}t{t}" for t in range(TILES)]
    z_order += [f"bc{s}{h}" for s in (2, 3, 4, 5) for h in range(2)]
    z_order += [f"out{j}t{t}" for j in range(2) for t in range(TILES)]
    z_order += ["logits", "rank", "starts", "etab"]
    t_order = ["ws0", "ws1"]
    t_order += [f"ya{t}{h}" for t in range(TILES) for h in range(2)]
    t_order += [f"q{t}{h}" for t in range(TILES) for h in range(2)] + ["k"]
    for n in range(NCH):
        t_order += [f"p{n}0", f"p{n}1", f"o{n}"]
    t_order += [f"m{t}{h}" for t in range(TILES) for h in range(2)]
    t_order += [f"h{t}{h}" for t in range(TILES) for h in range(2)] + ["gT"]

    ctx = ExitStack()
    with ctx:
        ctx.enter_context(nc.allow_non_contiguous_dma(reason="small columns"))

        def sb(name, shape, dt=F32):
            return ctx.enter_context(nc.sbuf_tensor(name, shape, dt))

        def sem(name):
            return ctx.enter_context(nc.semaphore(name))

        gate_up = [sb(f"gate_up{s}", [P, KC, 2 * FF]) for s in range(2)]
        down = sb("down", [P, KC, D])
        ring = gate_up[1][:, 0:6, :].rearrange("p (s a) (b n) -> p s (a b) n", s=RING, n=COLS)
        spare = gate_up[1][:, 6:8, :].rearrange("p a b -> p (a b)")
        hT = down[:, 0:2, :].rearrange("p a (b n) -> p (a b) n", n=S)
        v_buf = down[:, 2:4, :]
        u_buf = down[:, 4:6, :]
        q_buf = down[:, 6:8, :]

        def as_T(buf):
            return buf.rearrange("p a (b n) -> p (a b) n", n=S)

        ws = spare[:, 0:1024].rearrange("p (h n) -> p h n", h=H)
        probs = spare[:, 0:1024].rearrange("p (r g n) -> p r g n", r=2, g=4)
        wsT = spare[:, 1024:2048].rearrange("p (h n) -> p h n", h=H)
        probsT = spare[:, 2048:3072].rearrange("p (r g n) -> p r g n", r=2, g=4)
        row_sel = spare[:, 3072:3584].rearrange("p (q n) -> p q n", q=NQT)
        tri = spare[:, 3584:3712]
        ones = spare[:, 3712:3840]
        wr = spare[:, 3840:4096].rearrange("p (k e) -> p k e", k=KC)

        x_sb = sb("x_sb", [P, TILES, D])
        h2 = sb("h2", [P, TILES, D])
        ln_gb = h2
        gt2 = sb("gt2", [P, D])
        bias_ring = gt2[:, :].rearrange("p (s n) -> p s n", s=2)
        front = sb("front", [P, 4 * D])
        sig_a = front[:, 0:2048].rearrange("p (t n) -> p t n", t=TILES)
        sig_b = front[:, 2048:4096].rearrange("p (t n) -> p t n", t=TILES)
        gt1 = front[:, 0:1024]
        mul2 = front[:, 1024:2048]
        sh2 = front[:, 2048:3072]
        g2bc = front[:, 3072:4096]
        mod = sb("mod", [P, 12, P])
        exp_bias = sb("exp_bias", [P, 2 * QW])
        kv = exp_bias[:, :].rearrange("p (t n) -> p t n", t=TILES)
        kT = mod[:, 4:8, :].rearrange("p a b -> p (a b)").rearrange("p (g n) -> p g n", g=NKV)
        kd = mod[:, 8:12, :].rearrange("p a b -> p (a b)").rearrange("p (t g u d) -> p t g u d", t=TILES, g=NKV, u=2)
        vp = spare[:, 1920:2048]
        rope_room = spare[:, 1024:1536]
        b_down_sb = mod[0:E, 0:8, :].rearrange("p a b -> p (a b)")
        crep = sb("crep", [P, KC, BM])
        ident = sb("ident", [P, P])

        at = [0]

        def cut(n):
            at[0] += n
            return front[:, at[0] - n:at[0]]

        def by_tile(ap):
            return ap.rearrange("p (t n) -> p t n", t=TILES)
        iota4 = cut(P).rearrange("p (q j) -> p q j", q=NQT)
        iota_g = cut(GMAX)
        slot_base = cut(GMAX)
        block_hot = cut(GMAX)
        slots_gates = cut(4 * E).rearrange("p (e n) -> p e n", n=4)
        tri_inc = cut(P)[0:E, :]
        tri_exc = cut(P)[0:E, :]
        sel = by_tile(cut(TILES * BM))
        selg = by_tile(cut(TILES * P))
        onehot = cut(BM)
        xe = cut(QW)
        xT = cut(2 * P).rearrange("p (i n) -> p i n", i=2)
        gT = cut(TILES * P)
        router_at = at[0]
        g_cap, g_sig, u_cap, gu_prod, hid = (cut(QW) for _ in range(5))
        hidT = cut(2 * P).rearrange("p (i n) -> p i n", i=2)
        y_sb = cut(QW)
        slot_next, slot_now = cut(TILES), cut(TILES)
        assert at[0] <= 4 * D
        at[0] = router_at
        lg, lrep, mask, ex, gates, dtmp = (by_tile(cut(TILES * E)) for _ in range(6))
        top8 = by_tile(cut(TILES * 8))
        negtop, esum = cut(TILES), cut(TILES)
        nbB, stB, enB = cut(E), cut(E), cut(E)
        nbT = cut(P)[0:E, :]
        gatesT = by_tile(cut(TILES * P))[0:E]
        block_e, cmp = cut(GMAX), cut(GMAX)
        ncol = cut(4)
        assert at[0] <= router_at + 6 * QW
        table = sb("table", [1, GMAX + 3 * E], I32)

        sm = sb("sm", [P, 320])
        cat = [0]

        def col(n):
            cat[0] += n
            assert cat[0] <= 320
            return sm[:, cat[0] - n:cat[0]]
        c_col, c_act = col(KC), col(KC)
        g1_col = col(KC)
        mod_col = col(2 * KC).rearrange("p (s k) -> p s k", s=2)
        mul1 = col(KC)
        ssq, var, rstd, nt = col(TILES), col(TILES), col(TILES), col(TILES)
        stats = col(TILES * 12).rearrange("p (t n s) -> p t n s", t=TILES, n=2)
        mv = col(TILES * 2).rearrange("p (t s) -> p t s", t=TILES)
        bs = col(H)
        pos_f = col(TILES)
        invf = col(HALF)
        ang = col(TILES * HALF).rearrange("p (t f) -> p t f", t=TILES)
        kf = col(TILES * HALF).rearrange("p (t f) -> p t f", t=TILES)
        cos = col(TILES * HALF).rearrange("p (t f) -> p t f", t=TILES)
        sin = col(TILES * HALF).rearrange("p (t f) -> p t f", t=TILES)
        sk = col(8).rearrange("p (r g) -> p r g", r=2)
        mx = col(8).rearrange("p (r g) -> p r g", r=2)
        negm = col(8).rearrange("p (r g) -> p r g", r=2)
        den = col(8).rearrange("p (r g) -> p r g", r=2)
        es = col(8).rearrange("p (r g) -> p r g", r=2)
        br = col(E)
        pos_i = sb("pos_i", [P, TILES], I32)
        banks = [ctx.enter_context(nc.psum_tensor(f"bank{i}", [P, COLS], F32)) for i in range(8)]
        NZ = 4

        x_in, cond_in, gmlp_in, attn_in, route_in = (sem(n) for n in ("x_in", "cond_in", "gmlp_in", "attn_in", "route_in"))
        ln_in, g2_in, gf_in, bd_in, stored = (sem(n) for n in ("ln_in", "g2_in", "gf_in", "bd_in", "stored"))
        exp_bias_in = sem("exp_bias_in")
        ring_in = [sem(f"ring_in{i}") for i in range(RING)]
        bias_in = [sem(f"bias_in{i}") for i in range(2)]
        z_full = [sem(f"z_full{i}") for i in range(NZ)]
        z_free = [sem(f"z_free{i}") for i in range(NZ)]
        t_full = [sem(f"t_full{i}") for i in range(2)]
        t_free = [sem(f"t_free{i}") for i in range(2)]
        gu_in = [[sem(f"gu_in{s}_{i}") for i in range(4)] for s in range(2)]
        dn_in = [sem(f"dn_in{i}") for i in range(4)]
        evs = {}

        def ev(name):
            if name not in evs:
                evs[name] = sem(name)
            return evs[name]

        def z_use(name):
            k = z_order.index(name)
            return k % NZ, k // NZ + 1

        def t_use(name):
            k = t_order.index(name)
            return k % 2, k // 2 + 1

        def z_wait(eng, name):
            b, n = z_use(name)
            eng.wait_ge(z_full[b], n)
            return banks[b]

        def t_wait(eng, name):
            b, n = t_use(name)
            eng.wait_ge(t_full[b], n)
            return banks[6 + b]

        def z_gone(eng, name):
            b, n = z_use(name)
            eng.wait_ge(z_free[b], n)

        def t_gone(eng, name):
            b, n = t_use(name)
            eng.wait_ge(t_free[b], n)

        def item_used(eng, name):
            if name.startswith("ada"):
                eng.wait_ge(ev("ada_made"), int(name[3:]) + 1)
            else:
                z_wait(eng, name + "t1")

        def z_done(ins, name):
            ins.then_inc(z_free[z_use(name)[0]], 1)

        def t_done(ins, name):
            ins.then_inc(t_free[t_use(name)[0]], 1)

        for n in EVENTS:
            ev(n)
        block = ctx.enter_context(nc.Block())

        yaT, ybT, mT, h2T = as_T(v_buf), as_T(q_buf), hT, as_T(v_buf)
        qT = u_buf.rearrange("p a (c k q) -> p (a c) k q", c=2, q=CH)
        merged = u_buf

        w_gu_view = w_gate_up[0].rearrange("e (k p) n -> p e k n", p=P)
        w_dn_view = w_down[0].rearrange("e (k p) n -> p e k n", p=P)

        def load_gate_up(eng, e, s):
            for i in range(4):
                eng.dma_start(gate_up[s][:, 2 * i:2 * i + 2, :],
                              w_gu_view[:, bass.ds(e, 1), 2 * i:2 * i + 2, :].rearrange("p a k n -> p (a k) n"))\
                   .then_inc(gu_in[s][i], 16)

        def load_down(eng, e):
            for i in range(4):
                eng.dma_start(down[:, 2 * i:2 * i + 2, :],
                              w_dn_view[:, bass.ds(e, 1), 2 * i:2 * i + 2, :].rearrange("p a k n -> p (a k) n"))\
                   .then_inc(dn_in[i], 16)

        @block.sync
        def _(sp):
            sp.dma_start(x_sb[:, :, :], x[0].rearrange("(t p) d -> p t d", p=P)).then_inc(x_in, 16)
            nb = 0
            prefetch = ("u1", "q1", "ga0", "ga1")
            for n, (name, w, b) in enumerate(items):
                if n >= RING:
                    item_used(sp, names[n - RING])
                cols = w.shape[1]
                sp.dma_start(ring[:, n % RING, :, 0:cols],
                             w.rearrange("(k p) n -> p k n", p=P)).then_inc(ring_in[n % RING], 16)
                if b is not None:
                    if nb >= 2:
                        z_gone(sp, biased[nb - 2] + "t1")
                    sp.dma_start(bias_ring[:, nb % 2, 0:cols],
                                 b.to_broadcast([P, cols])).then_inc(bias_in[nb % 2], 16)
                    nb += 1
                if name in prefetch:
                    i = prefetch.index(name)
                    sp.dma_start(gate_up[0][:, 2 * i:2 * i + 2, :],
                                 w_gu_view[:, 0, 2 * i:2 * i + 2, :]).then_inc(gu_in[0][i], 16)
            item_used(sp, "out1")
            for i in range(3):
                sp.dma_start(gate_up[1][:, 2 * i:2 * i + 2, :],
                             w_gu_view[:, 1, 2 * i:2 * i + 2, :]).then_inc(gu_in[1][i], 16)
            sp.wait_ge(z_full[z_use("logits")[0]], z_use("logits")[1])
            load_down(sp, 0)
            sp.wait_ge(ev("table_ready"), 1)
            sp.wait_ge(ev("slots_ready"), 1)
            sp.dma_start(gate_up[1][:, 6:8, :], w_gu_view[:, 1, 6:8, :]).then_inc(gu_in[1][3], 16)

            end = sp.value_load(table[0:1, GMAX + 2 * E:GMAX + 2 * E + 1], min_val=1, max_val=63)
            sp.wait_ge(ev("down_done"), end)
            load_down(sp, 1)
            with sp.Fori(1, E // 2) as p:
                for s in range(2):
                    e = p * 2 + s
                    end = sp.value_load(table[0:1, bass.ds(p * 2 + (s - 2 + GMAX + 2 * E), 1)], min_val=1, max_val=63)
                    sp.wait_ge(ev("gu_done"), end)
                    load_gate_up(sp, e, s)
                    end = sp.value_load(table[0:1, bass.ds(p * 2 + (s - 1 + GMAX + 2 * E), 1)], min_val=1, max_val=63)
                    sp.wait_ge(ev("down_done"), end)
                    load_down(sp, e)
            end = sp.value_load(table[0:1, GMAX + 2 * E + 30:GMAX + 2 * E + 31], min_val=1, max_val=63)
            sp.wait_ge(ev("gu_done"), end)
            sp.dma_start(gate_up[0][:, 0, 0:D], g_final.rearrange("(a d) -> a d", a=1).to_broadcast([P, D]))\
              .then_inc(gf_in, 16)
            for t in range(TILES):
                sp.wait_ge(ev("out_ready"), t + 1)
                sp.dma_start(out[0, t * P:(t + 1) * P, :], h2[:, t, :]).then_inc(stored, 16)
            sp.wait_ge(stored, 16 * TILES)

        @block.gpsimd
        def _(pool):
            pool.memset(ident[:, :], 0.0).then_inc(ev("pool_steps"), 1)
            pool.memset(tri, 1.0).then_inc(ev("pool_steps"), 1)
            pool.memset(row_sel, 0.0).then_inc(ev("pool_steps"), 1)
            pool.memset(ones, 1.0).then_inc(ev("pool_steps"), 1)
            for f in range(HALF):
                pool.memset(invf[:, f:f + 1], float(np.float32(THETA ** (-f / HALF)))).then_inc(ev("pool_steps"), 1)
            pool.wait_ge(ev("pool_steps"), 4 + HALF)
            pool.affine_select(out=ident[:, :], in_=ident[:, :], compare_op=ALU.not_equal, fill=1.0, base=0,
                               pattern=[[-1, P]], channel_multiplier=1).then_inc(ev("consts"), 1)
            pool.affine_select(out=tri, in_=tri, compare_op=ALU.is_gt, fill=0.0, base=0,
                               pattern=[[1, P]], channel_multiplier=-1).then_inc(ev("consts"), 1)
            pool.affine_select(out=row_sel, in_=row_sel, compare_op=ALU.not_equal, fill=1.0, base=0,
                               pattern=[[-BM, NQT], [0, P]], channel_multiplier=1).then_inc(ev("consts"), 1)
            pool.wait_ge(gmlp_in, 32)
            pool.memset(ws[0:CH, :, CH:P], 0.0).then_inc(ev("ws_masked"), 1)
            pool.wait_ge(ev("h2_ready"), TILES)
            pool.iota(iota4, pattern=[[0, NQT], [1, BM]], base=0, channel_multiplier=0,
                      allow_small_or_imprecise_dtypes=True).then_inc(ev("counters"), 1)
            pool.iota(iota_g, pattern=[[1, GMAX]], base=0, channel_multiplier=0,
                      allow_small_or_imprecise_dtypes=True).then_inc(ev("counters"), 1)
            pool.iota(slot_base, pattern=[[BM, GMAX]], base=0, channel_multiplier=0,
                      allow_small_or_imprecise_dtypes=True).then_inc(ev("counters"), 1)
            pool.memset(tri_inc, 1.0).then_inc(ev("pool_steps"), 1)
            pool.memset(tri_exc, 1.0).then_inc(ev("pool_steps"), 1)
            pool.wait_ge(ev("pool_steps"), 6 + HALF)
            pool.affine_select(out=tri_inc, in_=tri_inc, compare_op=ALU.is_ge, fill=0.0, base=0,
                               pattern=[[0, NQT], [1, E]], channel_multiplier=-1).then_inc(ev("counters"), 1)
            pool.affine_select(out=tri_exc, in_=tri_exc, compare_op=ALU.is_gt, fill=0.0, base=0,
                               pattern=[[0, NQT], [1, E]], channel_multiplier=-1).then_inc(ev("counters"), 1)

        @block.scalar
        def _(act):
            act.dma_start(c_col, c[0].rearrange("(k p) -> p k", p=P)).then_inc(cond_in, 16)
            act.dma_start(g1_col, g_norm1[0].rearrange("(k p) -> p k", p=P)).then_inc(cond_in, 16)
            b_ada_rows = b_ada[0].rearrange("(j q n) -> q j n", j=12, q=NQT)

            def load_b_ada(j0, j1):
                for q in range(NQT):
                    act.dma_start(mod[q * BM:(q + 1) * BM, j0:j1, :],
                                  b_ada_rows[q:q + 1, j0:j1, :].to_broadcast([BM, j1 - j0, P])).then_inc(cond_in, 16)
            load_b_ada(0, 4)
            act.dma_start(ws, w_spatial[0].rearrange("h i j -> i h j")).then_inc(gmlp_in, 16)
            act.dma_start(bs, b_spatial[0].rearrange("h i -> i h")).then_inc(gmlp_in, 16)
            act.dma_start(pos_i[:, :], positions[0].rearrange("(t p) -> p t", p=P)).then_inc(attn_in, 16)
            for hh in range(2):
                for r in range(2):
                    act.dma_start(sk[hh * CH:(hh + 1) * CH, r, :],
                                  sinks[0:1, :].rearrange("a (g m) -> a m g", m=4)[:, 2 * hh + r, :].to_broadcast([CH, 4]))\
                       .then_inc(attn_in, 16)
            act.dma_start(wr, w_router[0].rearrange("(k p) e -> p k e", p=P)).then_inc(route_in, 16)
            act.dma_start(br, b_router[0:1, :].to_broadcast([P, E])).then_inc(route_in, 16)

            act.wait_ge(cond_in, 96)
            act.activation(c_act, c_col, ACT.Silu).then_inc(ev("c_act_ready"), 1)
            act.wait_ge(x_in, 16)
            for t in range(TILES):
                act.activation(q_buf[:, t, :], x_sb[:, t, :], ACT.Square, accum_out=ssq[:, t:t + 1])\
                   .then_inc(ev("ssq_ready"), 1)
            act.wait_ge(ev("var_ready"), 1)
            act.activation(rstd, var, ACT.Sqrt).then_inc(ev("std_ready"), 1)
            act.wait_ge(ev("mod_col_ready"), 2)
            for h in range(2):
                name = f"xT1{h}"
                bank = z_wait(act, name)
                for i in range(4):
                    k = 4 * h + i
                    last = act.activation(hT[:, k, P:2 * P], bank[:, i * P:(i + 1) * P], ACT.Identity,
                                          bias=mod_col[:, 0, k:k + 1], scale=mul1[:, k:k + 1])
                z_done(last, name)
            for t in range(TILES):
                z_wait(act, f"xT{t}1")
            act.dma_start(ln_gb[:, 0, :], ln_v_g[0:1, :].to_broadcast([P, D])).then_inc(ln_in, 16)
            act.dma_start(ln_gb[:, 1, :], ln_v_b[0:1, :].to_broadcast([P, D])).then_inc(ln_in, 16)
            for h in range(2):
                bank = t_wait(act, f"ws{h}")
                t_done(act.activation(wsT[:, 4 * h:4 * h + 4, :].rearrange("p h n -> p (h n)"), bank[:, :], ACT.Copy),
                       f"ws{h}")
            for j in range(2):
                for t in range(TILES):
                    z_gone(act, f"v{j}t{t}")
                    act.activation(v_buf[:, t, j * COLS:(j + 1) * COLS], v_buf[:, t, j * COLS:(j + 1) * COLS],
                                   ACT.Gelu).then_inc(ev("v_gelu"), 1)
            act.wait_ge(ev("var_ready"), 2)
            act.activation(rstd, var, ACT.Sqrt).then_inc(ev("std_ready"), 1)
            for j in range(2):
                for t in range(TILES):
                    z_gone(act, f"u{j}t{t}")
                    act.activation(u_buf[:, t, j * COLS:(j + 1) * COLS], u_buf[:, t, j * COLS:(j + 1) * COLS],
                                   ACT.Gelu).then_inc(ev("u_gelu"), 1)
            act.wait_ge(ev("angle_ready"), 1)
            act.activation(sin, ang, ACT.Sin).then_inc(ev("trig_ready"), 1)
            act.activation(cos, ang, ACT.Sin, scale=0.5).then_inc(ev("trig_ready"), 1)

            def copy_T(dst, kind):
                for t in range(TILES):
                    for h in range(2):
                        name = f"{kind}{t}{h}"
                        bank = t_wait(act, name)
                        t_done(act.activation(dst[:, 4 * h:4 * h + 4, t * P:(t + 1) * P],
                                              bank[:, :].rearrange("p (k n) -> p k n", k=4), ACT.Copy), name)
            copy_T(yaT, "ya")
            for t in range(TILES):
                for h in range(2):
                    name = f"q{t}{h}"
                    bank = t_wait(act, name)
                    t_done(act.activation(qT[:, 2 * t:2 * t + 2, 4 * h:4 * h + 4, :],
                                          bank[:, :].rearrange("p (k c q) -> p c k q", k=4, c=2), ACT.Copy), name)
            bank = t_wait(act, "k")
            t_done(act.activation(kT, bank[:, :].rearrange("p (g n) -> p g n", g=NKV), ACT.Copy), "k")
            for n in range(NCH):
                keys = CH if n == 0 else P
                act.wait_ge(ev("negm_ready"), n + 1)
                for r in range(2):
                    for g in range(4):
                        act.activation(probs[:, r, g, 0:keys], banks[4 + r][:, g * P:g * P + keys], ACT.Exp,
                                       bias=negm[:, r, g:g + 1], scale=1.0 / math.sqrt(CH),
                                       accum_out=den[:, r, g:g + 1]).then_inc(ev("exp_done"), 1)
                act.activation(es, es, ACT.Exp).then_inc(ev("exp_done"), 1)
                if n:
                    t_wait(act, f"o{n - 1}")
                for r in range(2):
                    name = f"p{n}{r}"
                    bank = t_wait(act, name)
                    t_done(act.activation(probsT[0:keys, r, :, :].rearrange("p g n -> p (g n)"), bank[0:keys, :],
                                          ACT.Copy), name)
            for sig, kind in ((sig_a, "ga"), (sig_b, "gb")):
                for t in range(TILES):
                    for j in range(2):
                        z_gone(act, f"{kind}{j}t{t}")
                    act.activation(sig[:, t, :], sig[:, t, :], ACT.Sigmoid).then_inc(ev("sig_done"), 1)
            act.wait_ge(ev("s_done"), NCH)
            load_b_ada(4, 12)
            z_gone(act, "kvt1")
            for n in range(NCH):
                t_wait(act, f"o{n}")
            b_gu_rows = b_gate_up[0].rearrange("e (a n) -> e a n", a=2)
            for q in range(NQT):
                act.dma_start(exp_bias[q * BM:(q + 1) * BM, :].rearrange("e (a n) -> e a n", a=2),
                              b_gu_rows[:, :, q * QW:(q + 1) * QW]).then_inc(exp_bias_in, 16)
            act.wait_ge(ev("merged_ready"), 2 * TILES)
            act.dma_start(g2bc, g_norm2[0:1, :].to_broadcast([P, D])).then_inc(g2_in, 16)
            copy_T(mT, "m")
            for name, dst in (("bc2", gt1), ("bc3", sh2)):
                for h in range(2):
                    bank = z_wait(act, f"{name}{h}")
                    z_done(act.activation(dst[:, h * COLS:(h + 1) * COLS], bank[:, :], ACT.Copy), f"{name}{h}")
            for h in range(2):
                bank = z_wait(act, f"bc5{h}")
                z_done(act.activation(gt2[:, h * COLS:(h + 1) * COLS], bank[:, :], ACT.Copy), f"bc5{h}")
            z_wait(act, "bc51")
            act.dma_start(b_down_sb, b_down[0]).then_inc(bd_in, 16)
            for t in range(TILES):
                act.wait_ge(ev("x2_ready"), t + 1)
                act.activation(h2[:, t, :], x_sb[:, t, :], ACT.Square, accum_out=ssq[:, t:t + 1])\
                   .then_inc(ev("ssq_ready"), 1)
            act.wait_ge(ev("var_ready"), 3)
            act.activation(rstd, var, ACT.Sqrt).then_inc(ev("std_ready"), 1)
            copy_T(h2T, "h")
            act.wait_ge(ev("negtop_ready"), 1)
            for t in range(TILES):
                act.activation(ex[:, t, :], lg[:, t, :], ACT.Exp, bias=negtop[:, t:t + 1]).then_inc(ev("ex_ready"), 1)
            bank = t_wait(act, "gT")
            t_done(act.activation(gatesT.rearrange("p t n -> p (t n)"), bank[0:E, 0:TILES * P], ACT.Copy), "gT")

            act.wait_ge(ev("xt_done"), 1)
            act.activation(xT.rearrange("p i n -> p (i n)"), banks[5][:, QW:2 * QW], ACT.Copy)\
               .then_inc(ev("xT_ready"), 1)
            act.wait_ge(ev("table_ready"), 1)
            total = act.value_load(table[0:1, GMAX + 3 * E - 1:GMAX + 3 * E], min_val=1, max_val=GMAX - 1)
            with act.Fori(0, total) as g:
                act.wait_ge(ev("g_ready"), g + 1)
                act.activation(g_sig, g_cap, ACT.Sigmoid, scale=ALPHA).then_inc(ev("sig_ready"), 1)
                act.wait_ge(ev("ht_done"), g + 1)
                act.activation(hidT.rearrange("p i n -> p (i n)"), banks[6][:, 0:QW], ACT.Copy)\
                   .then_inc(ev("hidT_ready"), 1)
                act.wait_ge(ev("xt_done"), g + 2)
                act.activation(xT.rearrange("p i n -> p (i n)"), banks[5][:, QW:2 * QW], ACT.Copy)\
                   .then_inc(ev("xT_ready"), 1)
                act.wait_ge(ev("down_done"), g + 1)
                act.activation(y_sb, banks[6][:, QW:2 * QW], ACT.Copy).then_inc(ev("y_ready"), 1)

            for t in range(TILES):
                act.wait_ge(ev("y2_ready"), t + 1)
                act.activation(h2[:, t, :], x_sb[:, t, :], ACT.Square, accum_out=ssq[:, t:t + 1])\
                   .then_inc(ev("ssq_ready"), 1)
            act.wait_ge(ev("var_ready"), 4)
            act.activation(rstd, var, ACT.Sqrt).then_inc(ev("std_ready"), 1)

        @block.vector
        def _(dve):
            steps = [0]

            def link(ins):
                steps[0] += 1
                ins.then_inc(ev("vec_steps"), 1)
                dve.wait_ge(ev("vec_steps"), steps[0])

            norms = [0]

            def inverse_std(var_from_ssq):
                norms[0] += 1
                if var_from_ssq:
                    dve.wait_ge(ev("ssq_ready"), {1: 2, 3: 4, 4: 6}[norms[0]])
                    dve.tensor_scalar(var, ssq, 1.0 / D, EPS, ALU.mult, ALU.add).then_inc(ev("var_ready"), 1)
                else:
                    dve.tensor_scalar(var, mv[:, :, 1], 1.0, EPS, ALU.mult, ALU.add).then_inc(ev("var_ready"), 1)
                dve.wait_ge(ev("std_ready"), norms[0])
                link(dve.reciprocal(rstd, rstd))
                link(dve.tensor_tensor(nt, rstd, rstd, ALU.mult))
                link(dve.tensor_tensor(nt, nt, var, ALU.mult))
                link(dve.tensor_scalar(nt, nt, -0.5, 1.5, ALU.mult, ALU.add))
                link(dve.tensor_tensor(rstd, rstd, nt, ALU.mult))

            link(dve.memset(h2[:, 0, 0:BM], 1.0))
            dve.wait_ge(ev("c_act_ready"), 1)
            for k in range(KC):
                last = dve.tensor_scalar(crep[:, k, :], h2[:, 0, 0:BM], c_act[:, k:k + 1], None, ALU.mult)
            last.then_inc(ev("crep_ready"), 1)
            dve.wait_ge(ev("crep_ready"), 1)
            inverse_std(True)
            for t in range(TILES):
                dve.tensor_scalar(h2[:, t, :], x_sb[:, t, :], rstd[:, t:t + 1], None, ALU.mult).then_inc(ev("xn_ready"), 1)
            dve.wait_ge(attn_in, 80)
            dve.wait_ge(ev("consts"), 1)
            link(dve.tensor_copy(pos_f, pos_i[:, :]))
            for t in range(TILES):
                last = dve.tensor_scalar(ang[:, t, :], invf, pos_f[:, t:t + 1], None, ALU.mult)
            link(last)
            link(dve.tensor_scalar(kf, ang, 1.0 / (2 * math.pi), BIG, ALU.mult, ALU.add))
            link(dve.tensor_scalar(kf, kf, BIG, None, ALU.subtract))
            c1 = 6.28125
            c2 = float(np.float32(math.floor((2 * math.pi - c1) * 2 ** 20) / 2 ** 20))
            c3 = float(np.float32(2 * math.pi - c1 - c2))
            for part in (c1, c2, c3):
                link(dve.scalar_tensor_tensor(ang, kf, -part, ang, ALU.mult, ALU.add))
            dve.tensor_scalar(ang, ang, -3.1415925, 3.1415925, ALU.max, ALU.min).then_inc(ev("angle_ready"), 1)
            dve.wait_ge(ev("ada_made"), 4)
            dve.tensor_tensor(mod[:, 0:4, :].rearrange("p j n -> p (j n)"), mod[:, 0:4, :].rearrange("p j n -> p (j n)"),
                              banks[4][:, :], ALU.add).then_inc(ev("ada_added"), 1)
            dve.wait_ge(ev("modT_done"), 1)
            link(dve.tensor_copy(mod_col.rearrange("p s k -> p (s k)"),
                                 banks[5][:, :].rearrange("p (m n) -> p m n", n=BM)[:, :, 0]))
            dve.scalar_tensor_tensor(mul1, mod_col[:, 1, :], 1.0, g1_col, ALU.add, ALU.mult)\
               .then_inc(ev("mod_col_ready"), 2)
            dve.wait_ge(ev("mod_col_ready"), 2)
            for h in range(2):
                name = f"xT0{h}"
                bank = z_wait(dve, name)
                for i in range(4):
                    k = 4 * h + i
                    last = dve.tensor_scalar(hT[:, k, 0:P], bank[:, i * P:(i + 1) * P], mul1[:, k:k + 1],
                                             mod_col[:, 0, k:k + 1], ALU.mult, ALU.add)
                z_done(last, name)

            def add_bias(item, dst):
                n = biased.index(item)
                cols = 2 * P if item == "kv" else COLS
                dve.wait_ge(bias_in[n % 2], 16 * (n // 2 + 1))
                for t in range(TILES):
                    name = f"{item}t{t}"
                    bank = z_wait(dve, name)
                    z_done(dve.tensor_tensor(dst(t), bank[:, 0:cols], bias_ring[:, n % 2, 0:cols], ALU.add), name)

            def half(buf, j):
                return lambda t: buf[:, t, j * COLS:(j + 1) * COLS]

            add_bias("v0", half(v_buf, 0))
            add_bias("v1", half(v_buf, 1))
            for t in range(TILES):
                for j in range(2):
                    dve.wait_ge(ev("v_gelu"), 2 * j + t + 1)
                    last = dve.bn_stats(stats[:, t, j, :], v_buf[:, t, j * COLS:(j + 1) * COLS])
            link(last)
            for t in range(TILES):
                last = dve.bn_aggr(mv[:, t, :], stats[:, t, :, :])
            link(last)
            add_bias("u0", half(u_buf, 0))
            inverse_std(False)
            dve.wait_ge(ln_in, 32)
            for t in range(TILES):
                link(dve.tensor_scalar(v_buf[:, t, :], v_buf[:, t, :], mv[:, t, 0:1], rstd[:, t:t + 1],
                                       ALU.subtract, ALU.mult))
                link(dve.tensor_tensor(v_buf[:, t, :], v_buf[:, t, :], ln_gb[:, 0, :], ALU.mult))
                dve.tensor_tensor(v_buf[:, t, :], v_buf[:, t, :], ln_gb[:, 1, :], ALU.add).then_inc(ev("vn_ready"), 1)
            add_bias("u1", half(u_buf, 1))
            for t in range(TILES):
                for h in range(2):
                    dve.wait_ge(ev("u_gelu"), 2 * h + t + 1)
                    name = f"f{t}{h}"
                    bank = z_wait(dve, name)
                    for i in range(4):
                        w = slice((4 * h + i) * P, (4 * h + i + 1) * P)
                        last = dve.scalar_tensor_tensor(u_buf[:, t, w], bank[:, i * P:(i + 1) * P],
                                                        bs[:, 4 * h + i:4 * h + i + 1], u_buf[:, t, w], ALU.add, ALU.mult)
                    z_done(last, name)
            add_bias("q0", half(q_buf, 0))
            add_bias("q1", half(q_buf, 1))
            add_bias("kv", lambda t: kv[:, t, :])
            dve.wait_ge(ev("trig_ready"), 2)
            link(dve.tensor_tensor(cos, cos, cos, ALU.mult))
            link(dve.tensor_scalar(cos, cos, -2.0, 1.0, ALU.mult, ALU.add))
            for name in ("q0t1", "q1t1", "kvt1"):
                z_gone(dve, name)
            for t in range(TILES):
                for view, heads in ((q_buf[:, t, :].rearrange("p (h d) -> p h d", d=CH), NQ),
                                    (kv[:, t, 0:P].rearrange("p (h d) -> p h d", d=CH), NKV)):
                    t1, t2 = view[:, :, 0:HALF], view[:, :, HALF:2 * HALF]
                    shape = [P, heads, HALF]
                    co = cos[:, t, :].unsqueeze(1).to_broadcast(shape)
                    si = sin[:, t, :].unsqueeze(1).to_broadcast(shape)
                    a, b, cc, d = (rope_room[:, i * P:i * P + heads * HALF].rearrange("p (h f) -> p h f", f=HALF)
                                   for i in range(4))
                    dve.tensor_tensor(a, t1, co, ALU.mult)
                    dve.tensor_tensor(b, t2, si, ALU.mult)
                    dve.tensor_tensor(cc, t2, co, ALU.mult)
                    link(dve.tensor_tensor(d, t1, si, ALU.mult))
                    dve.tensor_tensor(t1, a, b, ALU.subtract)
                    link(dve.tensor_tensor(t2, cc, d, ALU.add))
                for u in range(2):
                    last = dve.tensor_copy(kd[:, t, :, u, :], kv[:, t, 0:P].rearrange("p (g d) -> p g d", g=NKV))
                last.then_inc(ev("rope_ready"), 1)

            def gates_out(n, t):
                item = ("ga0", "ga1", "gb0", "gb1")[n]
                dst = (sig_a, sig_a, sig_b, sig_b)[n][:, t, (n % 2) * COLS:(n % 2 + 1) * COLS]
                m = biased.index(item)
                dve.wait_ge(bias_in[m % 2], 16 * (m // 2 + 1))
                name = f"{item}t{t}"
                bank = z_wait(dve, name)
                z_done(dve.tensor_tensor(dst, bank[:, :], bias_ring[:, m % 2, :], ALU.add), name)

            def softmax_max(n):
                keys = CH if n == 0 else P
                dve.wait_ge(ev("s_done"), n + 1)
                for r in range(2):
                    last = dve.tensor_reduce(mx[:, r, :], banks[4 + r][:, :].rearrange("p (g k) -> p g k", g=4)[:, :, 0:keys],
                                             AX.X, ALU.max)
                link(last)
                link(dve.scalar_tensor_tensor(mx, mx, 1.0 / math.sqrt(CH), sk, ALU.mult, ALU.max))
                link(dve.tensor_tensor(es, sk, mx, ALU.subtract))
                dve.tensor_scalar(negm, mx, -1.0, None, ALU.mult).then_inc(ev("negm_ready"), 1)

            def softmax_norm(n):
                keys = CH if n == 0 else P
                dve.wait_ge(ev("exp_done"), 9 * (n + 1))
                link(dve.tensor_tensor(den, den, es, ALU.add))
                link(dve.reciprocal(den, den))
                dve.tensor_tensor(probs[:, :, :, 0:keys].rearrange("p r g k -> p (r g) k"),
                                  probs[:, :, :, 0:keys].rearrange("p r g k -> p (r g) k"),
                                  den.rearrange("p r g -> p (r g)").unsqueeze(2).to_broadcast([P, 8, keys]), ALU.mult)\
                   .then_inc(ev("p_norm"), 1)

            def values(n):
                t = n // 2
                dve.tensor_copy(vp[0:CH, :], kv[0:CH, t, P:2 * P])
                dve.tensor_copy(vp[CH:P, :], kv[CH:P, t - 1, P:2 * P]).then_inc(ev("vp_ready"), 1)

            def attn_out(n):
                name = f"o{n}"
                bank = t_wait(dve, name)
                t_done(dve.tensor_copy(ybT[:, :, n * CH:(n + 1) * CH], bank[:, :].rearrange("p (k q) -> p k q", q=CH)), name)

            values(2)
            order = [(n, t) for n in range(4) for t in range(TILES)]
            gates_out(*order[0])
            gates_out(*order[1])
            softmax_max(0)
            softmax_norm(0)
            gates_out(*order[2])
            for n in range(1, NCH):
                softmax_max(n)
                gates_out(*order[2 * n + 1])
                attn_out(n - 1)
                softmax_norm(n)
                if 2 * n + 2 < 8:
                    gates_out(*order[2 * n + 2])
            attn_out(NCH - 1)

            for kind, sig, need in (("oa", sig_a, 2), ("ob", sig_b, 4)):
                dve.wait_ge(ev("sig_done"), need)
                for j in range(2):
                    for t in range(TILES):
                        w = slice(j * COLS, (j + 1) * COLS)
                        name = f"{kind}{j}t{t}"
                        bank = z_wait(dve, name)
                        if kind == "oa":
                            z_done(dve.tensor_tensor(merged[:, t, w], bank[:, :], sig[:, t, w], ALU.mult), name)
                        else:
                            z_done(dve.tensor_tensor(sig[:, t, w], bank[:, :], sig[:, t, w], ALU.mult), name)
                            z_gone(dve, name)
                            z_gone(dve, f"oa{j}t{t}")
                            dve.tensor_tensor(merged[:, t, w], merged[:, t, w], sig[:, t, w], ALU.add)\
                               .then_inc(ev("merged_ready"), 1)
            dve.wait_ge(cond_in, 16 * 10)
            for j in (4, 8):
                dve.wait_ge(ev("ada_made"), j + 4)
                rows = mod[:, j:j + 4, :].rearrange("p j n -> p (j n)")
                dve.tensor_tensor(rows, rows, banks[j // 4 + 3][:, :], ALU.add).then_inc(ev("ada_added"), 1)
            dve.wait_ge(g2_in, 16)
            for h in range(2):
                w = slice(h * COLS, (h + 1) * COLS)
                bank = z_wait(dve, f"bc4{h}")
                z_done(dve.scalar_tensor_tensor(mul2[:, w], bank[:, :], 1.0, g2bc[:, w], ALU.add, ALU.mult), f"bc4{h}")
            z_gone(dve, "bc21")
            z_gone(dve, "bc20")
            for j in range(2):
                for t in range(TILES):
                    w = slice(j * COLS, (j + 1) * COLS)
                    name = f"out{j}t{t}"
                    bank = z_wait(dve, name)
                    z_done(dve.tensor_tensor(merged[:, t, w], bank[:, :], gt1[:, w], ALU.mult), name)
                    z_gone(dve, name)
                    last = dve.tensor_tensor(x_sb[:, t, w], x_sb[:, t, w], merged[:, t, w], ALU.add)
                    if j:
                        last.then_inc(ev("x2_ready"), 1)
            inverse_std(True)
            for h in range(2):
                z_gone(dve, f"bc4{h}")
                z_gone(dve, f"bc3{h}")
            for t in range(TILES):
                link(dve.scalar_tensor_tensor(h2[:, t, :], x_sb[:, t, :], rstd[:, t:t + 1], mul2, ALU.mult, ALU.mult))
                dve.tensor_tensor(h2[:, t, :], h2[:, t, :], sh2, ALU.add).then_inc(ev("h2_ready"), 1)

            dve.wait_ge(ev("h2_ready"), TILES)
            bank = z_wait(dve, "logits")
            for t in range(TILES):
                last = dve.tensor_tensor(lg[:, t, :], bank[:, t * E:(t + 1) * E], br, ALU.add)
            z_done(last, "logits")
            z_gone(dve, "logits")
            for t in range(TILES):
                last = dve.max(top8[:, t, :], lg[:, t, :])
            link(last)
            dve.tensor_scalar(negtop, top8[:, :, 0], -1.0, None, ALU.mult).then_inc(ev("negtop_ready"), 1)
            link(dve.memset(top8[:, :, TOPK:8], 3.0e38))
            for t in range(TILES):
                link(dve.match_replace(lrep[:, t, :], top8[:, t, :], lg[:, t, :], -3.0e38))
            dve.tensor_tensor(mask, lg, lrep, ALU.not_equal).then_inc(ev("mask_ready"), 1)
            dve.wait_ge(ev("mask_ready"), 1)
            dve.wait_ge(ev("ex_ready"), TILES)
            link(dve.tensor_tensor(ex, ex, mask, ALU.mult))
            link(dve.tensor_reduce(esum, ex, AX.X, ALU.add))
            link(dve.reciprocal(esum, esum))
            for t in range(TILES):
                last = dve.tensor_scalar(gates[:, t, :], ex[:, t, :], esum[:, t:t + 1], None, ALU.mult)
            last.then_inc(ev("gates_ready"), 1)
            dve.wait_ge(ev("gates_ready"), 1)
            for t in range(TILES):
                dve.tensor_copy(slots_gates[:, :, 2 + t], gates[:, t, :])
            bank = z_wait(dve, "rank")

            def blocks_of(dst, counts):
                link(dve.tensor_scalar(dst, counts, BM / 2 - 0.5, 1.0 / BM, ALU.add, ALU.mult))
                link(dve.tensor_scalar(dst, dst, BIG, None, ALU.add))
                return dve.tensor_scalar(dst, dst, BIG, 1.0, ALU.subtract, ALU.max)
            blocks_of(nbT, bank[0:E, 2 * P:3 * P]).then_inc(ev("counts_ready"), 1)
            link(blocks_of(nbB, bank[:, 2 * E:3 * E]))
            dve.tensor_scalar(dtmp.rearrange("p t e -> p (t e)"), bank[:, 0:TILES * E], 1.0, None, ALU.add)\
               .then_inc(z_free[z_use("rank")[0]], 1)
            z_gone(dve, "rank")
            bank = z_wait(dve, "starts")
            dve.tensor_copy(stB, bank[:, 0:E])
            z_done(dve.tensor_copy(ncol, bank[:, 2 * E:2 * E + 4]), "starts")
            z_gone(dve, "starts")
            link(dve.tensor_tensor(enB, stB, nbB, ALU.add))
            dve.wait_ge(ev("counters"), 5)
            dve.tensor_scalar(cmp[0:E, :], iota_g[0:E, :], ncol[0:E, 2:3], None, ALU.is_ge).then_inc(ev("cmp_ready"), 1)
            for t in range(TILES):
                link(dve.scalar_tensor_tensor(dtmp[:, t, :], stB, float(BM), dtmp[:, t, :], ALU.mult, ALU.add))
                link(dve.tensor_tensor(dtmp[:, t, :], dtmp[:, t, :], mask[:, t, :], ALU.mult))
                link(dve.tensor_scalar(slots_gates[:, :, t], dtmp[:, t, :], -1.0, None, ALU.add))
            link(dve.tensor_scalar(block_hot, iota_g, ncol[:, 0:1], None, ALU.is_ge))
            link(dve.scalar_tensor_tensor(block_hot, iota_g, ncol[:, 2:3], block_hot, ALU.is_lt, ALU.mult))
            dve.tensor_copy(table[0:1, GMAX:GMAX + E], nbB[0:1, :])
            dve.tensor_copy(table[0:1, GMAX + E:GMAX + 2 * E], stB[0:1, :])
            dve.tensor_copy(table[0:1, GMAX + 2 * E:GMAX + 3 * E], enB[0:1, :]).then_inc(ev("slots_ready"), 1)
            dve.wait_ge(ev("slots_ready"), 1)
            bank = z_wait(dve, "etab")
            link(dve.tensor_scalar(block_e, bank[:, 0:GMAX], float(E - 1), None, ALU.min))
            dve.tensor_copy(table[0:1, 0:GMAX], block_e[0:1, :]).then_inc(ev("table_ready"), 1)
            dve.wait_ge(ev("table_ready"), 1)

            dve.memset(y_sb, 0.0).then_inc(ev("y_ready"), 1)
            dve.memset(gT, 0.0).then_inc(ev("gT_ready"), 1)

            def choose(g, slots, e):
                return dve.tensor_scalar(slots, slots_gates[:, bass.ds(e, 1), 0:2].rearrange("p a t -> p (a t)"),
                                         slot_base[:, bass.ds(g, 1)], None, ALU.subtract)

            def gather_map(g, slots):
                for t in range(TILES):
                    last = dve.tensor_scalar(sel[:, t, :], iota4[:, 0, :], slots[:, t:t + 1], None, ALU.is_equal)
                return last

            def bias_map(g):
                return dve.tensor_scalar(onehot, iota4[:, 0, :], 0.0, block_hot[:, bass.ds(g, 1)], ALU.mult, ALU.add)

            e0 = dve.value_load(table[0:1, 0:1], min_val=0, max_val=E - 1)
            choose(0, slot_next, e0).then_inc(ev("next_ready"), 1)
            dve.wait_ge(ev("next_ready"), 1)
            gather_map(0, slot_next).then_inc(ev("sel_ready"), 1)
            bias_map(0).then_inc(ev("hot_ready"), 1)
            dve.wait_ge(ev("xg_done"), 1)
            dve.tensor_copy(xe, banks[5][:, 0:QW]).then_inc(ev("xe_ready"), 1)
            total = dve.value_load(table[0:1, GMAX + 3 * E - 1:GMAX + 3 * E], min_val=1, max_val=GMAX - 1)
            with dve.Fori(0, total) as g:
                e_next = dve.value_load(table[0:1, bass.ds(g + 1, 1)], min_val=0, max_val=E - 1)
                e_now = dve.value_load(table[0:1, bass.ds(g, 1)], min_val=0, max_val=E - 1)
                choose(g + 1, slot_next, e_next).then_inc(ev("next_ready"), 1)
                choose(g, slot_now, e_now).then_inc(ev("now_ready"), 1)
                dve.wait_ge(ev("next_ready"), g + 2)
                dve.wait_ge(ev("xg_done"), g + 1)
                gather_map(g + 1, slot_next).then_inc(ev("sel_ready"), 1)
                dve.wait_ge(ev("now_ready"), g + 1)
                dve.wait_ge(ev("gT_ready"), g + 1)
                for t in range(TILES):
                    last = dve.tensor_scalar(selg[:, t, :].rearrange("p (q j) -> p q j", q=NQT), iota4,
                                             slot_now[:, t:t + 1],
                                             slots_gates[:, bass.ds(e_now, 1), 2 + t:3 + t].rearrange("p a t -> p (a t)"),
                                             ALU.is_equal, ALU.mult)
                last.then_inc(ev("selg_ready"), 1)
                dve.wait_ge(ev("gu_done"), g + 1)
                dve.tensor_scalar(g_cap, banks[4][:, 0:QW], LIMIT, None, ALU.min).then_inc(ev("g_ready"), 1)
                dve.tensor_scalar(u_cap, banks[4][:, QW:2 * QW], -LIMIT, LIMIT, ALU.max, ALU.min).then_inc(ev("u_ready"), 1)
                bias_map(g + 1).then_inc(ev("hot_ready"), 1)
                dve.wait_ge(ev("u_ready"), g + 1)
                dve.scalar_tensor_tensor(gu_prod, u_cap, 1.0, g_cap, ALU.add, ALU.mult).then_inc(ev("prod_ready"), 1)
                dve.wait_ge(ev("prod_ready"), g + 1)
                dve.wait_ge(ev("sig_ready"), g + 1)
                dve.tensor_tensor(hid, gu_prod, g_sig, ALU.mult).then_inc(ev("hid_ready"), 1)
                dve.wait_ge(ev("xg_done"), g + 2)
                dve.tensor_copy(xe, banks[5][:, 0:QW]).then_inc(ev("xe_ready"), 1)
                dve.wait_ge(ev("gt_done"), g + 1)
                dve.tensor_copy(gT, banks[7][:, 0:QW]).then_inc(ev("gT_ready"), 1)

            dve.wait_ge(ev("comb_done"), total + 1)
            for t in range(TILES):
                for q in range(NQT):
                    w = slice(q * QW, (q + 1) * QW)
                    last = dve.tensor_tensor(h2[:, t, w], banks[q][:, t * QW:(t + 1) * QW], gt2[:, w], ALU.mult)
                link(last)
                dve.tensor_tensor(x_sb[:, t, :], x_sb[:, t, :], h2[:, t, :], ALU.add).then_inc(ev("y2_ready"), 1)
            inverse_std(True)
            dve.wait_ge(gf_in, 16)
            for t in range(TILES):
                dve.scalar_tensor_tensor(h2[:, t, :], x_sb[:, t, :], rstd[:, t:t + 1], gate_up[0][:, 0, 0:D],
                                         ALU.mult, ALU.mult).then_inc(ev("out_ready"), 1)

        @block.tensor
        def _(pe):
            def z_open(name):
                b, n = z_use(name)
                if n > 1:
                    pe.wait_ge(z_free[b], n - 1)
                return banks[b]

            def t_open(name):
                b, n = t_use(name)
                if n > 1:
                    pe.wait_ge(t_free[b], n - 1)
                return banks[6 + b]

            def z_put(ins, name):
                ins.then_inc(z_full[z_use(name)[0]], 1)

            def t_put(ins, name):
                ins.then_inc(t_full[t_use(name)[0]], 1)

            def weights(name):
                s, n = ring_slot(name)
                pe.wait_ge(ring_in[s], n)
                return ring[:, s]

            def rows_times(item, t, lhsT, cols=COLS):
                w = weights(item)
                name = f"{item}t{t}"
                bank = z_open(name)
                for k in range(KC):
                    last = pe.matmul(bank[:, 0:cols], lhsT[:, k, t * P:(t + 1) * P], w[:, k, 0:cols],
                                     start=(k == 0), stop=(k == KC - 1))
                z_put(last, name)

            def transposes(src, kind):
                for t in range(TILES):
                    for h in range(2):
                        name = f"{kind}{t}{h}"
                        bank = t_open(name)
                        for i in range(4):
                            k = 4 * h + i
                            last = pe.transpose(bank[:, i * P:(i + 1) * P], src[:, t, k * P:(k + 1) * P], ident[:, :])
                        t_put(last, name)

            def ada(j, bank, col):
                w = weights(f"ada{j}")
                for k in range(KC):
                    for q in range(NQT):
                        last = pe.matmul(bank[q * BM:(q + 1) * BM, col * P:(col + 1) * P], crep[:, k, :],
                                         w[:, k, q * P:(q + 1) * P], start=(k == 0), stop=(k == KC - 1),
                                         skip_group_check=True)
                return last

            pe.wait_ge(ev("consts"), 3)
            pe.wait_ge(ev("xn_ready"), TILES)
            for t in range(TILES):
                for h in range(2):
                    name = f"xT{t}{h}"
                    bank = z_open(name)
                    for i in range(4):
                        k = 4 * h + i
                        last = pe.transpose(bank[:, i * P:(i + 1) * P], h2[:, t, k * P:(k + 1) * P], ident[:, :])
                    z_put(last, name)
            pe.wait_ge(ev("crep_ready"), 1)
            for j in range(4):
                ada(j, banks[4], j).then_inc(ev("ada_made"), 1)
            pe.wait_ge(ev("ada_added"), 1)
            for j in range(4):
                last = pe.transpose(banks[5][:, j * P:(j + 1) * P], mod[:, j, :], ident[:, :])
            last.then_inc(ev("modT_done"), 1)
            pe.wait_ge(ev("ws_masked"), 1)
            for h in range(2):
                name = f"ws{h}"
                bank = t_open(name)
                for i in range(4):
                    last = pe.transpose(bank[:, i * P:(i + 1) * P], ws[:, 4 * h + i, :], ident[:, :])
                t_put(last, name)
            for t in range(TILES):
                for h in range(2):
                    z_gone(pe, f"xT{t}{h}")

            for item in ("v0", "v1", "u0", "u1"):
                for t in range(TILES):
                    rows_times(item, t, hT)
            for h in range(2):
                t_gone(pe, f"ws{h}")
            pe.wait_ge(ev("vn_ready"), TILES)
            for t in range(TILES):
                for h in range(2):
                    name = f"f{t}{h}"
                    bank = z_open(name)
                    for i in range(4):
                        last = pe.matmul(bank[:, i * P:(i + 1) * P], wsT[:, 4 * h + i, :],
                                         v_buf[:, t, (4 * h + i) * P:(4 * h + i + 1) * P], start=True, stop=True,
                                         skip_group_check=True)
                    z_put(last, name)
            for t in range(TILES):
                rows_times("q0", t, hT)
            for t in range(TILES):
                for h in range(2):
                    z_gone(pe, f"f{t}{h}")
            transposes(u_buf, "ya")
            for t in range(TILES):
                rows_times("q1", t, hT)
            for t in range(TILES):
                rows_times("kv", t, hT, 2 * P)
            rows_times("ga0", 0, hT)
            pe.wait_ge(ev("rope_ready"), TILES)
            transposes(q_buf, "q")
            bank = t_open("k")
            for g in range(NKV):
                for t in range(TILES):
                    last = pe.transpose(bank[:, g * S + t * P:g * S + (t + 1) * P],
                                        kd[:, t, g, :, :].rearrange("p u d -> p (u d)"), ident[:, :])
            t_put(last, "k")
            rows_times("ga0", 1, hT)

            def scores(n):
                if n == 0:
                    for t in range(TILES):
                        for h in range(2):
                            t_gone(pe, f"q{t}{h}")
                    t_gone(pe, "k")
                else:
                    pe.wait_ge(ev("exp_done"), 9 * n)
                for g in range(NKV):
                    for j in range(2):
                        for r in range(2):
                            rows = slice(r * CH, (r + 1) * CH)
                            col = (2 * g + j) * P
                            lhsT = qT[rows, n, 4 * g + 2 * j:4 * g + 2 * j + 2, :].rearrange("p k q -> p (k q)")
                            if n == 0:
                                parts = [(0, 0, CH)]
                            elif n % 2:
                                parts = [(0, (n - 1) * CH, P)]
                            else:
                                parts = [(0, n * CH, CH), (CH, (n - 1) * CH, CH)]
                            for off, key, width in parts:
                                last = pe.matmul(banks[4 + r][:, col + off:col + off + width], lhsT,
                                                 kT[rows, g, key:key + width], start=True, stop=True,
                                                 skip_group_check=True)
                last.then_inc(ev("s_done"), 1)

            def probs_T(n):
                keys = CH if n == 0 else P
                pe.wait_ge(ev("p_norm"), n + 1)
                for r in range(2):
                    name = f"p{n}{r}"
                    bank = t_open(name)
                    for g in range(4):
                        last = pe.transpose(bank[0:keys, g * P:(g + 1) * P], probs[:, r, g, 0:keys], ident[:, :])
                    t_put(last, name)

            def attend(n):
                keys = CH if n == 0 else P
                for r in range(2):
                    t_gone(pe, f"p{n}{r}")
                if n % 2 == 0 and n:
                    pe.wait_ge(ev("vp_ready"), 1)
                name = f"o{n}"
                bank = t_open(name)
                for g in range(NKV):
                    for r in range(2):
                        cols = slice(g * CH, (g + 1) * CH)
                        v = vp[0:keys, cols] if n % 2 == 0 and n else kv[0:keys, n // 2, P + g * CH:P + (g + 1) * CH]
                        last = pe.matmul(bank[r * CH:(r + 1) * CH, g * 256:(g + 1) * 256], v,
                                         probsT[0:keys, r, 2 * g:2 * g + 2, :].rearrange("p g n -> p (g n)"),
                                         start=True, stop=True, skip_group_check=True)
                t_put(last, name)

            scores(0)
            rows_times("ga1", 0, hT)
            probs_T(0)
            scores(1)
            rows_times("ga1", 1, hT)
            attend(0)
            rows_times("gb0", 0, hT)
            probs_T(1)
            scores(2)
            rows_times("gb0", 1, hT)
            attend(1)
            rows_times("gb1", 0, hT)
            probs_T(2)
            scores(3)
            rows_times("gb1", 1, hT)
            attend(2)
            rows_times("oa0", 0, yaT)
            probs_T(3)
            rows_times("oa0", 1, yaT)
            attend(3)
            for t in range(TILES):
                rows_times("oa1", t, yaT)
            for n in range(NCH):
                t_gone(pe, f"o{n}")
            for item in ("ob0", "ob1"):
                for t in range(TILES):
                    rows_times(item, t, ybT)
            pe.wait_ge(ev("exp_done"), 9 * NCH)
            for j in range(4, 12):
                ada(j, banks[j // 4 + 3], j % 4).then_inc(ev("ada_made"), 1)
            pe.wait_ge(ev("merged_ready"), 2 * TILES)
            transposes(merged, "m")
            pe.wait_ge(ev("ada_added"), 3)
            for s in (2, 3, 4, 5):
                for h in range(2):
                    name = f"bc{s}{h}"
                    bank = z_open(name)
                    for q in range(NQT):
                        last = pe.matmul(bank[:, q * P:(q + 1) * P], row_sel[:, q, :], mod[:, 2 * s + h, :],
                                         start=True, stop=True, skip_group_check=True)
                    z_put(last, name)
            for t in range(TILES):
                for h in range(2):
                    t_gone(pe, f"m{t}{h}")
            for item in ("out0", "out1"):
                for t in range(TILES):
                    rows_times(item, t, mT)

            pe.wait_ge(ev("h2_ready"), TILES)
            transposes(h2, "h")
            pe.wait_ge(route_in, 32)
            for t in range(TILES):
                for h in range(2):
                    t_gone(pe, f"h{t}{h}")
            bank = z_open("logits")
            for t in range(TILES):
                for k in range(KC):
                    last = pe.matmul(bank[:, t * E:(t + 1) * E], h2T[:, k, t * P:(t + 1) * P], wr[:, k, :],
                                     start=(k == 0), stop=(k == KC - 1), skip_group_check=True)
            z_put(last, "logits")
            pe.wait_ge(ev("mask_ready"), 1)
            bank = z_open("rank")
            pe.matmul(bank[:, 0:E], tri, mask[:, 0, :], start=True, stop=True, skip_group_check=True)
            pe.matmul(bank[:, E:2 * E], tri, mask[:, 1, :], start=True, stop=False, skip_group_check=True)
            pe.matmul(bank[:, E:2 * E], ones, mask[:, 0, :], start=False, stop=True, skip_group_check=True)
            for t in range(TILES):
                pe.matmul(bank[:, 2 * E:3 * E], ones, mask[:, t, :], start=(t == 0), stop=(t == 1), skip_group_check=True)
            for t in range(TILES):
                last = pe.matmul(bank[0:E, 2 * P:3 * P], mask[:, t, :], ones, start=(t == 0), stop=(t == 1),
                                 skip_group_check=True)
            z_put(last, "rank")
            pe.wait_ge(ev("gates_ready"), 1)
            bank = t_open("gT")
            for t in range(TILES):
                last = pe.transpose(bank[0:E, t * P:(t + 1) * P], gates[:, t, :], ident[:, :])
            t_put(last, "gT")
            pe.wait_ge(ev("counts_ready"), 1)
            pe.wait_ge(ev("counters"), 5)
            bank = z_open("starts")
            pe.matmul(bank[:, 0:E], nbT, tri_exc[:, 0:E], start=True, stop=True, skip_group_check=True)
            pe.matmul(bank[:, 2 * E:2 * E + 2], tri_exc, nbT[:, 0:2], start=True, stop=True, skip_group_check=True)
            last = pe.matmul(bank[:, 2 * E + 2:2 * E + 4], tri_inc, nbT[:, 0:2], start=True, stop=True,
                             skip_group_check=True)
            z_put(last, "starts")
            pe.wait_ge(ev("cmp_ready"), 1)
            bank = z_open("etab")
            last = pe.matmul(bank[:, 0:GMAX], ones[0:E, :], cmp[0:E, :], start=True, stop=True)
            z_put(last, "etab")

            pe.wait_ge(ev("table_ready"), 1)
            pe.wait_ge(bd_in, 16)
            t_gone(pe, "gT")
            for q in range(NQT):
                for t in range(TILES):
                    last = pe.matmul(banks[q][:, t * QW:(t + 1) * QW], gatesT[:, t, :], b_down_sb[:, q * QW:(q + 1) * QW],
                                     start=(t == 0), stop=True, skip_group_check=True)
            last.then_inc(ev("acc_init"), 1)

            def gather():
                for t in range(TILES):
                    for q in range(NQT):
                        last = pe.matmul(banks[5][q * BM:(q + 1) * BM, 0:QW], sel[:, t, :], h2[:, t, q * QW:(q + 1) * QW],
                                         start=(t == 0), stop=(t == 1), skip_group_check=True)
                last.then_inc(ev("xg_done"), 1)

            def gather_T():
                for i in range(2):
                    last = pe.transpose(banks[5][:, QW + i * P:QW + (i + 1) * P], xe[:, i * P:(i + 1) * P], ident[:, :])
                last.then_inc(ev("xt_done"), 1)

            def combine():
                for t in range(TILES):
                    for q in range(NQT):
                        rows = slice(q * BM, (q + 1) * BM)
                        last = pe.matmul(banks[q][:, t * QW:(t + 1) * QW], gT[rows, t * P:(t + 1) * P], y_sb[rows, :],
                                         start=False, stop=True, skip_group_check=True)
                last.then_inc(ev("comb_done"), 1)

            pe.wait_ge(exp_bias_in, 64)
            pe.wait_ge(ev("sel_ready"), 1)
            gather()
            pe.wait_ge(ev("xe_ready"), 1)
            gather_T()
            with pe.Fori(0, E // 2) as p:
                for s in range(2):
                    first = pe.value_load(table[0:1, bass.ds(p * 2 + (s + GMAX + E), 1)], min_val=0, max_val=GMAX - 1)
                    blocks = pe.value_load(table[0:1, bass.ds(p * 2 + (s + GMAX), 1)], min_val=1, max_val=8)
                    with pe.Fori(0, blocks) as b:
                        g = first + b
                        pe.wait_ge(ev("xT_ready"), g + 1)
                        pe.wait_ge(ev("hot_ready"), g + 1)
                        for k in range(KC):
                            if k % 2 == 0:
                                pe.wait_ge(gu_in[s][k // 2], p * 16 + 16)
                            for q in range(NQT):
                                last = pe.matmul(banks[4][q * BM:(q + 1) * BM, :].rearrange("p (a n) -> p a n", a=2),
                                                 xT[:, k % 2, (k // 2) * BM:(k // 2 + 1) * BM],
                                                 gate_up[s][:, k, :].rearrange("p (a n) -> p a n", a=2)[:, :, q * QW:(q + 1) * QW],
                                                 start=(k == 0), stop=(k == KC - 1), skip_group_check=True)
                            if k == 0:
                                for q in range(NQT):
                                    rows = slice(q * BM, (q + 1) * BM)
                                    pe.matmul(banks[4][rows, :], onehot[rows, :], exp_bias[rows, :], start=False,
                                              stop=False, skip_group_check=True)
                        last.then_inc(ev("gu_done"), 1)
                        pe.wait_ge(ev("gT_ready"), g + 1)
                        pe.wait_ge(ev("y_ready"), g + 1)
                        combine()
                        pe.wait_ge(ev("sel_ready"), g + 2)
                        gather()
                        pe.wait_ge(ev("selg_ready"), g + 1)
                        for t in range(TILES):
                            last = pe.transpose(banks[7][:, t * P:(t + 1) * P], selg[:, t, :], ident[:, :])
                        last.then_inc(ev("gt_done"), 1)
                        pe.wait_ge(ev("hid_ready"), g + 1)
                        for i in range(2):
                            last = pe.transpose(banks[6][:, i * P:(i + 1) * P], hid[:, i * P:(i + 1) * P], ident[:, :])
                        last.then_inc(ev("ht_done"), 1)
                        pe.wait_ge(ev("xe_ready"), g + 2)
                        gather_T()
                        pe.wait_ge(ev("hidT_ready"), g + 1)
                        for k in range(KC):
                            if k % 2 == 0:
                                pe.wait_ge(dn_in[k // 2], p * 32 + (16 * s + 16))
                            for q in range(NQT):
                                last = pe.matmul(banks[6][q * BM:(q + 1) * BM, QW:2 * QW],
                                                 hidT[:, k % 2, (k // 2) * BM:(k // 2 + 1) * BM],
                                                 down[:, k, q * QW:(q + 1) * QW],
                                                 start=(k == 0), stop=(k == KC - 1), skip_group_check=True)
                        last.then_inc(ev("down_done"), 1)
            total = pe.value_load(table[0:1, GMAX + 3 * E - 1:GMAX + 3 * E], min_val=1, max_val=GMAX - 1)
            pe.wait_ge(ev("y_ready"), total + 1)
            pe.wait_ge(ev("gT_ready"), total + 1)
            combine()


_INS = ["x", "c", "positions", "w_ada", "b_ada", "g_norm1", "w_in", "b_in", "ln_v_g", "ln_v_b", "w_spatial",
        "b_spatial", "sinks", "w_o_a", "w_o_b", "w_out", "g_norm2", "w_router", "b_router", "w_gate_up",
        "b_gate_up", "w_down", "b_down", "g_final"]


def kernel(**inputs):
    import numpy as _np
    import concourse.bacc as _bacc
    from concourse import mybir as _mybir
    from concourse.bass_utils import run_bass_kernel_spmd as _run

    nc = _bacc.Bacc("TRN2", target_bir_lowering=False, num_devices=1)
    arrays, args = {}, []
    for name in _INS:
        a = _np.ascontiguousarray(inputs[name])
        arrays[f"in_{name}_dram"] = a
        args.append(nc.dram_tensor(f"in_{name}_dram", a.shape, _mybir.dt.from_np(a.dtype), kind="ExternalInput").ap())
    args.append(nc.dram_tensor("out_dram", (1, S, D), F32, kind="ExternalOutput").ap())
    bass_hybrid_layer(nc, *args)
    r = _run(nc, [arrays], core_ids=[0])
    return r.results[0]["out_dram"]
```

```python
from contextlib import ExitStack
import math

import numpy as np
import concourse.bass as bass
from concourse import mybir

F32 = mybir.dt.float32
I32 = mybir.dt.int32
ALU = mybir.AluOpType
ACT = mybir.ActivationFunctionType
AX = mybir.AxisListType

P = 128
D = 1024
S = 256
TILES = S // P
KC = D // P
COLS = 512
H = 8
CH = 64
NCH = S // CH
NQ = 16
NKV = 2
HALF = 8
THETA = 500000.0
IN_W = 5376
E = 32
TOPK = 4
FF = 1024
ALPHA = 1.702
LIMIT = 7.0
EPS = 1e-5
BM = 64
NH = P // BM
HW = D // NH
QR = 32
NQT = P // QR
GMAX = 64
BIG = 12582912.0

EVENTS = ("acc_init", "ada_added", "ada_made", "angle_ready", "c_act_ready", "cmp_ready", "comb_done",
          "consts", "counters", "counts_ready", "crep_ready", "down_used", "ex_ready", "exp_done",
          "gT_ready", "g_ready", "heads_ready", "gates_ready", "gt_done", "gu_used", "h2_ready", "hidT_ready",
          "hid_ready", "hot_ready", "ht_done", "mask_ready", "merged_ready", "modT_done", "mod_col_ready",
          "negm_ready", "negtop_ready", "next_ready", "now_ready", "out_ready", "p_norm", "part_out", "rows_made", "pool_steps",
          "prod_ready", "rope_ready", "s_done", "sel_ready", "selg_ready", "sig_done", "sig_ready",
          "slots_ready", "ssq_ready", "std_ready", "table_ready", "trig_ready", "u_gelu", "u_ready",
          "v_gelu", "var_ready", "vec_steps", "vn_ready", "vp_ready", "ws_masked", "x2_ready", "xT_ready",
          "xe_ready", "xg_done", "xn_ready", "xt_done", "y2_ready", "y_ready")


def bass_hybrid_layer(nc, x, c, positions, w_ada, b_ada, g_norm1, w_in, b_in, ln_v_g, ln_v_b,
                      w_spatial, b_spatial, sinks, w_o_a, w_o_b, w_out, g_norm2, w_router,
                      b_router, w_gate_up, b_gate_up, w_down, b_down, g_final, out):
    RING = 3
    items = []
    for j in range(4):
        items.append((f"ada{j}", w_ada[0, :, j * COLS:(j + 1) * COLS], None))
    ADA_AFTER = {"v0": 4, "v1": 5, "u0": 6, "u1": 7, "q0": 8, "q1": 9, "kv": 10, "ga0": 11}

    OFF_V, OFF_Q, OFF_K, OFF_GA, OFF_GB = 1024, 2048, 3072, 3328, 4352
    def add_item(name, w, b=None):
        items.append((name, w, b))
        if name in ADA_AFTER:
            j = ADA_AFTER[name]
            items.append((f"ada{j}", w_ada[0, :, j * COLS:(j + 1) * COLS], None))

    for name, off, w in [("v0", OFF_V, 512), ("v1", OFF_V + 512, 512), ("u0", 0, 512), ("u1", 512, 512),
                         ("q0", OFF_Q, 512), ("q1", OFF_Q + 512, 512), ("kv", OFF_K, 256),
                         ("ga0", OFF_GA, 512), ("ga1", OFF_GA + 512, 512),
                         ("gb0", OFF_GB, 512), ("gb1", OFF_GB + 512, 512)]:
        add_item(name, w_in[0, :, off:off + w], b_in[0:1, off:off + w])
    for name, w in [("oa", w_o_a), ("ob", w_o_b), ("out", w_out)]:
        for j in range(2):
            add_item(f"{name}{j}", w[0, :, j * COLS:(j + 1) * COLS])
    names = [n for n, _, _ in items]
    biased = [n for n, _, b in items if b is not None]

    def ring_slot(name):
        n = names.index(name)
        return n % RING, 16 * (n // RING + 1)

    z_order = [f"xT{t}{h}" for t in range(TILES) for h in range(2)]
    z_order += ["v0t0", "v0t1", "v1t0", "am4", "v1t1", "u0t0", "am5", "u0t1", "u1t0", "am6", "u1t1"]
    z_order += [f"f{t}{h}" for t in range(TILES) for h in range(2)]
    z_order += ["am7", "q0t0", "q0t1", "q1t0", "am8", "q1t1", "kvt0", "am9", "kvt1", "ga0t0", "am10", "ga0t1", "am11"]
    for n in ["ga1", "gb0", "gb1", "oa0", "oa1", "ob0", "ob1"]:
        z_order += [f"{n}t{t}" for t in range(TILES)]
    z_order += [f"bc{s}{h}" for s in (2, 3, 4, 5) for h in range(2)]
    z_order += [f"out{j}t{t}" for j in range(2) for t in range(TILES)]
    z_order += ["logits", "rank", "starts", "etab"]
    t_order = ["ws0", "ws1"]
    t_order += [f"ya{t}{h}" for t in range(TILES) for h in range(2)]
    t_order += [f"q{t}{h}" for t in range(TILES) for h in range(2)] + ["k"]
    for n in range(NCH):
        t_order += [f"p{n}0", f"p{n}1", f"o{n}"]
    t_order += [f"m{t}{h}" for t in range(TILES) for h in range(2)]
    t_order += [f"h{t}{h}" for t in range(TILES) for h in range(2)] + ["gT"]

    ctx = ExitStack()
    with ctx:
        ctx.enter_context(nc.allow_non_contiguous_dma(reason="small columns"))

        def sb(name, shape, dt=F32):
            return ctx.enter_context(nc.sbuf_tensor(name, shape, dt))

        def sem(name):
            return ctx.enter_context(nc.semaphore(name))

        gate_up = [sb(f"gate_up{s}", [P, KC, 2 * FF]) for s in range(2)]
        down = sb("down", [P, KC, D])
        ring = gate_up[1][:, 0:6, :].rearrange("p (s a) (b n) -> p s (a b) n", s=RING, n=COLS)
        spare = gate_up[1][:, 6:8, :].rearrange("p a b -> p (a b)")
        hT = down[:, 0:2, :].rearrange("p a (b n) -> p (a b) n", n=S)
        v_buf = down[:, 2:4, :]
        u_buf = down[:, 4:6, :]
        q_buf = down[:, 6:8, :]

        def as_T(buf):
            return buf.rearrange("p a (b n) -> p (a b) n", n=S)

        ws = spare[:, 0:1024].rearrange("p (h n) -> p h n", h=H)
        probs = spare[:, 0:1024].rearrange("p (r g n) -> p r g n", r=2, g=4)
        wsT = spare[:, 1024:2048].rearrange("p (h n) -> p h n", h=H)
        probsT = spare[:, 2048:3072].rearrange("p (r g n) -> p r g n", r=2, g=4)
        row_sel = spare[:, 3072:3584].rearrange("p (q n) -> p q n", q=NQT)
        tri = spare[:, 3584:3712]
        ones = spare[:, 3712:3840]
        wr = spare[:, 3840:4096].rearrange("p (k e) -> p k e", k=KC)

        x_sb = sb("x_sb", [P, TILES, D])
        h2 = sb("h2", [P, TILES, D])
        ln_gb = h2
        gt2 = sb("gt2", [P, D])
        bias_ring = gt2[:, :].rearrange("p (s n) -> p s n", s=2)
        front = sb("front", [P, 4 * D])
        sig_a = front[:, 0:2048].rearrange("p (t n) -> p t n", t=TILES)
        sig_b = front[:, 2048:4096].rearrange("p (t n) -> p t n", t=TILES)
        gt1 = front[:, 0:1024]
        mul2 = front[:, 1024:2048]
        sh2 = front[:, 2048:3072]
        g2bc = front[:, 3072:4096]
        mod = sb("mod", [P, 12, P])
        exp_bias = sb("exp_bias", [P, HW])
        kv = exp_bias[:, :].rearrange("p (t n) -> p t n", t=TILES)
        kT = h2[:, 0, 0:512].rearrange("p (g n) -> p g n", g=NKV)
        kd = h2[:, 0, 512:1024].rearrange("p (t g u d) -> p t g u d", t=TILES, g=NKV, u=2)
        vp = spare[:, 1920:2048]
        rope_room = spare[:, 1024:1536]
        b_down_sb = mod[0:E, 0:8, :].rearrange("p a b -> p (a b)")
        xT = mod[:, 0:4, :].rearrange("p i (h n) -> p i h n", h=NH)
        hidT = mod[:, 4:8, :].rearrange("p i (h n) -> p i h n", h=NH)
        y_sb = mod[:, 8:12, :].rearrange("p a b -> p (a b)")
        crep = sb("crep", [P, KC, QR])
        ident = sb("ident", [P, P])
        quarter_head = sb("quarter_head", [P, QR])

        def part(j):
            room = spare[:, 2048:3072] if j < 8 else h2[:, 1, :]
            return room[:, (j % 2) * COLS:(j % 2 + 1) * COLS]

        at = [0]

        def cut(n):
            at[0] += n
            return front[:, at[0] - n:at[0]]

        def by_tile(ap):
            return ap.rearrange("p (t n) -> p t n", t=TILES)
        iota_h = cut(P).rearrange("p (h j) -> p h j", h=NH)
        iota_g = cut(GMAX)
        slot_base = cut(GMAX)
        block_hot = cut(GMAX)
        slots_gates = cut(4 * E).rearrange("p (e n) -> p e n", n=4)
        tri_inc = cut(P)[0:E, :]
        tri_exc = cut(P)[0:E, :]
        sel = by_tile(cut(TILES * BM))
        selg = by_tile(cut(TILES * P))
        onehot = cut(BM)
        xe = cut(HW)
        gT = cut(TILES * P)
        slot_next, slot_now = cut(TILES), cut(TILES)
        router_at = at[0]
        g_cap, g_sig, hid = (cut(HW) for _ in range(3))
        assert at[0] <= 4 * D
        at[0] = router_at
        lg, lrep, mask, ex, gates, dtmp = (by_tile(cut(TILES * E)) for _ in range(6))
        top8 = by_tile(cut(TILES * 8))
        negtop, esum = cut(TILES), cut(TILES)
        nbB, stB, enB = cut(E), cut(E), cut(E)
        nbT = cut(P)[0:E, :]
        gatesT = by_tile(cut(TILES * P))[0:E]
        block_e, cmp = cut(GMAX), cut(GMAX)
        ncol = cut(4)
        assert at[0] <= 4 * D
        table = sb("table", [1, GMAX + 3 * E + 1], I32)

        sm = sb("sm", [P, 320])
        cat = [0]

        def col(n):
            cat[0] += n
            assert cat[0] <= 320
            return sm[:, cat[0] - n:cat[0]]
        c_col, c_act = col(KC), col(KC)
        g1_col = col(KC)
        mod_col = col(2 * KC).rearrange("p (s k) -> p s k", s=2)
        mul1 = col(KC)
        ssq, var, rstd, nt = col(TILES), col(TILES), col(TILES), col(TILES)
        stats = col(TILES * 12).rearrange("p (t n s) -> p t n s", t=TILES, n=2)
        mv = col(TILES * 2).rearrange("p (t s) -> p t s", t=TILES)
        bs = col(H)
        pos_f = col(TILES)
        invf = col(HALF)
        ang = col(TILES * HALF).rearrange("p (t f) -> p t f", t=TILES)
        kf = col(TILES * HALF).rearrange("p (t f) -> p t f", t=TILES)
        cos = col(TILES * HALF).rearrange("p (t f) -> p t f", t=TILES)
        sin = col(TILES * HALF).rearrange("p (t f) -> p t f", t=TILES)
        sk = col(8).rearrange("p (r g) -> p r g", r=2)
        mx = col(8).rearrange("p (r g) -> p r g", r=2)
        negm = col(8).rearrange("p (r g) -> p r g", r=2)
        den = col(8).rearrange("p (r g) -> p r g", r=2)
        es = col(8).rearrange("p (r g) -> p r g", r=2)
        br = col(E)
        pos_i = sb("pos_i", [P, TILES], I32)
        banks = [ctx.enter_context(nc.psum_tensor(f"bank{i}", [P, COLS], F32)) for i in range(8)]
        NZ = 4

        x_in, cond_in, gmlp_in, attn_in, route_in = (sem(n) for n in ("x_in", "cond_in", "gmlp_in", "attn_in", "route_in"))
        c_in, b_ada_in, ln_in, g2_in, gf_in, bd_in, stored = (sem(n) for n in ("c_in", "b_ada_in", "ln_in", "g2_in", "gf_in", "bd_in", "stored"))
        exp_bias_in = sem("exp_bias_in")
        ring_in = [sem(f"ring_in{i}") for i in range(RING)]
        bias_in = [sem(f"bias_in{i}") for i in range(2)]
        z_full = [sem(f"z_full{i}") for i in range(NZ)]
        z_free = [sem(f"z_free{i}") for i in range(NZ)]
        t_full = [sem(f"t_full{i}") for i in range(2)]
        t_free = [sem(f"t_free{i}") for i in range(2)]
        gu_in = [[sem(f"gu_in{s}_{i}") for i in range(4)] for s in range(2)]
        dn_in = [sem(f"dn_in{i}") for i in range(4)]
        evs = {}

        def ev(name):
            if name not in evs:
                evs[name] = sem(name)
            return evs[name]

        def z_use(name):
            k = z_order.index(name)
            return k % NZ, k // NZ + 1

        def t_use(name):
            k = t_order.index(name)
            return k % 2, k // 2 + 1

        def z_wait(eng, name):
            b, n = z_use(name)
            eng.wait_ge(z_full[b], n)
            return banks[b]

        def t_wait(eng, name):
            b, n = t_use(name)
            eng.wait_ge(t_full[b], n)
            return banks[6 + b]

        def z_gone(eng, name):
            b, n = z_use(name)
            eng.wait_ge(z_free[b], n)

        def t_gone(eng, name):
            b, n = t_use(name)
            eng.wait_ge(t_free[b], n)

        def item_used(eng, name):
            if name.startswith("ada"):
                eng.wait_ge(ev("ada_made"), int(name[3:]) + 1)
            else:
                z_wait(eng, name + "t1")

        def z_done(ins, name):
            ins.then_inc(z_free[z_use(name)[0]], 1)

        def t_done(ins, name):
            ins.then_inc(t_free[t_use(name)[0]], 1)

        for n in EVENTS:
            ev(n)
        block = ctx.enter_context(nc.Block())

        yaT, ybT, mT, h2T = as_T(v_buf), as_T(q_buf), hT, hT
        qT = u_buf.rearrange("p a (c k q) -> p (a c) k q", c=2, q=CH)
        merged = u_buf

        w_gu_view = w_gate_up[0].rearrange("e (k p) n -> p e k n", p=P)
        w_dn_view = w_down[0].rearrange("e (k p) n -> p e k n", p=P)

        def last_pieces(eng, at):
            return eng.value_load(table[0:1, at], min_val=1, max_val=4 * GMAX)

        def pieces_used(eng, used, pieces, i):
            eng.wait_ge(ev(used), pieces + i)

        def load_gate_up(eng, e, s, pieces):
            for i in range(4):
                pieces_used(eng, "gu_used", pieces, i)
                eng.dma_start(gate_up[s][:, 2 * i:2 * i + 2, :],
                              w_gu_view[:, bass.ds(e, 1), 2 * i:2 * i + 2, :].rearrange("p a k n -> p (a k) n"))\
                   .then_inc(gu_in[s][i], 16)

        def load_down(eng, e, pieces=None):
            for i in range(4):
                if pieces is not None:
                    pieces_used(eng, "down_used", pieces, i)
                eng.dma_start(down[:, 2 * i:2 * i + 2, :],
                              w_dn_view[:, bass.ds(e, 1), 2 * i:2 * i + 2, :].rearrange("p a k n -> p (a k) n"))\
                   .then_inc(dn_in[i], 16)

        @block.sync
        def _(sp):
            sp.dma_start(c_col, c[0].rearrange("(k p) -> p k", p=P)).then_inc(c_in, 16)
            sp.dma_start(x_sb[:, :, :], x[0].rearrange("(t p) d -> p t d", p=P)).then_inc(x_in, 16)
            sp.wait_ge(cond_in, 80)
            nb = 0
            prefetch = ("gb0", "gb1", "oa0", "oa1")
            for n, (name, w, b) in enumerate(items):
                if n >= RING:
                    item_used(sp, names[n - RING])
                cols = w.shape[1]
                sp.dma_start(ring[:, n % RING, :, 0:cols],
                             w.rearrange("(k p) n -> p k n", p=P)).then_inc(ring_in[n % RING], 16)
                if b is not None:
                    if nb >= 2:
                        z_gone(sp, biased[nb - 2] + "t1")
                    sp.dma_start(bias_ring[:, nb % 2, 0:cols],
                                 b.to_broadcast([P, cols])).then_inc(bias_in[nb % 2], 16)
                    nb += 1
                if name in prefetch:
                    i = prefetch.index(name)
                    sp.dma_start(gate_up[0][:, 2 * i:2 * i + 2, :],
                                 w_gu_view[:, 0, 2 * i:2 * i + 2, :]).then_inc(gu_in[0][i], 16)
            def first_gate_up(i):
                sp.dma_start(gate_up[1][:, 2 * i:2 * i + 2, :],
                             w_gu_view[:, 1, 2 * i:2 * i + 2, :]).then_inc(gu_in[1][i], 16)

            def first_down(i):
                sp.dma_start(down[:, 2 * i:2 * i + 2, :],
                             w_dn_view[:, 0, 2 * i:2 * i + 2, :]).then_inc(dn_in[i], 16)
            item_used(sp, "ob1")
            first_gate_up(ring_slot("ob1")[0])
            first_down(1)
            first_down(3)
            for name in ("out0", "out1"):
                item_used(sp, name)
                first_gate_up(ring_slot(name)[0])
            sp.wait_ge(ev("x2_ready"), TILES)
            first_down(2)
            z_wait(sp, "logits")
            first_down(0)
            sp.wait_ge(ev("table_ready"), 1)
            sp.wait_ge(ev("slots_ready"), 1)
            first_gate_up(3)

            pieces = last_pieces(sp, slice(GMAX + 2 * E, GMAX + 2 * E + 1))
            load_down(sp, 1, pieces)
            with sp.Fori(1, E // 2) as p:
                for s in range(2):
                    e = p * 2 + s
                    pieces = last_pieces(sp, bass.ds(p * 2 + (s - 2 + GMAX + 2 * E), 1))
                    load_gate_up(sp, e, s, pieces)
                    pieces = last_pieces(sp, bass.ds(p * 2 + (s - 1 + GMAX + 2 * E), 1))
                    load_down(sp, e, pieces)
            pieces = last_pieces(sp, slice(GMAX + 2 * E + 30, GMAX + 2 * E + 31))
            pieces_used(sp, "gu_used", pieces, 3)
            sp.dma_start(gate_up[0][:, 0, 0:D], g_final.rearrange("(a d) -> a d", a=1).to_broadcast([P, D]))\
              .then_inc(gf_in, 16)
            for t in range(TILES):
                sp.wait_ge(ev("out_ready"), t + 1)
                sp.dma_start(out[0, t * P:(t + 1) * P, :], h2[:, t, :]).then_inc(stored, 16)
            sp.wait_ge(stored, 16 * TILES)

        @block.gpsimd
        def _(pool):
            pool.memset(ident[:, :], 0.0).then_inc(ev("pool_steps"), 1)
            pool.memset(tri, 1.0).then_inc(ev("pool_steps"), 1)
            pool.memset(row_sel, 0.0).then_inc(ev("pool_steps"), 1)
            pool.memset(ones, 1.0).then_inc(ev("pool_steps"), 1)
            for f in range(HALF):
                pool.memset(invf[:, f:f + 1], float(np.float32(THETA ** (-f / HALF)))).then_inc(ev("pool_steps"), 1)
            pool.wait_ge(ev("pool_steps"), 4 + HALF)
            pool.affine_select(out=ident[:, :], in_=ident[:, :], compare_op=ALU.not_equal, fill=1.0, base=0,
                               pattern=[[-1, P]], channel_multiplier=1).then_inc(ev("consts"), 1)
            pool.affine_select(out=tri, in_=tri, compare_op=ALU.is_gt, fill=0.0, base=0,
                               pattern=[[1, P]], channel_multiplier=-1).then_inc(ev("consts"), 1)
            pool.affine_select(out=row_sel, in_=row_sel, compare_op=ALU.not_equal, fill=1.0, base=0,
                               pattern=[[-QR, NQT], [0, P]], channel_multiplier=1).then_inc(ev("consts"), 1)
            pool.wait_ge(gmlp_in, 32)
            pool.memset(ws[0:CH, :, CH:P], 0.0).then_inc(ev("ws_masked"), 1)
            pool.wait_ge(ev("h2_ready"), TILES)
            pool.iota(iota_h, pattern=[[0, NH], [1, BM]], base=0, channel_multiplier=0,
                      allow_small_or_imprecise_dtypes=True).then_inc(ev("counters"), 1)
            pool.iota(iota_g, pattern=[[1, GMAX]], base=0, channel_multiplier=0,
                      allow_small_or_imprecise_dtypes=True).then_inc(ev("counters"), 1)
            pool.iota(slot_base, pattern=[[BM, GMAX]], base=0, channel_multiplier=0,
                      allow_small_or_imprecise_dtypes=True).then_inc(ev("counters"), 1)
            pool.memset(tri_inc, 1.0).then_inc(ev("pool_steps"), 1)
            pool.memset(tri_exc, 1.0).then_inc(ev("pool_steps"), 1)
            pool.wait_ge(ev("pool_steps"), 6 + HALF)
            pool.affine_select(out=tri_inc, in_=tri_inc, compare_op=ALU.is_ge, fill=0.0, base=0,
                               pattern=[[0, NQT], [1, E]], channel_multiplier=-1).then_inc(ev("counters"), 1)
            pool.affine_select(out=tri_exc, in_=tri_exc, compare_op=ALU.is_gt, fill=0.0, base=0,
                               pattern=[[0, NQT], [1, E]], channel_multiplier=-1).then_inc(ev("counters"), 1)

        @block.scalar
        def _(act):
            act.dma_start(g1_col, g_norm1[0].rearrange("(k p) -> p k", p=P)).then_inc(cond_in, 16)
            b_ada_rows = b_ada[0].rearrange("(j q n) -> q j n", j=12, q=NQT)

            def load_b_ada(j0, j1, sem):
                for q in range(NQT):
                    act.dma_start(mod[q * QR:(q + 1) * QR, j0:j1, :],
                                  b_ada_rows[q:q + 1, j0:j1, :].to_broadcast([QR, j1 - j0, P])).then_inc(sem, 16)
            load_b_ada(0, 4, cond_in)
            act.dma_start(ws, w_spatial[0].rearrange("h i j -> i h j")).then_inc(gmlp_in, 16)
            act.dma_start(bs, b_spatial[0].rearrange("h i -> i h")).then_inc(gmlp_in, 16)
            act.dma_start(pos_i[:, :], positions[0].rearrange("(t p) -> p t", p=P)).then_inc(attn_in, 16)
            for hh in range(2):
                for r in range(2):
                    act.dma_start(sk[hh * CH:(hh + 1) * CH, r, :],
                                  sinks[0:1, :].rearrange("a (g m) -> a m g", m=4)[:, 2 * hh + r, :].to_broadcast([CH, 4]))\
                       .then_inc(attn_in, 16)
            act.dma_start(wr, w_router[0].rearrange("(k p) e -> p k e", p=P)).then_inc(route_in, 16)
            act.dma_start(br, b_router[0:1, :].to_broadcast([P, E])).then_inc(route_in, 16)
            load_b_ada(4, 12, b_ada_in)

            def part_copy(j):
                act.wait_ge(ev("ada_made"), j + 1)
                if j in (8, 9):
                    act.wait_ge(ev("vn_ready"), TILES)
                if 2 <= j < 6:
                    act.wait_ge(ev("rows_made"), j - 1)
                elif j >= 6:
                    z_wait(act, f"am{j - 2}")
                act.activation(part(j), banks[4 + j % 2][:, :], ACT.Copy).then_inc(ev("part_out"), 1)

            act.wait_ge(c_in, 16)
            act.activation(c_act, c_col, ACT.Silu).then_inc(ev("c_act_ready"), 1)
            act.wait_ge(x_in, 16)
            for t in range(TILES):
                act.activation(q_buf[:, t, :], x_sb[:, t, :], ACT.Square, accum_out=ssq[:, t:t + 1])\
                   .then_inc(ev("ssq_ready"), 1)
            act.wait_ge(ev("var_ready"), 1)
            act.activation(rstd, var, ACT.Sqrt).then_inc(ev("std_ready"), 1)
            for j in range(4):
                part_copy(j)
            act.wait_ge(ev("mod_col_ready"), 2)
            for h in range(2):
                name = f"xT1{h}"
                bank = z_wait(act, name)
                for i in range(4):
                    k = 4 * h + i
                    last = act.activation(hT[:, k, P:2 * P], bank[:, i * P:(i + 1) * P], ACT.Identity,
                                          bias=mod_col[:, 0, k:k + 1], scale=mul1[:, k:k + 1])
                z_done(last, name)
            for t in range(TILES):
                z_wait(act, f"xT{t}1")
            act.dma_start(ln_gb[:, 0, :], ln_v_g[0:1, :].to_broadcast([P, D])).then_inc(ln_in, 16)
            act.dma_start(ln_gb[:, 1, :], ln_v_b[0:1, :].to_broadcast([P, D])).then_inc(ln_in, 16)
            for h in range(2):
                bank = t_wait(act, f"ws{h}")
                t_done(act.activation(wsT[:, 4 * h:4 * h + 4, :].rearrange("p h n -> p (h n)"), bank[:, :], ACT.Copy),
                       f"ws{h}")
            for j in range(2):
                for t in range(TILES):
                    z_gone(act, f"v{j}t{t}")
                    act.activation(v_buf[:, t, j * COLS:(j + 1) * COLS], v_buf[:, t, j * COLS:(j + 1) * COLS],
                                   ACT.Gelu).then_inc(ev("v_gelu"), 1)
                part_copy(4 + j)
            act.wait_ge(ev("var_ready"), 2)
            act.activation(rstd, var, ACT.Sqrt).then_inc(ev("std_ready"), 1)
            for j in range(2):
                for t in range(TILES):
                    z_gone(act, f"u{j}t{t}")
                    act.activation(u_buf[:, t, j * COLS:(j + 1) * COLS], u_buf[:, t, j * COLS:(j + 1) * COLS],
                                   ACT.Gelu).then_inc(ev("u_gelu"), 1)
                part_copy(6 + j)
            act.wait_ge(ev("angle_ready"), 1)
            act.activation(sin, ang, ACT.Sin).then_inc(ev("trig_ready"), 1)
            act.activation(cos, ang, ACT.Sin, scale=0.5).then_inc(ev("trig_ready"), 1)

            def copy_T(dst, kind):
                for t in range(TILES):
                    for h in range(2):
                        name = f"{kind}{t}{h}"
                        bank = t_wait(act, name)
                        t_done(act.activation(dst[:, 4 * h:4 * h + 4, t * P:(t + 1) * P],
                                              bank[:, :].rearrange("p (k n) -> p k n", k=4), ACT.Copy), name)
            copy_T(yaT, "ya")
            for j in range(8, 12):
                part_copy(j)
            for t in range(TILES):
                for h in range(2):
                    name = f"q{t}{h}"
                    bank = t_wait(act, name)
                    t_done(act.activation(qT[:, 2 * t:2 * t + 2, 4 * h:4 * h + 4, :],
                                          bank[:, :].rearrange("p (k c q) -> p c k q", k=4, c=2), ACT.Copy), name)
            bank = t_wait(act, "k")
            t_done(act.activation(kT, bank[:, :].rearrange("p (g n) -> p g n", g=NKV), ACT.Copy), "k")
            for n in range(NCH):
                keys = CH if n == 0 else P
                act.wait_ge(ev("negm_ready"), n + 1)
                for r in range(2):
                    for g in range(4):
                        act.activation(probs[:, r, g, 0:keys], banks[4 + r][:, g * P:g * P + keys], ACT.Exp,
                                       bias=negm[:, r, g:g + 1], scale=1.0 / math.sqrt(CH),
                                       accum_out=den[:, r, g:g + 1]).then_inc(ev("exp_done"), 1)
                act.activation(es, es, ACT.Exp).then_inc(ev("exp_done"), 1)
                if n:
                    t_wait(act, f"o{n - 1}")
                for r in range(2):
                    name = f"p{n}{r}"
                    bank = t_wait(act, name)
                    t_done(act.activation(probsT[0:keys, r, :, :].rearrange("p g n -> p (g n)"), bank[0:keys, :],
                                          ACT.Copy), name)
            for sig, kind in ((sig_a, "ga"), (sig_b, "gb")):
                for t in range(TILES):
                    for j in range(2):
                        z_gone(act, f"{kind}{j}t{t}")
                    act.activation(sig[:, t, :], sig[:, t, :], ACT.Sigmoid).then_inc(ev("sig_done"), 1)
            z_gone(act, "kvt1")
            for n in range(NCH):
                t_wait(act, f"o{n}")
            b_gu_rows = b_gate_up[0].rearrange("e (a n) -> e a n", a=2)
            for h in range(NH):
                for a in range(2):
                    q = 2 * h + a
                    act.dma_start(exp_bias[q * QR:(q + 1) * QR, :], b_gu_rows[:, a, h * HW:(h + 1) * HW])\
                       .then_inc(exp_bias_in, 16)
            act.wait_ge(ev("merged_ready"), 2 * TILES)
            act.dma_start(g2bc, g_norm2[0:1, :].to_broadcast([P, D])).then_inc(g2_in, 16)
            copy_T(mT, "m")
            for name, dst in (("bc2", gt1), ("bc3", sh2)):
                for h in range(2):
                    bank = z_wait(act, f"{name}{h}")
                    z_done(act.activation(dst[:, h * COLS:(h + 1) * COLS], bank[:, :], ACT.Copy), f"{name}{h}")
            for h in range(2):
                bank = z_wait(act, f"bc5{h}")
                z_done(act.activation(gt2[:, h * COLS:(h + 1) * COLS], bank[:, :], ACT.Copy), f"bc5{h}")
            z_wait(act, "bc51")
            act.dma_start(b_down_sb, b_down[0]).then_inc(bd_in, 16)
            for t in range(TILES):
                act.wait_ge(ev("x2_ready"), t + 1)
                act.activation(h2[:, t, :], x_sb[:, t, :], ACT.Square, accum_out=ssq[:, t:t + 1])\
                   .then_inc(ev("ssq_ready"), 1)
            act.wait_ge(ev("var_ready"), 3)
            act.activation(rstd, var, ACT.Sqrt).then_inc(ev("std_ready"), 1)
            copy_T(h2T, "h")
            act.wait_ge(ev("negtop_ready"), 1)
            for t in range(TILES):
                act.activation(ex[:, t, :], lg[:, t, :], ACT.Exp, bias=negtop[:, t:t + 1]).then_inc(ev("ex_ready"), 1)
            bank = t_wait(act, "gT")
            t_done(act.activation(gatesT.rearrange("p t n -> p (t n)"), bank[0:E, 0:TILES * P], ACT.Copy), "gT")

            act.wait_ge(ev("xt_done"), 1)
            act.activation(xT.rearrange("p i h n -> p (i h n)"), banks[6][:, :], ACT.Copy)\
               .then_inc(ev("xT_ready"), 1)
            act.wait_ge(ev("table_ready"), 1)
            total = act.value_load(table[0:1, GMAX + 3 * E:GMAX + 3 * E + 1], min_val=1, max_val=GMAX - 1)
            with act.Fori(0, total) as g:
                act.wait_ge(ev("g_ready"), g + 1)
                act.activation(g_sig, g_cap, ACT.Sigmoid, scale=ALPHA).then_inc(ev("sig_ready"), 1)
                act.wait_ge(ev("ht_done"), g + 1)
                act.activation(hidT.rearrange("p i h n -> p (i h n)"), banks[7][:, :], ACT.Copy)\
                   .then_inc(ev("hidT_ready"), 1)
                act.wait_ge(ev("xt_done"), g + 2)
                act.activation(xT.rearrange("p i h n -> p (i h n)"), banks[6][:, :], ACT.Copy)\
                   .then_inc(ev("xT_ready"), 1)
                act.wait_ge(ev("down_used"), g * 4 + 4)
                act.activation(y_sb, banks[7][:, :], ACT.Copy).then_inc(ev("y_ready"), 1)

            for t in range(TILES):
                act.wait_ge(ev("y2_ready"), t + 1)
                act.activation(h2[:, t, :], x_sb[:, t, :], ACT.Square, accum_out=ssq[:, t:t + 1])\
                   .then_inc(ev("ssq_ready"), 1)
            act.wait_ge(ev("var_ready"), 4)
            act.activation(rstd, var, ACT.Sqrt).then_inc(ev("std_ready"), 1)

        @block.vector
        def _(dve):
            steps = [0]

            def link(ins):
                steps[0] += 1
                ins.then_inc(ev("vec_steps"), 1)
                dve.wait_ge(ev("vec_steps"), steps[0])

            norms = [0]

            def inverse_std(var_from_ssq):
                norms[0] += 1
                if var_from_ssq:
                    dve.wait_ge(ev("ssq_ready"), {1: 2, 3: 4, 4: 6}[norms[0]])
                    dve.tensor_scalar(var, ssq, 1.0 / D, EPS, ALU.mult, ALU.add).then_inc(ev("var_ready"), 1)
                else:
                    dve.tensor_scalar(var, mv[:, :, 1], 1.0, EPS, ALU.mult, ALU.add).then_inc(ev("var_ready"), 1)
                dve.wait_ge(ev("std_ready"), norms[0])
                link(dve.reciprocal(rstd, rstd))
                link(dve.tensor_tensor(nt, rstd, rstd, ALU.mult))
                link(dve.tensor_tensor(nt, nt, var, ALU.mult))
                link(dve.tensor_scalar(nt, nt, -0.5, 1.5, ALU.mult, ALU.add))
                link(dve.tensor_tensor(rstd, rstd, nt, ALU.mult))

            link(dve.memset(h2[:, 0, 0:QR], 1.0))
            dve.wait_ge(ev("c_act_ready"), 1)
            for k in range(KC):
                last = dve.tensor_scalar(crep[:, k, :], h2[:, 0, 0:QR], c_act[:, k:k + 1], None, ALU.mult)
            last.then_inc(ev("crep_ready"), 1)
            dve.wait_ge(ev("crep_ready"), 1)
            dve.wait_ge(ev("consts"), 3)
            link(dve.tensor_tensor(quarter_head[:, :], row_sel[:, 0, 0:QR], row_sel[:, 1, 0:QR], ALU.add))
            link(dve.tensor_tensor(quarter_head[:, :], quarter_head[:, :], row_sel[:, 2, 0:QR], ALU.add))
            dve.tensor_tensor(quarter_head[:, :], quarter_head[:, :], row_sel[:, 3, 0:QR], ALU.add)\
               .then_inc(ev("heads_ready"), 1)
            inverse_std(True)
            for t in range(TILES):
                dve.tensor_scalar(h2[:, t, :], x_sb[:, t, :], rstd[:, t:t + 1], None, ALU.mult).then_inc(ev("xn_ready"), 1)
            dve.wait_ge(attn_in, 80)
            dve.wait_ge(ev("consts"), 1)
            link(dve.tensor_copy(pos_f, pos_i[:, :]))
            for t in range(TILES):
                last = dve.tensor_scalar(ang[:, t, :], invf, pos_f[:, t:t + 1], None, ALU.mult)
            link(last)
            link(dve.tensor_scalar(kf, ang, 1.0 / (2 * math.pi), BIG, ALU.mult, ALU.add))
            link(dve.tensor_scalar(kf, kf, BIG, None, ALU.subtract))
            c1 = 6.28125
            c2 = float(np.float32(math.floor((2 * math.pi - c1) * 2 ** 20) / 2 ** 20))
            c3 = float(np.float32(2 * math.pi - c1 - c2))
            for part in (c1, c2, c3):
                link(dve.scalar_tensor_tensor(ang, kf, -part, ang, ALU.mult, ALU.add))
            dve.tensor_scalar(ang, ang, -3.1415925, 3.1415925, ALU.max, ALU.min).then_inc(ev("angle_ready"), 1)
            dve.wait_ge(cond_in, 16 * 5)
            dve.wait_ge(ev("rows_made"), 4)
            dve.tensor_tensor(mod[:, 0:4, :].rearrange("p j n -> p (j n)"), mod[:, 0:4, :].rearrange("p j n -> p (j n)"),
                              banks[6][:, :], ALU.add).then_inc(ev("ada_added"), 1)
            dve.wait_ge(ev("modT_done"), 1)
            link(dve.tensor_copy(mod_col.rearrange("p s k -> p (s k)"),
                                 banks[5][:, :].rearrange("p (m n) -> p m n", n=QR)[:, :, 0]))
            dve.scalar_tensor_tensor(mul1, mod_col[:, 1, :], 1.0, g1_col, ALU.add, ALU.mult)\
               .then_inc(ev("mod_col_ready"), 2)
            dve.wait_ge(ev("mod_col_ready"), 2)
            for h in range(2):
                name = f"xT0{h}"
                bank = z_wait(dve, name)
                for i in range(4):
                    k = 4 * h + i
                    last = dve.tensor_scalar(hT[:, k, 0:P], bank[:, i * P:(i + 1) * P], mul1[:, k:k + 1],
                                             mod_col[:, 0, k:k + 1], ALU.mult, ALU.add)
                z_done(last, name)

            def add_mod(j):
                bank = z_wait(dve, f"am{j}")
                z_done(dve.tensor_tensor(mod[:, j, :], mod[:, j, :], bank[:, 0:P], ALU.add), f"am{j}")

            def add_bias(item, dst, ada=None):
                n = biased.index(item)
                cols = 2 * P if item == "kv" else COLS
                dve.wait_ge(bias_in[n % 2], 16 * (n // 2 + 1))
                for t in range(TILES):
                    name = f"{item}t{t}"
                    bank = z_wait(dve, name)
                    z_done(dve.tensor_tensor(dst(t), bank[:, 0:cols], bias_ring[:, n % 2, 0:cols], ALU.add), name)
                    if t == 0 and ada:
                        add_mod(ada)

            def half(buf, j):
                return lambda t: buf[:, t, j * COLS:(j + 1) * COLS]

            add_bias("v0", half(v_buf, 0))
            dve.wait_ge(b_ada_in, 16 * NQT)
            add_bias("v1", half(v_buf, 1), 4)
            for t in range(TILES):
                for j in range(2):
                    dve.wait_ge(ev("v_gelu"), 2 * j + t + 1)
                    last = dve.bn_stats(stats[:, t, j, :], v_buf[:, t, j * COLS:(j + 1) * COLS])
            link(last)
            for t in range(TILES):
                last = dve.bn_aggr(mv[:, t, :], stats[:, t, :, :])
            link(last)
            add_bias("u0", half(u_buf, 0), 5)
            inverse_std(False)
            dve.wait_ge(ln_in, 32)
            for t in range(TILES):
                link(dve.tensor_scalar(v_buf[:, t, :], v_buf[:, t, :], mv[:, t, 0:1], rstd[:, t:t + 1],
                                       ALU.subtract, ALU.mult))
                link(dve.tensor_tensor(v_buf[:, t, :], v_buf[:, t, :], ln_gb[:, 0, :], ALU.mult))
                dve.tensor_tensor(v_buf[:, t, :], v_buf[:, t, :], ln_gb[:, 1, :], ALU.add).then_inc(ev("vn_ready"), 1)
            add_bias("u1", half(u_buf, 1), 6)
            for t in range(TILES):
                for h in range(2):
                    dve.wait_ge(ev("u_gelu"), 2 * h + t + 1)
                    name = f"f{t}{h}"
                    bank = z_wait(dve, name)
                    for i in range(4):
                        w = slice((4 * h + i) * P, (4 * h + i + 1) * P)
                        last = dve.scalar_tensor_tensor(u_buf[:, t, w], bank[:, i * P:(i + 1) * P],
                                                        bs[:, 4 * h + i:4 * h + i + 1], u_buf[:, t, w], ALU.add, ALU.mult)
                    z_done(last, name)
            add_mod(7)
            add_bias("q0", half(q_buf, 0))
            add_bias("q1", half(q_buf, 1), 8)
            add_bias("kv", lambda t: kv[:, t, :], 9)
            dve.wait_ge(ev("trig_ready"), 2)
            link(dve.tensor_tensor(cos, cos, cos, ALU.mult))
            link(dve.tensor_scalar(cos, cos, -2.0, 1.0, ALU.mult, ALU.add))
            for name in ("q0t1", "q1t1", "kvt1"):
                z_gone(dve, name)
            for t in range(TILES):
                for view, heads in ((q_buf[:, t, :].rearrange("p (h d) -> p h d", d=CH), NQ),
                                    (kv[:, t, 0:P].rearrange("p (h d) -> p h d", d=CH), NKV)):
                    t1, t2 = view[:, :, 0:HALF], view[:, :, HALF:2 * HALF]
                    shape = [P, heads, HALF]
                    co = cos[:, t, :].unsqueeze(1).to_broadcast(shape)
                    si = sin[:, t, :].unsqueeze(1).to_broadcast(shape)
                    a, b, cc, d = (rope_room[:, i * P:i * P + heads * HALF].rearrange("p (h f) -> p h f", f=HALF)
                                   for i in range(4))
                    dve.tensor_tensor(a, t1, co, ALU.mult)
                    dve.tensor_tensor(b, t2, si, ALU.mult)
                    dve.tensor_tensor(cc, t2, co, ALU.mult)
                    link(dve.tensor_tensor(d, t1, si, ALU.mult))
                    dve.tensor_tensor(t1, a, b, ALU.subtract)
                    link(dve.tensor_tensor(t2, cc, d, ALU.add))
                for u in range(2):
                    last = dve.tensor_copy(kd[:, t, :, u, :], kv[:, t, 0:P].rearrange("p (g d) -> p g d", g=NKV))
                last.then_inc(ev("rope_ready"), 1)

            def gates_out(n, t):
                item = ("ga0", "ga1", "gb0", "gb1")[n]
                dst = (sig_a, sig_a, sig_b, sig_b)[n][:, t, (n % 2) * COLS:(n % 2 + 1) * COLS]
                m = biased.index(item)
                dve.wait_ge(bias_in[m % 2], 16 * (m // 2 + 1))
                name = f"{item}t{t}"
                bank = z_wait(dve, name)
                z_done(dve.tensor_tensor(dst, bank[:, :], bias_ring[:, m % 2, :], ALU.add), name)

            def softmax_max(n):
                keys = CH if n == 0 else P
                dve.wait_ge(ev("s_done"), n + 1)
                for r in range(2):
                    last = dve.tensor_reduce(mx[:, r, :], banks[4 + r][:, :].rearrange("p (g k) -> p g k", g=4)[:, :, 0:keys],
                                             AX.X, ALU.max)
                link(last)
                link(dve.scalar_tensor_tensor(mx, mx, 1.0 / math.sqrt(CH), sk, ALU.mult, ALU.max))
                link(dve.tensor_tensor(es, sk, mx, ALU.subtract))
                dve.tensor_scalar(negm, mx, -1.0, None, ALU.mult).then_inc(ev("negm_ready"), 1)

            def softmax_norm(n):
                keys = CH if n == 0 else P
                dve.wait_ge(ev("exp_done"), 9 * (n + 1))
                link(dve.tensor_tensor(den, den, es, ALU.add))
                link(dve.reciprocal(den, den))
                dve.tensor_tensor(probs[:, :, :, 0:keys].rearrange("p r g k -> p (r g) k"),
                                  probs[:, :, :, 0:keys].rearrange("p r g k -> p (r g) k"),
                                  den.rearrange("p r g -> p (r g)").unsqueeze(2).to_broadcast([P, 8, keys]), ALU.mult)\
                   .then_inc(ev("p_norm"), 1)

            def values(n):
                t = n // 2
                dve.tensor_copy(vp[0:CH, :], kv[0:CH, t, P:2 * P])
                dve.tensor_copy(vp[CH:P, :], kv[CH:P, t - 1, P:2 * P]).then_inc(ev("vp_ready"), 1)

            def attn_out(n):
                name = f"o{n}"
                bank = t_wait(dve, name)
                t_done(dve.tensor_copy(ybT[:, :, n * CH:(n + 1) * CH], bank[:, :].rearrange("p (k q) -> p k q", q=CH)), name)

            values(2)
            order = [(n, t) for n in range(4) for t in range(TILES)]
            gates_out(*order[0])
            add_mod(10)
            gates_out(*order[1])
            add_mod(11)
            softmax_max(0)
            softmax_norm(0)
            gates_out(*order[2])
            for n in range(1, NCH):
                softmax_max(n)
                gates_out(*order[2 * n + 1])
                attn_out(n - 1)
                softmax_norm(n)
                if 2 * n + 2 < 8:
                    gates_out(*order[2 * n + 2])
            attn_out(NCH - 1)

            for kind, sig, need in (("oa", sig_a, 2), ("ob", sig_b, 4)):
                dve.wait_ge(ev("sig_done"), need)
                for j in range(2):
                    for t in range(TILES):
                        w = slice(j * COLS, (j + 1) * COLS)
                        name = f"{kind}{j}t{t}"
                        bank = z_wait(dve, name)
                        if kind == "oa":
                            z_done(dve.tensor_tensor(merged[:, t, w], bank[:, :], sig[:, t, w], ALU.mult), name)
                        else:
                            z_done(dve.tensor_tensor(sig[:, t, w], bank[:, :], sig[:, t, w], ALU.mult), name)
                            z_gone(dve, name)
                            z_gone(dve, f"oa{j}t{t}")
                            dve.tensor_tensor(merged[:, t, w], merged[:, t, w], sig[:, t, w], ALU.add)\
                               .then_inc(ev("merged_ready"), 1)
            dve.wait_ge(g2_in, 16)
            for h in range(2):
                w = slice(h * COLS, (h + 1) * COLS)
                bank = z_wait(dve, f"bc4{h}")
                z_done(dve.scalar_tensor_tensor(mul2[:, w], bank[:, :], 1.0, g2bc[:, w], ALU.add, ALU.mult), f"bc4{h}")
            z_gone(dve, "bc21")
            z_gone(dve, "bc20")
            for j in range(2):
                for t in range(TILES):
                    w = slice(j * COLS, (j + 1) * COLS)
                    name = f"out{j}t{t}"
                    bank = z_wait(dve, name)
                    z_done(dve.tensor_tensor(merged[:, t, w], bank[:, :], gt1[:, w], ALU.mult), name)
                    z_gone(dve, name)
                    last = dve.tensor_tensor(x_sb[:, t, w], x_sb[:, t, w], merged[:, t, w], ALU.add)
                    if j:
                        last.then_inc(ev("x2_ready"), 1)
            inverse_std(True)
            for h in range(2):
                z_gone(dve, f"bc4{h}")
                z_gone(dve, f"bc3{h}")
            for t in range(TILES):
                link(dve.scalar_tensor_tensor(h2[:, t, :], x_sb[:, t, :], rstd[:, t:t + 1], mul2, ALU.mult, ALU.mult))
                dve.tensor_tensor(h2[:, t, :], h2[:, t, :], sh2, ALU.add).then_inc(ev("h2_ready"), 1)

            dve.wait_ge(ev("h2_ready"), TILES)
            bank = z_wait(dve, "logits")
            for t in range(TILES):
                last = dve.tensor_tensor(lg[:, t, :], bank[:, t * E:(t + 1) * E], br, ALU.add)
            z_done(last, "logits")
            z_gone(dve, "logits")
            for t in range(TILES):
                last = dve.max(top8[:, t, :], lg[:, t, :])
            link(last)
            dve.tensor_scalar(negtop, top8[:, :, 0], -1.0, None, ALU.mult).then_inc(ev("negtop_ready"), 1)
            link(dve.memset(top8[:, :, TOPK:8], 3.0e38))
            for t in range(TILES):
                link(dve.match_replace(lrep[:, t, :], top8[:, t, :], lg[:, t, :], -3.0e38))
            dve.tensor_tensor(mask, lg, lrep, ALU.not_equal).then_inc(ev("mask_ready"), 1)
            dve.wait_ge(ev("mask_ready"), 1)
            dve.wait_ge(ev("ex_ready"), TILES)
            link(dve.tensor_tensor(ex, ex, mask, ALU.mult))
            link(dve.tensor_reduce(esum, ex, AX.X, ALU.add))
            link(dve.reciprocal(esum, esum))
            for t in range(TILES):
                last = dve.tensor_scalar(gates[:, t, :], ex[:, t, :], esum[:, t:t + 1], None, ALU.mult)
            last.then_inc(ev("gates_ready"), 1)
            dve.wait_ge(ev("gates_ready"), 1)
            for t in range(TILES):
                dve.tensor_copy(slots_gates[:, :, 2 + t], gates[:, t, :])
            bank = z_wait(dve, "rank")

            def blocks_of(dst, counts):
                link(dve.tensor_scalar(dst, counts, BM / 2 - 0.5, 1.0 / BM, ALU.add, ALU.mult))
                link(dve.tensor_scalar(dst, dst, BIG, None, ALU.add))
                return dve.tensor_scalar(dst, dst, BIG, 1.0, ALU.subtract, ALU.max)
            blocks_of(nbT, bank[0:E, 2 * P:3 * P]).then_inc(ev("counts_ready"), 1)
            link(blocks_of(nbB, bank[:, 2 * E:3 * E]))
            dve.tensor_scalar(dtmp.rearrange("p t e -> p (t e)"), bank[:, 0:TILES * E], 1.0, None, ALU.add)\
               .then_inc(z_free[z_use("rank")[0]], 1)
            z_gone(dve, "rank")
            bank = z_wait(dve, "starts")
            dve.tensor_copy(stB, bank[:, 0:E])
            z_done(dve.tensor_copy(ncol, bank[:, 2 * E:2 * E + 4]), "starts")
            z_gone(dve, "starts")
            link(dve.tensor_tensor(enB, stB, nbB, ALU.add))
            dve.wait_ge(ev("counters"), 5)
            dve.tensor_scalar(cmp[0:E, :], iota_g[0:E, :], ncol[0:E, 2:3], None, ALU.is_ge).then_inc(ev("cmp_ready"), 1)
            for t in range(TILES):
                link(dve.scalar_tensor_tensor(dtmp[:, t, :], stB, float(BM), dtmp[:, t, :], ALU.mult, ALU.add))
                link(dve.tensor_tensor(dtmp[:, t, :], dtmp[:, t, :], mask[:, t, :], ALU.mult))
                link(dve.tensor_scalar(slots_gates[:, :, t], dtmp[:, t, :], -1.0, None, ALU.add))
            link(dve.tensor_scalar(block_hot, iota_g, ncol[:, 0:1], None, ALU.is_ge))
            link(dve.scalar_tensor_tensor(block_hot, iota_g, ncol[:, 2:3], block_hot, ALU.is_lt, ALU.mult))
            dve.tensor_copy(table[0:1, GMAX:GMAX + E], nbB[0:1, :])
            dve.tensor_copy(table[0:1, GMAX + E:GMAX + 2 * E], stB[0:1, :])
            dve.tensor_copy(table[0:1, GMAX + 3 * E:GMAX + 3 * E + 1], enB[0:1, E - 1:E])
            dve.tensor_scalar(table[0:1, GMAX + 2 * E:GMAX + 3 * E], enB[0:1, :], 4.0, -3.0, ALU.mult, ALU.add)\
               .then_inc(ev("slots_ready"), 1)
            dve.wait_ge(ev("slots_ready"), 1)
            bank = z_wait(dve, "etab")
            link(dve.tensor_scalar(block_e, bank[:, 0:GMAX], float(E - 1), None, ALU.min))
            dve.tensor_copy(table[0:1, 0:GMAX], block_e[0:1, :]).then_inc(ev("table_ready"), 1)
            dve.wait_ge(ev("table_ready"), 1)

            dve.memset(y_sb, 0.0).then_inc(ev("y_ready"), 1)
            dve.memset(gT, 0.0).then_inc(ev("gT_ready"), 1)

            def choose(g, slots, e):
                return dve.tensor_scalar(slots, slots_gates[:, bass.ds(e, 1), 0:2].rearrange("p a t -> p (a t)"),
                                         slot_base[:, bass.ds(g, 1)], None, ALU.subtract)

            def gather_map(g, slots):
                for t in range(TILES):
                    last = dve.tensor_scalar(sel[:, t, :], iota_h[:, 0, :], slots[:, t:t + 1], None, ALU.is_equal)
                return last

            def bias_map(g):
                return dve.tensor_scalar(onehot, iota_h[:, 0, :], 0.0, block_hot[:, bass.ds(g, 1)], ALU.mult, ALU.add)

            e0 = dve.value_load(table[0:1, 0:1], min_val=0, max_val=E - 1)
            choose(0, slot_next, e0).then_inc(ev("next_ready"), 1)
            dve.wait_ge(ev("next_ready"), 1)
            gather_map(0, slot_next).then_inc(ev("sel_ready"), 1)
            bias_map(0).then_inc(ev("hot_ready"), 1)
            dve.wait_ge(ev("xg_done"), 1)
            dve.tensor_copy(xe, banks[6][:, :]).then_inc(ev("xe_ready"), 1)
            total = dve.value_load(table[0:1, GMAX + 3 * E:GMAX + 3 * E + 1], min_val=1, max_val=GMAX - 1)
            with dve.Fori(0, total) as g:
                e_next = dve.value_load(table[0:1, bass.ds(g + 1, 1)], min_val=0, max_val=E - 1)
                e_now = dve.value_load(table[0:1, bass.ds(g, 1)], min_val=0, max_val=E - 1)
                choose(g + 1, slot_next, e_next).then_inc(ev("next_ready"), 1)
                choose(g, slot_now, e_now).then_inc(ev("now_ready"), 1)
                dve.wait_ge(ev("next_ready"), g + 2)
                dve.wait_ge(ev("xg_done"), g + 1)
                gather_map(g + 1, slot_next).then_inc(ev("sel_ready"), 1)
                dve.wait_ge(ev("now_ready"), g + 1)
                dve.wait_ge(ev("gT_ready"), g + 1)
                for t in range(TILES):
                    last = dve.tensor_scalar(selg[:, t, :].rearrange("p (h j) -> p h j", h=NH), iota_h,
                                             slot_now[:, t:t + 1],
                                             slots_gates[:, bass.ds(e_now, 1), 2 + t:3 + t].rearrange("p a t -> p (a t)"),
                                             ALU.is_equal, ALU.mult)
                last.then_inc(ev("selg_ready"), 1)
                dve.wait_ge(ev("gu_used"), g * 4 + 4)
                dve.tensor_scalar(g_cap, banks[4][:, :], LIMIT, None, ALU.min).then_inc(ev("g_ready"), 1)
                dve.tensor_scalar(hid, banks[5][:, :], -LIMIT, LIMIT, ALU.max, ALU.min).then_inc(ev("u_ready"), 1)
                bias_map(g + 1).then_inc(ev("hot_ready"), 1)
                dve.wait_ge(ev("u_ready"), g + 1)
                dve.scalar_tensor_tensor(hid, hid, 1.0, g_cap, ALU.add, ALU.mult).then_inc(ev("prod_ready"), 1)
                dve.wait_ge(ev("prod_ready"), g + 1)
                dve.wait_ge(ev("sig_ready"), g + 1)
                dve.tensor_tensor(hid, hid, g_sig, ALU.mult).then_inc(ev("hid_ready"), 1)
                dve.wait_ge(ev("xg_done"), g + 2)
                dve.tensor_copy(xe, banks[6][:, :]).then_inc(ev("xe_ready"), 1)
                dve.wait_ge(ev("gt_done"), g + 1)
                dve.tensor_copy(gT, banks[4][:, 0:TILES * P]).then_inc(ev("gT_ready"), 1)

            dve.wait_ge(ev("comb_done"), total + 1)
            for t in range(TILES):
                for h in range(NH):
                    w = slice(h * HW, (h + 1) * HW)
                    last = dve.tensor_tensor(h2[:, t, w], banks[2 * h + t][:, :], gt2[:, w], ALU.mult)
                link(last)
                dve.tensor_tensor(x_sb[:, t, :], x_sb[:, t, :], h2[:, t, :], ALU.add).then_inc(ev("y2_ready"), 1)
            inverse_std(True)
            dve.wait_ge(gf_in, 16)
            for t in range(TILES):
                dve.scalar_tensor_tensor(h2[:, t, :], x_sb[:, t, :], rstd[:, t:t + 1], gate_up[0][:, 0, 0:D],
                                         ALU.mult, ALU.mult).then_inc(ev("out_ready"), 1)

        @block.tensor
        def _(pe):
            def z_open(name):
                b, n = z_use(name)
                if n > 1:
                    pe.wait_ge(z_free[b], n - 1)
                return banks[b]

            def t_open(name):
                b, n = t_use(name)
                if n > 1:
                    pe.wait_ge(t_free[b], n - 1)
                return banks[6 + b]

            def z_put(ins, name):
                ins.then_inc(z_full[z_use(name)[0]], 1)

            def t_put(ins, name):
                ins.then_inc(t_full[t_use(name)[0]], 1)

            def weights(name):
                s, n = ring_slot(name)
                pe.wait_ge(ring_in[s], n)
                return ring[:, s]

            def rows_times(item, t, lhsT, cols=COLS):
                w = weights(item)
                name = f"{item}t{t}"
                bank = z_open(name)
                for k in range(KC):
                    last = pe.matmul(bank[:, 0:cols], lhsT[:, k, t * P:(t + 1) * P], w[:, k, 0:cols],
                                     start=(k == 0), stop=(k == KC - 1))
                z_put(last, name)

            def transposes(src, kind):
                for t in range(TILES):
                    for h in range(2):
                        name = f"{kind}{t}{h}"
                        bank = t_open(name)
                        for i in range(4):
                            k = 4 * h + i
                            last = pe.transpose(bank[:, i * P:(i + 1) * P], src[:, t, k * P:(k + 1) * P], ident[:, :])
                        t_put(last, name)

            def ada(j):
                w = weights(f"ada{j}")
                if j >= 2:
                    pe.wait_ge(ev("part_out"), j - 1)
                for a in range(2):
                    for q in range(NQT):
                        last = pe.matmul(banks[4 + j % 2][q * QR:(q + 1) * QR, :], crep[:, 4 * a + q, :],
                                         w[:, 4 * a + q, :], start=(a == 0), stop=(a == 1), skip_group_check=True)
                last.then_inc(ev("ada_made"), 1)

            def ada_rows(j, out):
                pe.wait_ge(ev("part_out"), j + 1)
                for q in range(NQT):
                    last = pe.matmul(out[q * QR:(q + 1) * QR, :], quarter_head[:, :], part(j)[:, q * P:(q + 1) * P],
                                     start=True, stop=True, skip_group_check=True)
                return last

            def late_rows(j):
                bank = z_open(f"am{j}")
                z_put(ada_rows(j, bank[:, 0:P]), f"am{j}")

            pe.wait_ge(ev("consts"), 3)
            pe.wait_ge(ev("xn_ready"), TILES)
            for t in range(TILES):
                for h in range(2):
                    name = f"xT{t}{h}"
                    bank = z_open(name)
                    for i in range(4):
                        k = 4 * h + i
                        last = pe.transpose(bank[:, i * P:(i + 1) * P], h2[:, t, k * P:(k + 1) * P], ident[:, :])
                    z_put(last, name)
            pe.wait_ge(ev("crep_ready"), 1)
            pe.wait_ge(ev("heads_ready"), 1)
            for j in range(4):
                ada(j)
                ada_rows(j, banks[6][:, j * P:(j + 1) * P]).then_inc(ev("rows_made"), 1)
            pe.wait_ge(ev("ada_added"), 1)
            for j in range(4):
                last = pe.transpose(banks[5][:, j * P:(j + 1) * P], mod[:, j, :], ident[:, :])
            last.then_inc(ev("modT_done"), 1)
            pe.wait_ge(ev("ws_masked"), 1)
            for h in range(2):
                name = f"ws{h}"
                bank = t_open(name)
                for i in range(4):
                    last = pe.transpose(bank[:, i * P:(i + 1) * P], ws[:, 4 * h + i, :], ident[:, :])
                t_put(last, name)
            for t in range(TILES):
                for h in range(2):
                    z_gone(pe, f"xT{t}{h}")

            for n, item in enumerate(("v0", "v1", "u0", "u1")):
                rows_times(item, 0, hT)
                if n:
                    late_rows(n + 3)
                rows_times(item, 1, hT)
                ada(n + 4)
            for h in range(2):
                t_gone(pe, f"ws{h}")
            pe.wait_ge(ev("vn_ready"), TILES)
            for t in range(TILES):
                for h in range(2):
                    name = f"f{t}{h}"
                    bank = z_open(name)
                    for i in range(4):
                        last = pe.matmul(bank[:, i * P:(i + 1) * P], wsT[:, 4 * h + i, :],
                                         v_buf[:, t, (4 * h + i) * P:(4 * h + i + 1) * P], start=True, stop=True,
                                         skip_group_check=True)
                    z_put(last, name)
            late_rows(7)
            for t in range(TILES):
                rows_times("q0", t, hT)
            for t in range(TILES):
                for h in range(2):
                    z_gone(pe, f"f{t}{h}")
            transposes(u_buf, "ya")
            ada(8)
            rows_times("q1", 0, hT)
            late_rows(8)
            rows_times("q1", 1, hT)
            ada(9)
            rows_times("kv", 0, hT, 2 * P)
            late_rows(9)
            rows_times("kv", 1, hT, 2 * P)
            ada(10)
            rows_times("ga0", 0, hT)
            late_rows(10)
            ada(11)
            pe.wait_ge(ev("rope_ready"), TILES)
            transposes(q_buf, "q")
            bank = t_open("k")
            for g in range(NKV):
                for t in range(TILES):
                    last = pe.transpose(bank[:, g * S + t * P:g * S + (t + 1) * P],
                                        kd[:, t, g, :, :].rearrange("p u d -> p (u d)"), ident[:, :])
            t_put(last, "k")
            rows_times("ga0", 1, hT)
            late_rows(11)

            def scores(n):
                if n == 0:
                    for t in range(TILES):
                        for h in range(2):
                            t_gone(pe, f"q{t}{h}")
                    t_gone(pe, "k")
                else:
                    pe.wait_ge(ev("exp_done"), 9 * n)
                for g in range(NKV):
                    for j in range(2):
                        for r in range(2):
                            rows = slice(r * CH, (r + 1) * CH)
                            col = (2 * g + j) * P
                            lhsT = qT[rows, n, 4 * g + 2 * j:4 * g + 2 * j + 2, :].rearrange("p k q -> p (k q)")
                            if n == 0:
                                parts = [(0, 0, CH)]
                            elif n % 2:
                                parts = [(0, (n - 1) * CH, P)]
                            else:
                                parts = [(0, n * CH, CH), (CH, (n - 1) * CH, CH)]
                            for off, key, width in parts:
                                last = pe.matmul(banks[4 + r][:, col + off:col + off + width], lhsT,
                                                 kT[rows, g, key:key + width], start=True, stop=True,
                                                 skip_group_check=True)
                last.then_inc(ev("s_done"), 1)

            def probs_T(n):
                keys = CH if n == 0 else P
                pe.wait_ge(ev("p_norm"), n + 1)
                for r in range(2):
                    name = f"p{n}{r}"
                    bank = t_open(name)
                    for g in range(4):
                        last = pe.transpose(bank[0:keys, g * P:(g + 1) * P], probs[:, r, g, 0:keys], ident[:, :])
                    t_put(last, name)

            def attend(n):
                keys = CH if n == 0 else P
                for r in range(2):
                    t_gone(pe, f"p{n}{r}")
                if n % 2 == 0 and n:
                    pe.wait_ge(ev("vp_ready"), 1)
                name = f"o{n}"
                bank = t_open(name)
                for g in range(NKV):
                    for r in range(2):
                        cols = slice(g * CH, (g + 1) * CH)
                        v = vp[0:keys, cols] if n % 2 == 0 and n else kv[0:keys, n // 2, P + g * CH:P + (g + 1) * CH]
                        last = pe.matmul(bank[r * CH:(r + 1) * CH, g * 256:(g + 1) * 256], v,
                                         probsT[0:keys, r, 2 * g:2 * g + 2, :].rearrange("p g n -> p (g n)"),
                                         start=True, stop=True, skip_group_check=True)
                t_put(last, name)

            scores(0)
            rows_times("ga1", 0, hT)
            probs_T(0)
            scores(1)
            rows_times("ga1", 1, hT)
            attend(0)
            rows_times("gb0", 0, hT)
            probs_T(1)
            scores(2)
            rows_times("gb0", 1, hT)
            attend(1)
            rows_times("gb1", 0, hT)
            probs_T(2)
            scores(3)
            rows_times("gb1", 1, hT)
            attend(2)
            rows_times("oa0", 0, yaT)
            probs_T(3)
            rows_times("oa0", 1, yaT)
            attend(3)
            for t in range(TILES):
                rows_times("oa1", t, yaT)
            for n in range(NCH):
                t_gone(pe, f"o{n}")
            for item in ("ob0", "ob1"):
                for t in range(TILES):
                    rows_times(item, t, ybT)
            pe.wait_ge(ev("merged_ready"), 2 * TILES)
            transposes(merged, "m")
            z_gone(pe, "am11")
            for s in (2, 3, 4, 5):
                for h in range(2):
                    name = f"bc{s}{h}"
                    bank = z_open(name)
                    for q in range(NQT):
                        last = pe.matmul(bank[:, q * P:(q + 1) * P], row_sel[:, q, :], mod[:, 2 * s + h, :],
                                         start=True, stop=True, skip_group_check=True)
                    z_put(last, name)
            for t in range(TILES):
                for h in range(2):
                    t_gone(pe, f"m{t}{h}")
            for item in ("out0", "out1"):
                for t in range(TILES):
                    rows_times(item, t, mT)

            pe.wait_ge(ev("h2_ready"), TILES)
            transposes(h2, "h")
            pe.wait_ge(route_in, 32)
            for t in range(TILES):
                for h in range(2):
                    t_gone(pe, f"h{t}{h}")
            bank = z_open("logits")
            for t in range(TILES):
                for k in range(KC):
                    last = pe.matmul(bank[:, t * E:(t + 1) * E], h2T[:, k, t * P:(t + 1) * P], wr[:, k, :],
                                     start=(k == 0), stop=(k == KC - 1), skip_group_check=True)
            z_put(last, "logits")
            pe.wait_ge(ev("mask_ready"), 1)
            bank = z_open("rank")
            pe.matmul(bank[:, 0:E], tri, mask[:, 0, :], start=True, stop=True, skip_group_check=True)
            pe.matmul(bank[:, E:2 * E], tri, mask[:, 1, :], start=True, stop=False, skip_group_check=True)
            pe.matmul(bank[:, E:2 * E], ones, mask[:, 0, :], start=False, stop=True, skip_group_check=True)
            for t in range(TILES):
                pe.matmul(bank[:, 2 * E:3 * E], ones, mask[:, t, :], start=(t == 0), stop=(t == 1), skip_group_check=True)
            for t in range(TILES):
                last = pe.matmul(bank[0:E, 2 * P:3 * P], mask[:, t, :], ones, start=(t == 0), stop=(t == 1),
                                 skip_group_check=True)
            z_put(last, "rank")
            pe.wait_ge(ev("gates_ready"), 1)
            bank = t_open("gT")
            for t in range(TILES):
                last = pe.transpose(bank[0:E, t * P:(t + 1) * P], gates[:, t, :], ident[:, :])
            t_put(last, "gT")
            pe.wait_ge(ev("counts_ready"), 1)
            pe.wait_ge(ev("counters"), 5)
            bank = z_open("starts")
            pe.matmul(bank[:, 0:E], nbT, tri_exc[:, 0:E], start=True, stop=True, skip_group_check=True)
            pe.matmul(bank[:, 2 * E:2 * E + 2], tri_exc, nbT[:, 0:2], start=True, stop=True, skip_group_check=True)
            last = pe.matmul(bank[:, 2 * E + 2:2 * E + 4], tri_inc, nbT[:, 0:2], start=True, stop=True,
                             skip_group_check=True)
            z_put(last, "starts")
            pe.wait_ge(ev("cmp_ready"), 1)
            bank = z_open("etab")
            last = pe.matmul(bank[:, 0:GMAX], ones[0:E, :], cmp[0:E, :], start=True, stop=True)
            z_put(last, "etab")

            pe.wait_ge(ev("table_ready"), 1)
            pe.wait_ge(bd_in, 16)
            t_gone(pe, "gT")
            for h in range(NH):
                for t in range(TILES):
                    last = pe.matmul(banks[2 * h + t][:, :], gatesT[:, t, :], b_down_sb[:, h * HW:(h + 1) * HW],
                                     start=True, stop=True, skip_group_check=True)
            last.then_inc(ev("acc_init"), 1)

            def gather():
                for t in range(TILES):
                    for h in range(NH):
                        last = pe.matmul(banks[6][h * BM:(h + 1) * BM, :], sel[:, t, :], h2[:, t, h * HW:(h + 1) * HW],
                                         start=(t == 0), stop=(t == 1), skip_group_check=True)
                last.then_inc(ev("xg_done"), 1)

            def gather_T():
                for i in range(4):
                    last = pe.transpose(banks[6][:, i * P:(i + 1) * P], xe[:, i * P:(i + 1) * P], ident[:, :])
                last.then_inc(ev("xt_done"), 1)

            def combine():
                for t in range(TILES):
                    for h in range(NH):
                        rows = slice(h * BM, (h + 1) * BM)
                        last = pe.matmul(banks[2 * h + t][:, :], gT[rows, t * P:(t + 1) * P], y_sb[rows, :],
                                         start=False, stop=True, skip_group_check=True)
                last.then_inc(ev("comb_done"), 1)

            pe.wait_ge(exp_bias_in, 64)
            pe.wait_ge(ev("sel_ready"), 1)
            gather()
            pe.wait_ge(ev("xe_ready"), 1)
            gather_T()
            with pe.Fori(0, E // 2) as p:
                for s in range(2):
                    first = pe.value_load(table[0:1, bass.ds(p * 2 + (s + GMAX + E), 1)], min_val=0, max_val=GMAX - 1)
                    blocks = pe.value_load(table[0:1, bass.ds(p * 2 + (s + GMAX), 1)], min_val=1, max_val=S // BM)
                    with pe.Fori(0, blocks) as b:
                        g = first + b
                        pe.wait_ge(ev("xT_ready"), g + 1)
                        pe.wait_ge(ev("hot_ready"), g + 1)
                        pe.wait_ge(ev("gT_ready"), g + 1)
                        for k in range(KC):
                            if k % 2 == 0:
                                pe.wait_ge(gu_in[s][k // 2], p * 16 + 16)
                            for a in range(2):
                                for h in range(NH):
                                    last = pe.matmul(banks[4 + a][h * BM:(h + 1) * BM, :], xT[:, k % 4, k // 4, :],
                                                     gate_up[s][:, k, a * FF + h * HW:a * FF + (h + 1) * HW],
                                                     start=(k == 0), stop=(k == KC - 1), skip_group_check=True)
                            if k % 2:
                                last.then_inc(ev("gu_used"), 1)
                            if k == 0:
                                for a in range(2):
                                    for h in range(NH):
                                        rows = slice((2 * h + a) * QR, (2 * h + a + 1) * QR)
                                        pe.matmul(banks[4 + a][h * BM:(h + 1) * BM, :], onehot[rows, :],
                                                  exp_bias[rows, :], start=False, stop=False, skip_group_check=True)
                        pe.wait_ge(ev("y_ready"), g + 1)
                        combine()
                        pe.wait_ge(ev("sel_ready"), g + 2)
                        gather()
                        pe.wait_ge(ev("hid_ready"), g + 1)
                        for i in range(4):
                            last = pe.transpose(banks[7][:, i * P:(i + 1) * P], hid[:, i * P:(i + 1) * P], ident[:, :])
                        last.then_inc(ev("ht_done"), 1)
                        pe.wait_ge(ev("xe_ready"), g + 2)
                        gather_T()
                        pe.wait_ge(ev("selg_ready"), g + 1)
                        for t in range(TILES):
                            last = pe.transpose(banks[4][:, t * P:(t + 1) * P], selg[:, t, :], ident[:, :])
                        last.then_inc(ev("gt_done"), 1)
                        pe.wait_ge(ev("hidT_ready"), g + 1)
                        for k in range(KC):
                            if k % 2 == 0:
                                pe.wait_ge(dn_in[k // 2], p * 32 + (16 * s + 16))
                            for h in range(NH):
                                last = pe.matmul(banks[7][h * BM:(h + 1) * BM, :], hidT[:, k % 4, k // 4, :],
                                                 down[:, k, h * HW:(h + 1) * HW],
                                                 start=(k == 0), stop=(k == KC - 1), skip_group_check=True)
                            if k % 2:
                                last.then_inc(ev("down_used"), 1)
            total = pe.value_load(table[0:1, GMAX + 3 * E:GMAX + 3 * E + 1], min_val=1, max_val=GMAX - 1)
            pe.wait_ge(ev("y_ready"), total + 1)
            pe.wait_ge(ev("gT_ready"), total + 1)
            combine()


_INS = ["x", "c", "positions", "w_ada", "b_ada", "g_norm1", "w_in", "b_in", "ln_v_g", "ln_v_b", "w_spatial",
        "b_spatial", "sinks", "w_o_a", "w_o_b", "w_out", "g_norm2", "w_router", "b_router", "w_gate_up",
        "b_gate_up", "w_down", "b_down", "g_final"]


def kernel(**inputs):
    import numpy as _np
    import concourse.bacc as _bacc
    from concourse import mybir as _mybir
    from concourse.bass_utils import run_bass_kernel_spmd as _run

    nc = _bacc.Bacc("TRN2", target_bir_lowering=False, num_devices=1)
    arrays, args = {}, []
    for name in _INS:
        a = _np.ascontiguousarray(inputs[name])
        arrays[f"in_{name}_dram"] = a
        args.append(nc.dram_tensor(f"in_{name}_dram", a.shape, _mybir.dt.from_np(a.dtype), kind="ExternalInput").ap())
    args.append(nc.dram_tensor("out_dram", (1, S, D), F32, kind="ExternalOutput").ap())
    bass_hybrid_layer(nc, *args)
    r = _run(nc, [arrays], core_ids=[0])
    return r.results[0]["out_dram"]
```

```python
from contextlib import ExitStack
import math

import numpy as np
import concourse.bass as bass
from concourse import mybir

F32 = mybir.dt.float32
F32R = mybir.dt.float32r
I32 = mybir.dt.int32
BF16 = mybir.dt.bfloat16
ALU = mybir.AluOpType
ACT = mybir.ActivationFunctionType
AX = mybir.AxisListType

P = 128
D = 1024
S = 256
TILES = S // P
KC = D // P
COLS = 512
H = 8
CH = 64
NCH = S // CH
NQ = 16
NKV = 2
HALF = 8
THETA = 500000.0
IN_W = 5376
E = 32
TOPK = 4
FF = 1024
ALPHA = 1.702
LIMIT = 7.0
EPS = 1e-5
BM = 64
NH = P // BM
HW = D // NH
QR = 32
NQT = P // QR
GMAX = 48
BIG = 12582912.0

EVENTS = ("acc_init", "ada_added", "ada_made", "angle_ready", "bias_part_ready", "bias_rest_ready",
          "c_act_ready", "cmp_ready", "comb_done", "consts", "counters", "counts_ready", "crep_ready",
          "down_used", "ex_ready", "exp_done", "g_ready", "gained", "gates_ready", "gt_done", "gT_ready",
          "gu_used", "h2_ready", "heads_ready", "hid_ready", "hidT_ready", "hot_ready", "ht_done", "hT_parts",
          "mask_ready", "merged_ready", "mod_col_ready", "modT_done", "mT_parts", "negm_ready", "negtop_ready",
          "next_ready", "now_ready", "out_ready", "p_norm", "part_out", "pool_steps", "prod_ready",
          "rope_ready", "rows_made", "s_done", "sel_ready", "selg_ready", "sig_done", "sig_ready",
          "slot_gate_ready", "slots_ready", "ssq_ready", "std_ready", "table_ready", "trig_ready", "u_gelu",
          "u_ready", "v_gelu", "var_ready", "vec_steps", "vn_ready", "vp_ready", "w_lower_dve", "w_lower_pool",
          "w_upper_ready", "ws_masked", "x2_ready", "xe_ready", "xg_done", "xn_ready", "xt_done", "xT_ready",
          "y2_ready", "y_out", "y_ready", "yaT_parts", "ybT_parts")


def bass_hybrid_layer(nc, x, c, positions, w_ada, b_ada, g_norm1, w_in, b_in, ln_v_g, ln_v_b,
                      w_spatial, b_spatial, sinks, w_o_a, w_o_b, w_out, g_norm2, w_router,
                      b_router, w_gate_up, b_gate_up, w_down, b_down, g_final, out):
    RING = 3
    dense = []
    OFF_V, OFF_Q, OFF_K, OFF_GA, OFF_GB = 1024, 2048, 3072, 3328, 4352
    for name, off, w in [("v0", OFF_V, 512), ("v1", OFF_V + 512, 512), ("u0", 0, 512), ("u1", 512, 512),
                         ("q0", OFF_Q, 512), ("q1", OFF_Q + 512, 512), ("kv", OFF_K, 256),
                         ("ga0", OFF_GA, 512), ("ga1", OFF_GA + 512, 512),
                         ("gb0", OFF_GB, 512), ("gb1", OFF_GB + 512, 512)]:
        dense.append((name, w_in[0, :, off:off + w], b_in[0:1, off:off + w]))
    for name, w in [("oa", w_o_a), ("ob", w_o_b), ("out", w_out)]:
        for j in range(2):
            dense.append((f"{name}{j}", w[0, :, j * COLS:(j + 1) * COLS], None))
    names = [n for n, _, _ in dense]

    def ring_slot(name):
        if name.startswith("ada"):
            j = int(name[3:])
            s, nth = (j - 1, 1) if 1 <= j <= RING else (RING, max(1, j - 2))
        else:
            i = names.index(name)
            s, nth = i % RING, i // RING + 2
        return s, 16 * nth

    z_order = [f"xT{t}{h}" for t in range(TILES) for h in range(2)]
    z_order += ["v0t0", "v0t1", "v1t0", "am4", "v1t1", "u0t0", "am5", "u0t1", "u1t0", "am6", "u1t1"]
    z_order += [f"f{t}{h}" for t in range(TILES) for h in range(2)]
    z_order += ["am7", "q0t0", "q0t1", "q1t0", "am8", "q1t1", "kvt0", "am9", "kvt1", "ga0t0", "am10", "ga0t1"]
    z_order += ["ga1t0", "part11", "ga1t1", "am11"]
    for n in ["gb0", "gb1", "oa0", "oa1", "ob0", "ob1"]:
        z_order += [f"{n}t{t}" for t in range(TILES)]
    z_order += [f"bc{s}{h}" for s in (2, 3, 4, 5) for h in range(2)]
    z_order += [f"out{j}t{t}" for t in range(TILES) for j in range(2)]
    z_order += ["logit_parts", "logits", "rank", "starts", "etab"]
    t_order = ["ws0", "ws1"]
    t_order += [f"ya{t}{h}" for t in range(TILES) for h in range(2)]
    t_order += [f"q{t}{h}" for t in range(TILES) for h in range(2)] + ["k"]
    for n in range(NCH):
        t_order += [f"p{n}0", f"p{n}1", f"o{n}"]
    t_order += [f"m{t}{h}" for t in range(TILES) for h in range(2)]
    t_order += [f"h{t}{h}" for t in range(TILES) for h in range(2)] + ["gT"]

    ctx = ExitStack()
    with ctx:
        ctx.enter_context(nc.allow_non_contiguous_dma(reason="small columns"))

        def sb(name, shape, dt=F32):
            return ctx.enter_context(nc.sbuf_tensor(name, shape, dt))

        def sem(name):
            return ctx.enter_context(nc.semaphore(name))

        with ExitStack() as same_room:
            gate_up_r = [same_room.enter_context(nc.sbuf_tensor(f"gate_up_r{s}", [P, KC, 2 * FF], F32R)) for s in range(2)]
            down_r = same_room.enter_context(nc.sbuf_tensor("down_r", [P, KC, D], F32R))
            front_r = same_room.enter_context(nc.sbuf_tensor("front_r", [P, 4 * D], F32R))
            mod_r = same_room.enter_context(nc.sbuf_tensor("mod_r", [P, 12, P], F32R))
        gate_up = [sb(f"gate_up{s}", [P, KC, 2 * FF]) for s in range(2)]
        down = sb("down", [P, KC, D])
        front = sb("front", [P, 4 * D])
        mod = sb("mod", [P, 12, P])

        def columns(buf):
            return buf.rearrange("p a (b n) -> p (a b) n", n=COLS)
        ring = [columns(gate_up[1][:, 2 * i:2 * i + 2, :]) for i in range(RING)] + [columns(gate_up[0][:, 6:8, :])]
        w_upper = [columns(gate_up_r[0][:, 2 * i:2 * i + 2, :]) for i in range(2)]
        w_lower = [columns(gate_up_r[1][:, 2 * i:2 * i + 2, :]) for i in range(RING)]
        upper_a, upper_b = (gate_up_r[0][:, k, :].rearrange("p (b n) -> p b n", n=S) for k in (4, 5))
        hT_lower, yaT_lower, ybT_lower = (down_r[:, k:k + 2, :].rearrange("p a (b n) -> p (a b) n", n=S) for k in (0, 2, 6))
        spare = gate_up[1][:, 6:8, :].rearrange("p a b -> p (a b)")
        hT = down[:, 0:2, :].rearrange("p a (b n) -> p (a b) n", n=S)
        v_buf = down[:, 2:4, :]
        u_buf = down[:, 4:6, :]
        q_buf = down[:, 6:8, :]

        def as_T(buf):
            return buf.rearrange("p a (b n) -> p (a b) n", n=S)

        ws = spare[:, 0:1024].rearrange("p (h n) -> p h n", h=H)
        probs = spare[:, 0:1024].rearrange("p (r g n) -> p r g n", r=2, g=4)
        wsT = spare[:, 1024:2048].rearrange("p (h n) -> p h n", h=H)
        probsT = spare[:, 2048:3072].rearrange("p (r g n) -> p r g n", r=2, g=4)
        row_sel = spare[:, 3072:3584].rearrange("p (q n) -> p q n", q=NQT)
        tri = spare[:, 3584:3712]
        ones = spare[:, 3712:3840]
        wr = spare[:, 3840:4096].rearrange("p (k e) -> p k e", k=KC)

        x_sb = sb("x_sb", [P, TILES, D])
        h2 = sb("h2", [P, TILES, D])
        ln_gb = h2
        gt2 = sb("gt2", [P, D])
        bias_ring = gt2[:, :].rearrange("p (s n) -> p s n", s=2)
        sig_a = front[:, 0:2048].rearrange("p (t n) -> p t n", t=TILES)
        sig_b = front[:, 2048:4096].rearrange("p (t n) -> p t n", t=TILES)
        gt1 = front[:, 0:1024]
        mul2 = front[:, 1024:2048]
        sh2 = front[:, 2048:3072]
        g2bc = h2[:, 1, :]
        exp_bias = sb("exp_bias", [P, HW])
        kv = exp_bias[:, :].rearrange("p (t n) -> p t n", t=TILES)
        kT = h2[:, 0, 0:512].rearrange("p (g n) -> p g n", g=NKV)
        kd = h2[:, 0, 512:1024].rearrange("p (t g u d) -> p t g u d", t=TILES, g=NKV, u=2)
        vp = spare[:, 1920:2048]
        rope_room = spare[:, 1024:1536]
        b_down_sb = mod[0:E, 0:8, :].rearrange("p a b -> p (a b)")
        xT = mod[:, 0:4, :].rearrange("p i (h n) -> p i h n", h=NH)
        hidT = mod[:, 4:8, :].rearrange("p i (h n) -> p i h n", h=NH)
        y_sb = mod[:, 8:12, :].rearrange("p a b -> p (a b)")
        y_lower = mod_r[:, 8:12, :].rearrange("p a b -> p (a b)")
        crep = sb("crep", [P, KC, QR])
        ident = sb("ident", [P, P])
        quarter_ident = sb("quarter_ident", [P, QR])
        quarter_head = sb("quarter_head", [P, QR])

        def part(j):
            room = spare[:, 2048:3072] if j < 8 else h2[:, 1, :]
            return room[:, (j % 2) * COLS:(j % 2 + 1) * COLS]

        at = [0]

        def cut(n):
            at[0] += n
            return front[:, at[0] - n:at[0]]

        def by_tile(ap):
            return ap.rearrange("p (t n) -> p t n", t=TILES)
        iota_h = cut(P).rearrange("p (h j) -> p h j", h=NH)
        iota_g = cut(GMAX)
        slot_base = cut(GMAX)
        block_hot = cut(GMAX)
        slots_gates = cut(4 * E).rearrange("p (e n) -> p e n", n=4)
        tri_inc = cut(P)[0:E, :]
        tri_exc = cut(P)[0:E, :]
        sel = by_tile(cut(TILES * BM))
        selg = by_tile(cut(TILES * P))
        onehot = cut(BM // 2).bitcast(BF16)
        xe = cut(HW)
        slot_gate = cut(1)
        gT = front_r[:, at[0]:at[0] + TILES * P]
        cut(TILES * P)
        slot_next, slot_now = cut(TILES), cut(TILES)
        router_at = at[0]
        g_cap = cut(HW)
        y_upper = front_r[:, at[0]:at[0] + HW]
        g_sig, hid = cut(HW), cut(HW)
        bias_parts = [exp_bias[:, :].bitcast(BF16), cut(HW).bitcast(BF16)]
        bias_rest = spare[:, 0:2048]
        assert at[0] <= 4 * D
        at[0] = router_at
        lg, lrep, mask, ex, gates, dtmp = (by_tile(cut(TILES * E)) for _ in range(6))
        top8 = by_tile(cut(TILES * 8))
        negtop, esum = cut(TILES), cut(TILES)
        nbB, stB, enB = cut(E), cut(E), cut(E)
        nbT = cut(P)[0:E, :]
        gatesT = by_tile(cut(TILES * P))[0:E]
        block_e, cmp = cut(GMAX), cut(GMAX)
        logit_parts = cut(S)
        ncol = cut(4)
        assert at[0] <= 4 * D
        table = sb("table", [1, 2 * GMAX + 3 * E + 4], I32)
        DOWN_AT = GMAX + 3 * E + 1

        sm = sb("sm", [P, 320])
        cat = [0]

        def col(n):
            cat[0] += n
            assert cat[0] <= 320
            return sm[:, cat[0] - n:cat[0]]
        c_col, c_act = col(KC), col(KC)
        g1_col = col(KC)
        mod_col = col(2 * KC).rearrange("p (s k) -> p s k", s=2)
        mul1 = col(KC)
        ssq, var, rstd, nt = col(TILES), col(TILES), col(TILES), col(TILES)
        stats = col(TILES * 12).rearrange("p (t n s) -> p t n s", t=TILES, n=2)
        mv = col(TILES * 2).rearrange("p (t s) -> p t s", t=TILES)
        bs = col(H)
        pos_f = col(TILES)
        invf = col(HALF)
        ang = col(TILES * HALF).rearrange("p (t f) -> p t f", t=TILES)
        kf = col(TILES * HALF).rearrange("p (t f) -> p t f", t=TILES)
        cos = col(TILES * HALF).rearrange("p (t f) -> p t f", t=TILES)
        sin = col(TILES * HALF).rearrange("p (t f) -> p t f", t=TILES)
        sk = col(8).rearrange("p (r g) -> p r g", r=2)
        mx = col(8).rearrange("p (r g) -> p r g", r=2)
        negm = col(8).rearrange("p (r g) -> p r g", r=2)
        den = col(8).rearrange("p (r g) -> p r g", r=2)
        es = col(8).rearrange("p (r g) -> p r g", r=2)
        br = col(E)
        pos_i = sb("pos_i", [P, TILES], I32)
        banks = [ctx.enter_context(nc.psum_tensor(f"bank{i}", [P, COLS], F32)) for i in range(8)]
        NZ = 4

        x_in, cond_in, gmlp_in, attn_in, route_in = (sem(n) for n in ("x_in", "cond_in", "gmlp_in", "attn_in", "route_in"))
        c_in, b_ada_in, ln_in, g2_in, gf_in, bd_in, stored = (sem(n) for n in ("c_in", "b_ada_in", "ln_in", "g2_in", "gf_in", "bd_in", "stored"))
        exp_bias_in = sem("exp_bias_in")
        ring_in = [sem(f"ring_in{i}") for i in range(RING + 1)]
        bias_in = [sem(f"bias_in{i}") for i in range(2)]
        z_full = [sem(f"z_full{i}") for i in range(NZ)]
        z_free = [sem(f"z_free{i}") for i in range(NZ)]
        t_full = [sem(f"t_full{i}") for i in range(2)]
        t_free = [sem(f"t_free{i}") for i in range(2)]
        gu_in = [[sem(f"gu_in{s}_{i}") for i in range(4)] for s in range(2)]
        dn_in = [sem(f"dn_in{i}") for i in range(4)]
        evs = {}

        def ev(name):
            if name not in evs:
                evs[name] = sem(name)
            return evs[name]

        def z_use(name):
            k = z_order.index(name)
            return k % NZ, k // NZ + 1

        def t_use(name):
            k = t_order.index(name)
            return k % 2, k // 2 + 1

        def z_wait(eng, name):
            b, n = z_use(name)
            eng.wait_ge(z_full[b], n)
            return banks[b]

        def t_wait(eng, name):
            b, n = t_use(name)
            eng.wait_ge(t_full[b], n)
            return banks[6 + b]

        def z_gone(eng, name):
            b, n = z_use(name)
            eng.wait_ge(z_free[b], n)

        def t_gone(eng, name):
            b, n = t_use(name)
            eng.wait_ge(t_free[b], n)

        def item_used(eng, name):
            if name == "ada11":
                z_wait(eng, "part11")
            elif name.startswith("ada"):
                eng.wait_ge(ev("ada_made"), int(name[3:]) + 1)
            else:
                z_wait(eng, name + "t1")

        def z_done(ins, name):
            ins.then_inc(z_free[z_use(name)[0]], 1)

        def t_done(ins, name):
            ins.then_inc(t_free[t_use(name)[0]], 1)

        def lower(eng, i, chunks):
            cols = dense[i][1].shape[1]
            return eng.tensor_tensor(w_lower[i % RING][:, chunks, 0:cols], ring[i % RING][:, chunks, 0:cols],
                                     w_upper[i % 2][:, chunks, 0:cols], ALU.subtract)

        for n in EVENTS:
            ev(n)
        block = ctx.enter_context(nc.Block())

        yaT, ybT, mT, h2T = as_T(v_buf), as_T(q_buf), hT, hT
        qT = u_buf.rearrange("p a (c k q) -> p (a c) k q", c=2, q=CH)
        merged = u_buf

        w_gu_view = w_gate_up[0].rearrange("e (k p) n -> p e k n", p=P)
        w_dn_view = w_down[0].rearrange("e (k p) n -> p e k n", p=P)

        def last_pieces(eng, at):
            return eng.value_load(table[0:1, at], min_val=1, max_val=4 * GMAX)

        def pieces_used(eng, used, pieces, i):
            eng.wait_ge(ev(used), pieces + i)

        def load_gate_up(eng, e, s, pieces):
            for i in range(4):
                pieces_used(eng, "gu_used", pieces, i)
                eng.dma_start(gate_up[s][:, 2 * i:2 * i + 2, :],
                              w_gu_view[:, bass.ds(e, 1), 2 * i:2 * i + 2, :].rearrange("p a k n -> p (a k) n"))\
                   .then_inc(gu_in[s][i], 16)

        def load_down(eng, e, pieces):
            for i in range(4):
                pieces_used(eng, "down_used", pieces, 4 + i)
                eng.dma_start(down[:, 2 * i:2 * i + 2, :],
                              w_dn_view[:, bass.ds(e, 1), 2 * i:2 * i + 2, :].rearrange("p a k n -> p (a k) n"))\
                   .then_inc(dn_in[i], 16)

        b_ada_rows = b_ada[0].rearrange("(j q n) -> q j n", j=12, q=NQT)

        def load_b_ada(eng, j0, j1, sem):
            for q in range(NQT):
                eng.dma_start(mod[q * QR:(q + 1) * QR, j0:j1, :],
                              b_ada_rows[q:q + 1, j0:j1, :].to_broadcast([QR, j1 - j0, P])).then_inc(sem, 16)

        @block.sync
        def _(sp):
            sp.dma_start(c_col, c[0].rearrange("(k p) -> p k", p=P)).then_inc(c_in, 16)
            sp.dma_start(x_sb[:, :, :], x[0].rearrange("(t p) d -> p t d", p=P)).then_inc(x_in, 16)
            sp.wait_ge(cond_in, 80)

            def load(name, w, used=None):
                if used:
                    item_used(sp, used)
                slot = ring_slot(name)[0]
                sp.dma_start(ring[slot][:, :, 0:w.shape[1]],
                             w.rearrange("(k p) n -> p k n", p=P)).then_inc(ring_in[slot], 16)

            def load_ada(j, used=None):
                load(f"ada{j}", w_ada[0, :, j * COLS:(j + 1) * COLS], used)

            def load_bias(i):
                if dense[i][2] is not None:
                    if i >= 2:
                        z_gone(sp, names[i - 2] + "t1")
                    cols = dense[i][2].shape[1]
                    sp.dma_start(bias_ring[:, i % 2, 0:cols],
                                 dense[i][2].to_broadcast([P, cols])).then_inc(bias_in[i % 2], 16)
            for j in range(4):
                load_ada(j)
            load(*dense[0][:2], "ada1")
            load_bias(0)
            sp.dma_start(ws, w_spatial[0].rearrange("h i j -> i h j")).then_inc(gmlp_in, 16)
            sp.dma_start(bs, b_spatial[0].rearrange("h i -> i h")).then_inc(gmlp_in, 16)
            sp.dma_start(pos_i[:, :], positions[0].rearrange("(t p) -> p t", p=P)).then_inc(attn_in, 16)
            for hh in range(2):
                for r in range(2):
                    sp.dma_start(sk[hh * CH:(hh + 1) * CH, r, :],
                                  sinks[0:1, :].rearrange("a (g m) -> a m g", m=4)[:, 2 * hh + r, :].to_broadcast([CH, 4]))\
                       .then_inc(attn_in, 16)
            sp.dma_start(wr, w_router[0].rearrange("(k p) e -> p k e", p=P)).then_inc(route_in, 16)
            sp.dma_start(br, b_router[0:1, :].to_broadcast([P, E])).then_inc(route_in, 16)
            load_b_ada(sp, 4, 12, b_ada_in)
            load_ada(4, "ada0")
            load(*dense[1][:2], "ada2")
            load_bias(1)
            load(*dense[2][:2], "ada3")
            for i in range(len(dense) - RING):
                if 5 + i < 12:
                    load_ada(5 + i, f"ada{4 + i}")
                load(*dense[i + RING][:2], names[i])
                load_bias(i + 2)
                if names[i] == "ga1":
                    item_used(sp, "ada11")
                    sp.dma_start(gate_up[0][:, 6:8, :], w_gu_view[:, 0, 6:8, :]).then_inc(gu_in[0][3], 16)
            def first_gate_up(e, i):
                sp.dma_start(gate_up[e][:, 2 * i:2 * i + 2, :],
                             w_gu_view[:, e, 2 * i:2 * i + 2, :]).then_inc(gu_in[e][i], 16)

            def first_down(i):
                sp.dma_start(down[:, 2 * i:2 * i + 2, :],
                             w_dn_view[:, 0, 2 * i:2 * i + 2, :]).then_inc(dn_in[i], 16)
            item_used(sp, "ob1")
            first_gate_up(1, ring_slot("ob1")[0])
            first_down(1)
            first_down(3)
            item_used(sp, "out1")
            for i in range(3):
                first_gate_up(0, i)
            sp.wait_ge(ev("h2_ready"), TILES)
            first_down(2)
            z_wait(sp, "logit_parts")
            first_down(0)
            for name in ("out0", "out1"):
                first_gate_up(1, ring_slot(name)[0])
            sp.wait_ge(ev("table_ready"), 1)
            sp.wait_ge(ev("slots_ready"), 1)
            sp.wait_ge(ev("bias_part_ready"), 4)
            first_gate_up(1, 3)

            with sp.Fori(1, E // 2) as p:
                for s in range(2):
                    e = p * 2 + s
                    pieces = last_pieces(sp, bass.ds(p * 2 + (s - 2 + GMAX + 2 * E), 1))
                    load_gate_up(sp, e, s, pieces)
                    load_down(sp, p * 2 + (s - 1), pieces)
            pieces = last_pieces(sp, slice(GMAX + 2 * E + 30, GMAX + 2 * E + 31))
            load_down(sp, E - 1, pieces)
            pieces_used(sp, "gu_used", pieces, 3)
            sp.dma_start(gate_up[0][:, 0, 0:D], g_final.rearrange("(a d) -> a d", a=1).to_broadcast([P, D]))\
              .then_inc(gf_in, 16)
            for t in range(TILES):
                sp.wait_ge(ev("out_ready"), t + 1)
                sp.dma_start(out[0, t * P:(t + 1) * P, :], h2[:, t, :]).then_inc(stored, 16)
            sp.wait_ge(stored, 16 * TILES)

        @block.gpsimd
        def _(pool):
            pool.memset(ident[:, :], 0.0).then_inc(ev("pool_steps"), 1)
            pool.memset(tri, 1.0).then_inc(ev("pool_steps"), 1)
            pool.memset(row_sel, 0.0).then_inc(ev("pool_steps"), 1)
            pool.memset(ones, 1.0).then_inc(ev("pool_steps"), 1)
            for f in range(HALF):
                pool.memset(invf[:, f:f + 1], float(np.float32(THETA ** (-f / HALF)))).then_inc(ev("pool_steps"), 1)
            pool.wait_ge(ev("pool_steps"), 4 + HALF)
            pool.affine_select(out=ident[:, :], in_=ident[:, :], compare_op=ALU.not_equal, fill=1.0, base=0,
                               pattern=[[-1, P]], channel_multiplier=1).then_inc(ev("consts"), 1)
            pool.affine_select(out=tri, in_=tri, compare_op=ALU.is_gt, fill=0.0, base=0,
                               pattern=[[1, P]], channel_multiplier=-1).then_inc(ev("consts"), 1)
            pool.affine_select(out=row_sel, in_=row_sel, compare_op=ALU.not_equal, fill=1.0, base=0,
                               pattern=[[-QR, NQT], [0, P]], channel_multiplier=1).then_inc(ev("consts"), 1)
            pool.wait_ge(gmlp_in, 32)
            pool.memset(ws[0:CH, :, CH:P], 0.0).then_inc(ev("ws_masked"), 1)
            for i in range(len(dense)):
                pool.wait_ge(ev("w_upper_ready"), i + 1)
                lower(pool, i, slice(KC // 2, KC)).then_inc(ev("w_lower_pool"), 1)
            pool.wait_ge(ev("h2_ready"), TILES)
            pool.iota(iota_h, pattern=[[0, NH], [1, BM]], base=0, channel_multiplier=0,
                      allow_small_or_imprecise_dtypes=True).then_inc(ev("counters"), 1)
            pool.iota(iota_g, pattern=[[1, GMAX]], base=0, channel_multiplier=0,
                      allow_small_or_imprecise_dtypes=True).then_inc(ev("counters"), 1)
            pool.iota(slot_base, pattern=[[BM, GMAX]], base=0, channel_multiplier=0,
                      allow_small_or_imprecise_dtypes=True).then_inc(ev("counters"), 1)
            pool.memset(tri_inc, 1.0).then_inc(ev("pool_steps"), 1)
            pool.memset(tri_exc, 1.0).then_inc(ev("pool_steps"), 1)
            pool.wait_ge(ev("pool_steps"), 6 + HALF)
            pool.affine_select(out=tri_inc, in_=tri_inc, compare_op=ALU.is_ge, fill=0.0, base=0,
                               pattern=[[0, NQT], [1, E]], channel_multiplier=-1).then_inc(ev("counters"), 1)
            pool.affine_select(out=tri_exc, in_=tri_exc, compare_op=ALU.is_gt, fill=0.0, base=0,
                               pattern=[[0, NQT], [1, E]], channel_multiplier=-1).then_inc(ev("counters"), 1)
            pool.wait_ge(gf_in, 16)
            for t in range(TILES):
                pool.wait_ge(ev("y2_ready"), t + 1)
                pool.tensor_tensor(gate_up[0][:, 1 + t, 0:D], x_sb[:, t, :], gate_up[0][:, 0, 0:D], ALU.mult)\
                    .then_inc(ev("gained"), 1)

        @block.scalar
        def _(act):
            act.dma_start(g1_col, g_norm1[0].rearrange("(k p) -> p k", p=P)).then_inc(cond_in, 16)
            load_b_ada(act, 0, 4, cond_in)

            def part_copy(j):
                if j < 11:
                    act.wait_ge(ev("ada_made"), j + 1)
                if j in (8, 9):
                    act.wait_ge(ev("vn_ready"), TILES)
                if 2 <= j < 6:
                    act.wait_ge(ev("rows_made"), j - 1)
                elif j >= 6:
                    z_wait(act, f"am{j - 2}")
                bank = banks[4 + j % 2] if j < 11 else z_wait(act, "part11")
                last = act.activation(part(j), bank[:, :], ACT.Copy)
                if j < 11:
                    last.then_inc(ev("part_out"), 1)
                else:
                    z_done(last, "part11")

            act.wait_ge(c_in, 16)
            act.activation(c_act, c_col, ACT.Silu).then_inc(ev("c_act_ready"), 1)
            act.wait_ge(x_in, 16)
            for t in range(TILES):
                act.activation(q_buf[:, t, :], x_sb[:, t, :], ACT.Square, accum_out=ssq[:, t:t + 1])\
                   .then_inc(ev("ssq_ready"), 1)
            act.wait_ge(ev("var_ready"), 1)
            act.activation(rstd, var, ACT.Sqrt).then_inc(ev("std_ready"), 1)
            for j in range(4):
                part_copy(j)
            act.wait_ge(ev("mod_col_ready"), 2)
            for h in range(2):
                name = f"xT1{h}"
                bank = z_wait(act, name)
                for i in range(4):
                    k = 4 * h + i
                    last = act.activation(hT[:, k, P:2 * P], bank[:, i * P:(i + 1) * P], ACT.Identity,
                                          bias=mod_col[:, 0, k:k + 1], scale=mul1[:, k:k + 1])
                z_done(last, name)
            for t in range(TILES):
                z_wait(act, f"xT{t}1")
            act.dma_start(ln_gb[:, 0, :], ln_v_g[0:1, :].to_broadcast([P, D])).then_inc(ln_in, 16)
            act.dma_start(ln_gb[:, 1, :], ln_v_b[0:1, :].to_broadcast([P, D])).then_inc(ln_in, 16)
            for j in range(2):
                for t in range(TILES):
                    z_gone(act, f"v{j}t{t}")
                    act.activation(v_buf[:, t, j * COLS:(j + 1) * COLS], v_buf[:, t, j * COLS:(j + 1) * COLS],
                                   ACT.Gelu).then_inc(ev("v_gelu"), 1)
                part_copy(4 + j)
                if j == 0:
                    for h in range(2):
                        bank = t_wait(act, f"ws{h}")
                        t_done(act.activation(wsT[:, 4 * h:4 * h + 4, :].rearrange("p h n -> p (h n)"), bank[:, :], ACT.Copy),
                               f"ws{h}")
            act.wait_ge(ev("var_ready"), 2)
            act.activation(rstd, var, ACT.Sqrt).then_inc(ev("std_ready"), 1)
            for j in range(2):
                for t in range(TILES):
                    z_gone(act, f"u{j}t{t}")
                    act.activation(u_buf[:, t, j * COLS:(j + 1) * COLS], u_buf[:, t, j * COLS:(j + 1) * COLS],
                                   ACT.Gelu).then_inc(ev("u_gelu"), 1)
                part_copy(6 + j)
            act.wait_ge(ev("angle_ready"), 1)
            act.activation(sin, ang, ACT.Sin).then_inc(ev("trig_ready"), 1)
            act.activation(cos, ang, ACT.Sin, scale=0.5).then_inc(ev("trig_ready"), 1)

            def copy_T(dst, kind):
                for t in range(TILES):
                    for h in range(2):
                        name = f"{kind}{t}{h}"
                        bank = t_wait(act, name)
                        t_done(act.activation(dst[:, 4 * h:4 * h + 4, t * P:(t + 1) * P],
                                              bank[:, :].rearrange("p (k n) -> p k n", k=4), ACT.Copy), name)
            copy_T(yaT, "ya")
            for j in range(8, 11):
                part_copy(j)
            for t in range(TILES):
                for h in range(2):
                    name = f"q{t}{h}"
                    bank = t_wait(act, name)
                    t_done(act.activation(qT[:, 2 * t:2 * t + 2, 4 * h:4 * h + 4, :],
                                          bank[:, :].rearrange("p (k c q) -> p c k q", k=4, c=2), ACT.Copy), name)
            bank = t_wait(act, "k")
            t_done(act.activation(kT, bank[:, :].rearrange("p (g n) -> p g n", g=NKV), ACT.Copy), "k")
            for n in range(NCH):
                keys = CH if n == 0 else P
                act.wait_ge(ev("negm_ready"), n + 1)
                for r in range(2):
                    for g in range(4):
                        act.activation(probs[:, r, g, 0:keys], banks[4 + r][:, g * P:g * P + keys], ACT.Exp,
                                       bias=negm[:, r, g:g + 1], scale=1.0 / math.sqrt(CH),
                                       accum_out=den[:, r, g:g + 1]).then_inc(ev("exp_done"), 1)
                act.activation(es, es, ACT.Exp).then_inc(ev("exp_done"), 1)
                if n == 0:
                    part_copy(11)
                if n:
                    t_wait(act, f"o{n - 1}")
                for r in range(2):
                    name = f"p{n}{r}"
                    bank = t_wait(act, name)
                    t_done(act.activation(probsT[0:keys, r, :, :].rearrange("p g n -> p (g n)"), bank[0:keys, :],
                                          ACT.Copy), name)
            z_wait(act, "am11")
            act.dma_start(g2bc, g_norm2[0:1, :].to_broadcast([P, D])).then_inc(g2_in, 16)
            for sig, kind in ((sig_a, "ga"), (sig_b, "gb")):
                for t in range(TILES):
                    for j in range(2):
                        z_gone(act, f"{kind}{j}t{t}")
                    act.activation(sig[:, t, :], sig[:, t, :], ACT.Sigmoid).then_inc(ev("sig_done"), 1)
            z_gone(act, "kvt1")
            for n in range(NCH):
                t_gone(act, f"o{n}")
            for q in range(NQT):
                act.dma_start(bias_rest[q * QR:(q + 1) * QR, :], b_gate_up[0]).then_inc(exp_bias_in, 16)
            copy_T(mT, "m")
            for name, dst in (("bc2", gt1), ("bc3", sh2)):
                for h in range(2):
                    bank = z_wait(act, f"{name}{h}")
                    z_done(act.activation(dst[:, h * COLS:(h + 1) * COLS], bank[:, :], ACT.Copy), f"{name}{h}")
            for h in range(2):
                bank = z_wait(act, f"bc5{h}")
                z_done(act.activation(gt2[:, h * COLS:(h + 1) * COLS], bank[:, :], ACT.Copy), f"bc5{h}")
            z_wait(act, "bc51")
            act.dma_start(b_down_sb, b_down[0]).then_inc(bd_in, 16)

            def bias_part(rows):
                for a in range(2):
                    last = act.activation(bias_parts[a][rows, :], bias_rest[rows, a * FF:(a + 1) * FF], ACT.Copy)
                last.then_inc(ev("bias_part_ready"), 1)
            act.wait_ge(exp_bias_in, 64)
            bias_part(slice(0, P))

            def row_norms(ready, first):
                for t in range(TILES):
                    act.wait_ge(ev(ready), t + 1)
                    act.activation(h2[:, t, :], x_sb[:, t, :], ACT.Square, accum_out=ssq[:, t:t + 1])\
                       .then_inc(ev("ssq_ready"), 1)
                    act.wait_ge(ev("var_ready"), first + t)
                    act.activation(rstd[:, t:t + 1], var[:, t:t + 1], ACT.Sqrt).then_inc(ev("std_ready"), 1)
            row_norms("x2_ready", 3)
            copy_T(h2T, "h")
            bank = z_wait(act, "logit_parts")
            z_done(act.activation(logit_parts, bank[:, 0:S], ACT.Copy), "logit_parts")
            act.wait_ge(ev("negtop_ready"), 1)
            for t in range(TILES):
                act.activation(ex[:, t, :], lg[:, t, :], ACT.Exp, bias=negtop[:, t:t + 1]).then_inc(ev("ex_ready"), 1)
            bank = t_wait(act, "gT")
            t_done(act.activation(gatesT.rearrange("p t n -> p (t n)"), bank[0:E, 0:TILES * P], ACT.Copy), "gT")

            act.wait_ge(ev("bias_rest_ready"), 1)
            bias_part(slice(QR, 2 * QR))
            bias_part(slice(2 * QR, P))
            act.wait_ge(ev("bias_rest_ready"), 2)
            bias_part(slice(2 * QR, P))

            act.wait_ge(ev("xt_done"), 1)
            act.activation(xT.rearrange("p i h n -> p (i h n)"), banks[6][:, :], ACT.Copy)\
               .then_inc(ev("xT_ready"), 1)
            act.wait_ge(ev("table_ready"), 1)
            total = act.value_load(table[0:1, GMAX + 3 * E:GMAX + 3 * E + 1], min_val=1, max_val=GMAX - 1)

            def result_out(g, hidden):
                act.wait_ge(ev("down_used"), g * 4 + 4)
                act.wait_ge(ev("gT_ready"), g + 1)
                act.activation(y_sb, banks[7][:, :], ACT.Copy, scale=slot_gate).then_inc(ev("y_out"), 1)
                act.wait_ge(ev("hid_ready"), hidden)
                act.activation(y_upper, banks[7][:, :], ACT.Copy, scale=slot_gate).then_inc(ev("y_out"), 1)

            with act.Fori(0, total) as g:
                act.wait_ge(ev("g_ready"), g + 1)
                act.activation(g_sig, g_cap, ACT.Sigmoid, scale=ALPHA).then_inc(ev("sig_ready"), 1)
                result_out(g, g + 1)
                act.wait_ge(ev("ht_done"), g + 1)
                act.activation(hidT.rearrange("p i h n -> p (i h n)"), banks[7][:, :], ACT.Copy)\
                   .then_inc(ev("hidT_ready"), 1)
                act.wait_ge(ev("xt_done"), g + 2)
                act.activation(xT.rearrange("p i h n -> p (i h n)"), banks[6][:, :], ACT.Copy)\
                   .then_inc(ev("xT_ready"), 1)
            result_out(total, total)

            row_norms("y2_ready", 5)

        @block.vector
        def _(dve):
            steps = [0]

            def link(ins):
                steps[0] += 1
                ins.then_inc(ev("vec_steps"), 1)
                dve.wait_ge(ev("vec_steps"), steps[0])

            def upper(dst, src):
                return dve.tensor_copy(dst, src)

            def w_parts_upper(i):
                s, n = ring_slot(names[i])
                dve.wait_ge(ring_in[s], n)
                if i >= 2:
                    z_wait(dve, names[i - 2] + "t1")
                cols = dense[i][1].shape[1]
                upper(w_upper[i % 2][:, :, 0:cols], ring[s][:, :, 0:cols]).then_inc(ev("w_upper_ready"), 1)

            def w_parts_lower(i):
                dve.wait_ge(ev("w_upper_ready"), i + 1)
                lower(dve, i, slice(0, KC // 2)).then_inc(ev("w_lower_dve"), 1)

            def w_parts(name):
                i = names.index(name) + 2
                if i < len(dense):
                    w_parts_upper(i)
                    w_parts_lower(i)

            def x_parts(buf, up, low, event, cols=slice(0, S)):
                link(upper(up[:, :, cols], buf[:, :, cols]))
                dve.tensor_tensor(low[:, :, cols], buf[:, :, cols], up[:, :, cols], ALU.subtract)\
                   .then_inc(ev(event), 1)

            norms = [0]

            def inverse_std(squares, tile=slice(0, TILES)):
                norms[0] += 1
                v, inv, tmp = var[:, tile], rstd[:, tile], nt[:, tile]
                if squares:
                    dve.wait_ge(ev("ssq_ready"), squares)
                    dve.tensor_scalar(v, ssq[:, tile], 1.0 / D, EPS, ALU.mult, ALU.add).then_inc(ev("var_ready"), 1)
                else:
                    dve.tensor_scalar(v, mv[:, :, 1], 1.0, EPS, ALU.mult, ALU.add).then_inc(ev("var_ready"), 1)
                dve.wait_ge(ev("std_ready"), norms[0])
                link(dve.reciprocal(inv, inv))
                link(dve.tensor_tensor(tmp, inv, inv, ALU.mult))
                link(dve.tensor_tensor(tmp, tmp, v, ALU.mult))
                link(dve.tensor_scalar(tmp, tmp, -0.5, 1.5, ALU.mult, ALU.add))
                link(dve.tensor_tensor(inv, inv, tmp, ALU.mult))

            link(dve.memset(h2[:, 0, 0:QR], 1.0))
            dve.wait_ge(ev("c_act_ready"), 1)
            for k in range(KC):
                last = dve.tensor_scalar(crep[:, k, :], h2[:, 0, 0:QR], c_act[:, k:k + 1], None, ALU.mult)
            last.then_inc(ev("crep_ready"), 1)
            dve.wait_ge(ev("crep_ready"), 1)
            dve.wait_ge(ev("consts"), 3)
            link(dve.tensor_tensor(quarter_head[:, :], row_sel[:, 0, 0:QR], row_sel[:, 1, 0:QR], ALU.add))
            link(dve.tensor_tensor(quarter_head[:, :], quarter_head[:, :], row_sel[:, 2, 0:QR], ALU.add))
            dve.tensor_tensor(quarter_head[:, :], quarter_head[:, :], row_sel[:, 3, 0:QR], ALU.add)\
               .then_inc(ev("heads_ready"), 1)
            link(dve.tensor_tensor(quarter_ident[:, :], ident[:, 0:QR], ident[:, QR:2 * QR], ALU.add))
            for q in (2, 3):
                link(dve.tensor_tensor(quarter_ident[:, :], quarter_ident[:, :], ident[:, q * QR:(q + 1) * QR], ALU.add))
            inverse_std(2)
            for t in range(TILES):
                dve.tensor_scalar(h2[:, t, :], x_sb[:, t, :], rstd[:, t:t + 1], None, ALU.mult).then_inc(ev("xn_ready"), 1)
            dve.wait_ge(cond_in, 16 * 5)
            dve.wait_ge(ev("rows_made"), 4)
            dve.tensor_tensor(mod[:, 0:4, :].rearrange("p j n -> p (j n)"), mod[:, 0:4, :].rearrange("p j n -> p (j n)"),
                              banks[6][:, :], ALU.add).then_inc(ev("ada_added"), 1)
            dve.wait_ge(ev("modT_done"), 1)
            link(dve.tensor_copy(mod_col.rearrange("p s k -> p (s k)"),
                                 banks[5][:, :].rearrange("p (m n) -> p m n", n=QR)[:, :, 0]))
            dve.scalar_tensor_tensor(mul1, mod_col[:, 1, :], 1.0, g1_col, ALU.add, ALU.mult)\
               .then_inc(ev("mod_col_ready"), 2)
            dve.wait_ge(ev("mod_col_ready"), 2)
            for h in range(2):
                name = f"xT0{h}"
                bank = z_wait(dve, name)
                for i in range(4):
                    k = 4 * h + i
                    last = dve.tensor_scalar(hT[:, k, 0:P], bank[:, i * P:(i + 1) * P], mul1[:, k:k + 1],
                                             mod_col[:, 0, k:k + 1], ALU.mult, ALU.add)
                z_done(last, name)
            for t in range(TILES):
                for h in range(2):
                    z_gone(dve, f"xT{t}{h}")
                x_parts(hT, upper_a, hT_lower, "hT_parts", slice(t * P, (t + 1) * P))
                if t == 0:
                    w_parts_upper(0)
            w_parts_lower(0)
            w_parts_upper(1)
            w_parts_lower(1)

            def add_mod(j):
                bank = z_wait(dve, f"am{j}")
                z_done(dve.tensor_tensor(mod[:, j, :], mod[:, j, :], bank[:, 0:P], ALU.add), f"am{j}")

            def add_bias(item, dst, ada=None):
                n = names.index(item)
                cols = 2 * P if item == "kv" else COLS
                dve.wait_ge(bias_in[n % 2], 16 * (n // 2 + 1))
                for t in range(TILES):
                    name = f"{item}t{t}"
                    bank = z_wait(dve, name)
                    z_done(dve.tensor_tensor(dst(t), bank[:, 0:cols], bias_ring[:, n % 2, 0:cols], ALU.add), name)
                    if t == 0 and ada:
                        add_mod(ada)

            def half(buf, j):
                return lambda t: buf[:, t, j * COLS:(j + 1) * COLS]

            add_bias("v0", half(v_buf, 0))
            w_parts("v0")
            dve.wait_ge(attn_in, 80)
            dve.wait_ge(ev("consts"), 1)
            link(dve.tensor_copy(pos_f, pos_i[:, :]))
            for t in range(TILES):
                last = dve.tensor_scalar(ang[:, t, :], invf, pos_f[:, t:t + 1], None, ALU.mult)
            link(last)
            link(dve.tensor_scalar(kf, ang, 1.0 / (2 * math.pi), BIG, ALU.mult, ALU.add))
            link(dve.tensor_scalar(kf, kf, BIG, None, ALU.subtract))
            c1 = 6.28125
            c2 = float(np.float32(math.floor((2 * math.pi - c1) * 2 ** 20) / 2 ** 20))
            c3 = float(np.float32(2 * math.pi - c1 - c2))
            for part in (c1, c2, c3):
                link(dve.scalar_tensor_tensor(ang, kf, -part, ang, ALU.mult, ALU.add))
            dve.tensor_scalar(ang, ang, -3.1415925, 3.1415925, ALU.max, ALU.min).then_inc(ev("angle_ready"), 1)
            dve.wait_ge(b_ada_in, 16 * NQT)
            add_bias("v1", half(v_buf, 1), 4)
            for t in range(TILES):
                for j in range(2):
                    dve.wait_ge(ev("v_gelu"), 2 * j + t + 1)
                    last = dve.bn_stats(stats[:, t, j, :], v_buf[:, t, j * COLS:(j + 1) * COLS])
            link(last)
            for t in range(TILES):
                last = dve.bn_aggr(mv[:, t, :], stats[:, t, :, :])
            link(last)
            w_parts("v1")
            add_bias("u0", half(u_buf, 0), 5)
            inverse_std(0)
            dve.wait_ge(ln_in, 32)
            for t in range(TILES):
                link(dve.tensor_scalar(v_buf[:, t, :], v_buf[:, t, :], mv[:, t, 0:1], rstd[:, t:t + 1],
                                       ALU.subtract, ALU.mult))
                link(dve.tensor_tensor(v_buf[:, t, :], v_buf[:, t, :], ln_gb[:, 0, :], ALU.mult))
                dve.tensor_tensor(v_buf[:, t, :], v_buf[:, t, :], ln_gb[:, 1, :], ALU.add).then_inc(ev("vn_ready"), 1)
            w_parts("u0")
            add_bias("u1", half(u_buf, 1), 6)
            for t in range(TILES):
                for h in range(2):
                    dve.wait_ge(ev("u_gelu"), 2 * h + t + 1)
                    name = f"f{t}{h}"
                    bank = z_wait(dve, name)
                    for i in range(4):
                        w = slice((4 * h + i) * P, (4 * h + i + 1) * P)
                        last = dve.scalar_tensor_tensor(u_buf[:, t, w], bank[:, i * P:(i + 1) * P],
                                                        bs[:, 4 * h + i:4 * h + i + 1], u_buf[:, t, w], ALU.add, ALU.mult)
                    z_done(last, name)
            add_mod(7)
            w_parts("u1")
            add_bias("q0", half(q_buf, 0))
            w_parts("q0")
            add_bias("q1", half(q_buf, 1), 8)
            w_parts("q1")
            add_bias("kv", lambda t: kv[:, t, :], 9)
            dve.wait_ge(ev("trig_ready"), 2)
            link(dve.tensor_tensor(cos, cos, cos, ALU.mult))
            link(dve.tensor_scalar(cos, cos, -2.0, 1.0, ALU.mult, ALU.add))
            for name in ("q0t1", "q1t1", "kvt1"):
                z_gone(dve, name)
            for t in range(TILES):
                for view, heads in ((q_buf[:, t, :].rearrange("p (h d) -> p h d", d=CH), NQ),
                                    (kv[:, t, 0:P].rearrange("p (h d) -> p h d", d=CH), NKV)):
                    t1, t2 = view[:, :, 0:HALF], view[:, :, HALF:2 * HALF]
                    shape = [P, heads, HALF]
                    co = cos[:, t, :].unsqueeze(1).to_broadcast(shape)
                    si = sin[:, t, :].unsqueeze(1).to_broadcast(shape)
                    a, b, cc, d = (rope_room[:, i * P:i * P + heads * HALF].rearrange("p (h f) -> p h f", f=HALF)
                                   for i in range(4))
                    dve.tensor_tensor(a, t1, co, ALU.mult)
                    dve.tensor_tensor(b, t2, si, ALU.mult)
                    dve.tensor_tensor(cc, t2, co, ALU.mult)
                    link(dve.tensor_tensor(d, t1, si, ALU.mult))
                    dve.tensor_tensor(t1, a, b, ALU.subtract)
                    link(dve.tensor_tensor(t2, cc, d, ALU.add))
                for u in range(2):
                    last = dve.tensor_copy(kd[:, t, :, u, :], kv[:, t, 0:P].rearrange("p (g d) -> p g d", g=NKV))
                last.then_inc(ev("rope_ready"), 1)

            w_parts("kv")
            for t in range(TILES):
                for h in range(2):
                    t_gone(dve, f"ya{t}{h}")
            x_parts(yaT, upper_b, yaT_lower, "yaT_parts")

            def gates_out(n, t):
                item = ("ga0", "ga1", "gb0", "gb1")[n]
                dst = (sig_a, sig_a, sig_b, sig_b)[n][:, t, (n % 2) * COLS:(n % 2 + 1) * COLS]
                m = names.index(item)
                dve.wait_ge(bias_in[m % 2], 16 * (m // 2 + 1))
                name = f"{item}t{t}"
                bank = z_wait(dve, name)
                z_done(dve.tensor_tensor(dst, bank[:, :], bias_ring[:, m % 2, :], ALU.add), name)

            def softmax_max(n):
                keys = CH if n == 0 else P
                dve.wait_ge(ev("s_done"), n + 1)
                for r in range(2):
                    last = dve.tensor_reduce(mx[:, r, :], banks[4 + r][:, :].rearrange("p (g k) -> p g k", g=4)[:, :, 0:keys],
                                             AX.X, ALU.max)
                link(last)
                link(dve.scalar_tensor_tensor(mx, mx, 1.0 / math.sqrt(CH), sk, ALU.mult, ALU.max))
                link(dve.tensor_tensor(es, sk, mx, ALU.subtract))
                dve.tensor_scalar(negm, mx, -1.0, None, ALU.mult).then_inc(ev("negm_ready"), 1)

            def softmax_norm(n):
                keys = CH if n == 0 else P
                dve.wait_ge(ev("exp_done"), 9 * (n + 1))
                link(dve.tensor_tensor(den, den, es, ALU.add))
                link(dve.reciprocal(den, den))
                dve.tensor_tensor(probs[:, :, :, 0:keys].rearrange("p r g k -> p (r g) k"),
                                  probs[:, :, :, 0:keys].rearrange("p r g k -> p (r g) k"),
                                  den.rearrange("p r g -> p (r g)").unsqueeze(2).to_broadcast([P, 8, keys]), ALU.mult)\
                   .then_inc(ev("p_norm"), 1)

            def values(n):
                t = n // 2
                dve.tensor_copy(vp[0:CH, :], kv[0:CH, t, P:2 * P])
                dve.tensor_copy(vp[CH:P, :], kv[CH:P, t - 1, P:2 * P]).then_inc(ev("vp_ready"), 1)

            def attn_out(n):
                name = f"o{n}"
                bank = t_wait(dve, name)
                t_done(dve.tensor_copy(ybT[:, :, n * CH:(n + 1) * CH], bank[:, :].rearrange("p (k q) -> p k q", q=CH)), name)

            values(2)
            order = [(n, t) for n in range(4) for t in range(TILES)]
            gates_out(*order[0])
            add_mod(10)
            gates_out(*order[1])
            softmax_max(0)
            softmax_norm(0)
            w_parts("ga0")
            gates_out(*order[2])
            for n in range(1, NCH):
                softmax_max(n)
                gates_out(*order[2 * n + 1])
                if n == 1:
                    add_mod(11)
                attn_out(n - 1)
                softmax_norm(n)
                w_parts(("ga1", "gb0", "gb1")[n - 1])
                if 2 * n + 2 < 8:
                    gates_out(*order[2 * n + 2])
            attn_out(NCH - 1)
            for n in range(NCH):
                t_gone(dve, f"o{n}")
            x_parts(ybT, upper_a, ybT_lower, "ybT_parts")

            for kind, sig, need in (("oa", sig_a, 2), ("ob", sig_b, 4)):
                dve.wait_ge(ev("sig_done"), need)
                for j in range(2):
                    for t in range(TILES):
                        w = slice(j * COLS, (j + 1) * COLS)
                        name = f"{kind}{j}t{t}"
                        bank = z_wait(dve, name)
                        if kind == "oa":
                            z_done(dve.tensor_tensor(merged[:, t, w], bank[:, :], sig[:, t, w], ALU.mult), name)
                        else:
                            z_done(dve.tensor_tensor(sig[:, t, w], bank[:, :], sig[:, t, w], ALU.mult), name)
                            z_gone(dve, name)
                            z_gone(dve, f"oa{j}t{t}")
                            dve.tensor_tensor(merged[:, t, w], merged[:, t, w], sig[:, t, w], ALU.add)\
                               .then_inc(ev("merged_ready"), 1)
                    w_parts(f"{kind}{j}")
            for t in range(TILES):
                for h in range(2):
                    t_gone(dve, f"m{t}{h}")
                x_parts(mT, upper_b, hT_lower, "mT_parts", slice(t * P, (t + 1) * P))
            dve.wait_ge(g2_in, 16)
            for h in range(2):
                w = slice(h * COLS, (h + 1) * COLS)
                bank = z_wait(dve, f"bc4{h}")
                z_done(dve.scalar_tensor_tensor(mul2[:, w], bank[:, :], 1.0, g2bc[:, w], ALU.add, ALU.mult), f"bc4{h}")
            def bias_less(rows, n):
                dve.wait_ge(ev("bias_part_ready"), n)
                for a in range(2):
                    w = bias_rest[rows, a * FF:(a + 1) * FF]
                    last = dve.tensor_tensor(w, w, bias_parts[a][rows, :], ALU.subtract)
                last.then_inc(ev("bias_rest_ready"), 1)
            bias_less(slice(0, P), 1)
            z_gone(dve, "bc21")
            z_gone(dve, "bc20")
            for h in range(2):
                z_gone(dve, f"bc4{h}")
                z_gone(dve, f"bc3{h}")
            for t in range(TILES):
                for j in range(2):
                    w = slice(j * COLS, (j + 1) * COLS)
                    name = f"out{j}t{t}"
                    bank = z_wait(dve, name)
                    z_done(dve.tensor_tensor(merged[:, t, w], bank[:, :], gt1[:, w], ALU.mult), name)
                    z_gone(dve, name)
                    last = dve.tensor_tensor(x_sb[:, t, w], x_sb[:, t, w], merged[:, t, w], ALU.add)
                last.then_inc(ev("x2_ready"), 1)
                dve.wait_ge(ev("x2_ready"), t + 1)
                link(dve.tensor_tensor(merged[:, t, :], x_sb[:, t, :], mul2, ALU.mult))
                inverse_std(3 + t, slice(t, t + 1))
                dve.scalar_tensor_tensor(h2[:, t, :], merged[:, t, :], rstd[:, t:t + 1], sh2, ALU.mult, ALU.add)\
                   .then_inc(ev("h2_ready"), 1)

            dve.wait_ge(ev("h2_ready"), TILES)
            bank = z_wait(dve, "logits")
            for t in range(TILES):
                last = dve.tensor_tensor(lg[:, t, :], bank[:, t * E:(t + 1) * E], br, ALU.add)
            z_done(last, "logits")
            z_gone(dve, "logits")
            for t in range(TILES):
                last = dve.max(top8[:, t, :], lg[:, t, :])
            link(last)
            dve.tensor_scalar(negtop, top8[:, :, 0], -1.0, None, ALU.mult).then_inc(ev("negtop_ready"), 1)
            link(dve.memset(top8[:, :, TOPK:8], 3.0e38))
            for t in range(TILES):
                link(dve.match_replace(lrep[:, t, :], top8[:, t, :], lg[:, t, :], -3.0e38))
            dve.tensor_tensor(mask, lg, lrep, ALU.not_equal).then_inc(ev("mask_ready"), 1)
            dve.wait_ge(ev("mask_ready"), 1)
            dve.wait_ge(ev("ex_ready"), TILES)
            link(dve.tensor_tensor(ex, ex, mask, ALU.mult))
            link(dve.tensor_reduce(esum, ex, AX.X, ALU.add))
            link(dve.reciprocal(esum, esum))
            for t in range(TILES):
                last = dve.tensor_scalar(gates[:, t, :], ex[:, t, :], esum[:, t:t + 1], None, ALU.mult)
            last.then_inc(ev("gates_ready"), 1)
            dve.wait_ge(ev("gates_ready"), 1)
            for t in range(TILES):
                dve.tensor_copy(slots_gates[:, :, 2 + t], gates[:, t, :])
            bank = z_wait(dve, "rank")

            def blocks_of(dst, counts):
                link(dve.tensor_scalar(dst, counts, BM / 2 - 0.5, 1.0 / BM, ALU.add, ALU.mult))
                link(dve.tensor_scalar(dst, dst, BIG, None, ALU.add))
                return dve.tensor_scalar(dst, dst, BIG, 1.0, ALU.subtract, ALU.max)
            blocks_of(nbT, bank[0:E, 2 * P:3 * P]).then_inc(ev("counts_ready"), 1)
            link(blocks_of(nbB, bank[:, 2 * E:3 * E]))
            dve.tensor_scalar(dtmp.rearrange("p t e -> p (t e)"), bank[:, 0:TILES * E], 1.0, None, ALU.add)\
               .then_inc(z_free[z_use("rank")[0]], 1)
            z_gone(dve, "rank")
            bank = z_wait(dve, "starts")
            dve.tensor_copy(stB, bank[:, 0:E])
            z_done(dve.tensor_copy(ncol, bank[:, 2 * E:2 * E + 4]), "starts")
            z_gone(dve, "starts")
            link(dve.tensor_tensor(enB, stB, nbB, ALU.add))
            dve.wait_ge(ev("counters"), 5)
            dve.tensor_scalar(cmp[0:E, :], iota_g[0:E, :], ncol[0:E, 2:3], None, ALU.is_ge).then_inc(ev("cmp_ready"), 1)
            for t in range(TILES):
                link(dve.scalar_tensor_tensor(dtmp[:, t, :], stB, float(BM), dtmp[:, t, :], ALU.mult, ALU.add))
                link(dve.tensor_tensor(dtmp[:, t, :], dtmp[:, t, :], mask[:, t, :], ALU.mult))
                link(dve.tensor_scalar(slots_gates[:, :, t], dtmp[:, t, :], -1.0, None, ALU.add))
            def choose(g, slots, e):
                return dve.tensor_scalar(slots, slots_gates[:, bass.ds(e, 1), 0:2].rearrange("p a t -> p (a t)"),
                                         slot_base[:, bass.ds(g, 1)], None, ALU.subtract)

            def gather_map(g, slots):
                for t in range(TILES):
                    last = dve.tensor_scalar(sel[:, t, :], iota_h[:, 0, :], slots[:, t:t + 1], None, ALU.is_equal)
                return last

            def bias_map(g):
                return dve.tensor_scalar(onehot[0:3 * QR, :], iota_h[0:3 * QR, 0, :], 0.0,
                                         block_hot[0:3 * QR, bass.ds(g, 1)], ALU.mult, ALU.add)

            choose(0, slot_next, 0).then_inc(ev("next_ready"), 1)
            dve.wait_ge(ev("next_ready"), 1)
            gather_map(0, slot_next).then_inc(ev("sel_ready"), 1)
            link(dve.tensor_scalar(block_hot, iota_g, ncol[:, 0:1], None, ALU.is_ge))
            link(dve.scalar_tensor_tensor(block_hot, iota_g, ncol[:, 2:3], block_hot, ALU.is_lt, ALU.mult))
            dve.memset(onehot[3 * QR:P, :], 0.0)
            bias_map(0).then_inc(ev("hot_ready"), 1)
            dve.tensor_copy(table[0:1, GMAX:GMAX + E], nbB[0:1, :])
            dve.tensor_copy(table[0:1, GMAX + E:GMAX + 2 * E], stB[0:1, :])
            dve.tensor_copy(table[0:1, GMAX + 3 * E:GMAX + 3 * E + 1], enB[0:1, E - 1:E])
            dve.tensor_scalar(table[0:1, GMAX + 2 * E:GMAX + 3 * E], enB[0:1, :], 4.0, -3.0, ALU.mult, ALU.add)\
               .then_inc(ev("slots_ready"), 1)
            dve.wait_ge(ev("slots_ready"), 1)
            bank = z_wait(dve, "etab")
            link(dve.tensor_scalar(block_e, bank[:, 0:GMAX], float(E - 1), None, ALU.min))
            dve.tensor_copy(table[0:1, 0:GMAX], block_e[0:1, :])
            dve.memset(table[0:1, DOWN_AT:DOWN_AT + 1], 16)
            dve.tensor_scalar(table[0:1, DOWN_AT + 1:DOWN_AT + GMAX], block_e[0:1, 0:GMAX - 1], 16.0, 16.0,
                              ALU.mult, ALU.add).then_inc(ev("table_ready"), 1)
            dve.wait_ge(ev("table_ready"), 1)

            dve.memset(slot_gate, 0.0)
            for t in range(TILES):
                last = dve.tensor_scalar(gT[:, t * P:(t + 1) * P].rearrange("p (h j) -> p h j", h=NH), iota_h, 0.0, None,
                                         ALU.is_lt)
            last.then_inc(ev("gT_ready"), 1)

            def result_lower(g):
                dve.wait_ge(ev("y_out"), g * 2 + 2)
                dve.tensor_tensor(y_lower, y_sb, y_upper, ALU.subtract).then_inc(ev("y_ready"), 1)

            bias_less(slice(2 * QR, P), 3)
            dve.wait_ge(ev("xg_done"), 1)
            dve.tensor_copy(xe, banks[6][:, :]).then_inc(ev("xe_ready"), 1)
            dve.wait_ge(ev("acc_init"), 1)
            dve.memset(hidT.rearrange("p i h n -> p (i h n)"), 0.0).then_inc(ev("hidT_ready"), 1)
            total = dve.value_load(table[0:1, GMAX + 3 * E:GMAX + 3 * E + 1], min_val=1, max_val=GMAX - 1)
            with dve.Fori(0, total) as g:
                e_next = dve.value_load(table[0:1, bass.ds(g + 1, 1)], min_val=0, max_val=E - 1)
                e_now = dve.value_load(table[0:1, bass.ds(g, 1)], min_val=0, max_val=E - 1)
                choose(g + 1, slot_next, e_next).then_inc(ev("next_ready"), 1)
                choose(g, slot_now, e_now).then_inc(ev("now_ready"), 1)
                dve.wait_ge(ev("next_ready"), g + 2)
                dve.wait_ge(ev("xg_done"), g + 1)
                gather_map(g + 1, slot_next).then_inc(ev("sel_ready"), 1)
                dve.wait_ge(ev("now_ready"), g + 1)
                dve.wait_ge(ev("gT_ready"), g + 1)
                for t in range(TILES):
                    last = dve.tensor_scalar(selg[:, t, :].rearrange("p (h j) -> p h j", h=NH), iota_h,
                                             slot_now[:, t:t + 1],
                                             slots_gates[:, bass.ds(e_now, 1), 2 + t:3 + t].rearrange("p a t -> p (a t)"),
                                             ALU.is_equal, ALU.mult)
                last.then_inc(ev("selg_ready"), 1)
                dve.wait_ge(ev("gu_used"), g * 4 + 4)
                dve.tensor_scalar(g_cap, banks[4][:, :], LIMIT, None, ALU.min).then_inc(ev("g_ready"), 1)
                dve.tensor_scalar(hid, banks[5][:, :], -LIMIT, LIMIT, ALU.max, ALU.min).then_inc(ev("u_ready"), 1)
                bias_map(g + 1).then_inc(ev("hot_ready"), 1)
                dve.wait_ge(ev("u_ready"), g + 1)
                dve.scalar_tensor_tensor(hid, hid, 1.0, g_cap, ALU.add, ALU.mult).then_inc(ev("prod_ready"), 1)
                dve.wait_ge(ev("prod_ready"), g + 1)
                dve.wait_ge(ev("sig_ready"), g + 1)
                dve.tensor_tensor(hid, hid, g_sig, ALU.mult).then_inc(ev("hid_ready"), 1)
                result_lower(g)
                dve.wait_ge(ev("xg_done"), g + 2)
                dve.tensor_copy(xe, banks[6][:, :]).then_inc(ev("xe_ready"), 1)
                dve.wait_ge(ev("gt_done"), g + 1)
                dve.tensor_reduce(slot_gate, banks[5][:, 0:TILES * P], AX.X, ALU.max).then_inc(ev("slot_gate_ready"), 1)
                dve.wait_ge(ev("slot_gate_ready"), g + 1)
                dve.tensor_scalar(gT, banks[5][:, 0:TILES * P], 0.0, None, ALU.is_gt).then_inc(ev("gT_ready"), 1)
            result_lower(total)

            for t in range(TILES):
                dve.wait_ge(ev("comb_done"), total + (1 + t))
                for h in range(NH):
                    w = slice(h * HW, (h + 1) * HW)
                    last = dve.tensor_tensor(h2[:, t, w], banks[2 * h + t][:, :], gt2[:, w], ALU.mult)
                link(last)
                dve.tensor_tensor(x_sb[:, t, :], x_sb[:, t, :], h2[:, t, :], ALU.add).then_inc(ev("y2_ready"), 1)
            for t in range(TILES):
                inverse_std(5 + t, slice(t, t + 1))
                dve.wait_ge(ev("gained"), t + 1)
                dve.tensor_scalar(h2[:, t, :], gate_up[0][:, 1 + t, 0:D], rstd[:, t:t + 1], None, ALU.mult)\
                   .then_inc(ev("out_ready"), 1)

        @block.tensor
        def _(pe):
            def z_open(name):
                b, n = z_use(name)
                if n > 1:
                    pe.wait_ge(z_free[b], n - 1)
                return banks[b]

            def t_open(name):
                b, n = t_use(name)
                if n > 1:
                    pe.wait_ge(t_free[b], n - 1)
                return banks[6 + b]

            def z_put(ins, name):
                ins.then_inc(z_full[z_use(name)[0]], 1)

            def t_put(ins, name):
                ins.then_inc(t_full[t_use(name)[0]], 1)

            def weights(name):
                s, n = ring_slot(name)
                pe.wait_ge(ring_in[s], n)
                return ring[s]

            def rows_times(item, t, x, cols=COLS):
                i = names.index(item)
                rows, low, up = slice(t * P, (t + 1) * P), *x
                name = f"{item}t{t}"
                bank = z_open(name)
                pe.wait_ge(ev("w_upper_ready"), i + 1)
                for n, (lhsT, w) in enumerate(((up, w_upper[i % 2]), (low, w_upper[i % 2]), (up, w_lower[i % RING]))):
                    if n == 2:
                        pe.wait_ge(ev("w_lower_dve"), i + 1)
                        pe.wait_ge(ev("w_lower_pool"), i + 1)
                    for k in range(KC):
                        last = pe.matmul(bank[:, 0:cols], lhsT[:, k, rows], w[:, k, 0:cols],
                                         start=(n == 0 and k == 0), stop=(n == 2 and k == KC - 1))
                z_put(last, name)

            def transposes(src, kind, tiles=range(TILES)):
                for t in tiles:
                    for h in range(2):
                        name = f"{kind}{t}{h}"
                        bank = t_open(name)
                        for i in range(4):
                            k = 4 * h + i
                            last = pe.transpose(bank[:, i * P:(i + 1) * P], src[:, t, k * P:(k + 1) * P], ident[:, :])
                        t_put(last, name)

            def ada(j):
                w = weights(f"ada{j}")
                bank = banks[4 + j % 2] if j < 11 else z_open("part11")
                if 2 <= j < 11:
                    pe.wait_ge(ev("part_out"), j - 1)
                for a in range(2):
                    for q in range(NQT):
                        last = pe.matmul(bank[q * QR:(q + 1) * QR, :], crep[:, 4 * a + q, :],
                                         w[:, 4 * a + q, :], start=(a == 0), stop=(a == 1), skip_group_check=True)
                last.then_inc(ev("ada_made") if j < 11 else z_full[z_use("part11")[0]], 1)

            def ada_rows(j, out):
                if j < 11:
                    pe.wait_ge(ev("part_out"), j + 1)
                else:
                    z_gone(pe, "part11")
                for q in range(NQT):
                    last = pe.matmul(out[q * QR:(q + 1) * QR, :], quarter_head[:, :], part(j)[:, q * P:(q + 1) * P],
                                     start=True, stop=True, skip_group_check=True)
                return last

            def late_rows(j):
                bank = z_open(f"am{j}")
                z_put(ada_rows(j, bank[:, 0:P]), f"am{j}")

            h_parts, ya_parts, yb_parts, m_parts = ((hT_lower, upper_a), (yaT_lower, upper_b), (ybT_lower, upper_a),
                                                     (hT_lower, upper_b))

            pe.wait_ge(ev("consts"), 3)
            pe.wait_ge(ev("xn_ready"), TILES)
            for t in range(TILES):
                for h in range(2):
                    name = f"xT{t}{h}"
                    bank = z_open(name)
                    for i in range(4):
                        k = 4 * h + i
                        last = pe.transpose(bank[:, i * P:(i + 1) * P], h2[:, t, k * P:(k + 1) * P], ident[:, :])
                    z_put(last, name)
            pe.wait_ge(ev("crep_ready"), 1)
            pe.wait_ge(ev("heads_ready"), 1)
            for j in range(4):
                ada(j)
                ada_rows(j, banks[6][:, j * P:(j + 1) * P]).then_inc(ev("rows_made"), 1)
            pe.wait_ge(ev("ada_added"), 1)
            for j in range(4):
                last = pe.transpose(banks[5][:, j * P:(j + 1) * P], mod[:, j, :], ident[:, :])
            last.then_inc(ev("modT_done"), 1)
            for n, item in enumerate(("v0", "v1", "u0", "u1")):
                pe.wait_ge(ev("hT_parts"), 1)
                rows_times(item, 0, h_parts)
                pe.wait_ge(ev("hT_parts"), 2)
                if n:
                    late_rows(n + 3)
                rows_times(item, 1, h_parts)
                ada(n + 4)
                if n == 0:
                    pe.wait_ge(ev("ws_masked"), 1)
                    for h in range(2):
                        name = f"ws{h}"
                        bank = t_open(name)
                        for i in range(4):
                            last = pe.transpose(bank[:, i * P:(i + 1) * P], ws[:, 4 * h + i, :], ident[:, :])
                        t_put(last, name)
            for h in range(2):
                t_gone(pe, f"ws{h}")
            pe.wait_ge(ev("vn_ready"), TILES)
            for t in range(TILES):
                for h in range(2):
                    name = f"f{t}{h}"
                    bank = z_open(name)
                    for i in range(4):
                        last = pe.matmul(bank[:, i * P:(i + 1) * P], wsT[:, 4 * h + i, :],
                                         v_buf[:, t, (4 * h + i) * P:(4 * h + i + 1) * P], start=True, stop=True,
                                         skip_group_check=True)
                    z_put(last, name)
            late_rows(7)
            for t in range(TILES):
                rows_times("q0", t, h_parts)
            for t in range(TILES):
                for h in range(2):
                    z_gone(pe, f"f{t}{h}")
            transposes(u_buf, "ya")
            ada(8)
            rows_times("q1", 0, h_parts)
            late_rows(8)
            rows_times("q1", 1, h_parts)
            ada(9)
            rows_times("kv", 0, h_parts, 2 * P)
            late_rows(9)
            rows_times("kv", 1, h_parts, 2 * P)
            ada(10)
            rows_times("ga0", 0, h_parts)
            late_rows(10)
            pe.wait_ge(ev("rope_ready"), TILES)
            transposes(q_buf, "q")
            bank = t_open("k")
            for g in range(NKV):
                for t in range(TILES):
                    last = pe.transpose(bank[:, g * S + t * P:g * S + (t + 1) * P],
                                        kd[:, t, g, :, :].rearrange("p u d -> p (u d)"), ident[:, :])
            t_put(last, "k")
            rows_times("ga0", 1, h_parts)

            def scores(n):
                if n == 0:
                    for t in range(TILES):
                        for h in range(2):
                            t_gone(pe, f"q{t}{h}")
                    t_gone(pe, "k")
                    pe.wait_ge(ev("part_out"), 11)
                else:
                    pe.wait_ge(ev("exp_done"), 9 * n)
                for g in range(NKV):
                    for j in range(2):
                        for r in range(2):
                            rows = slice(r * CH, (r + 1) * CH)
                            col = (2 * g + j) * P
                            lhsT = qT[rows, n, 4 * g + 2 * j:4 * g + 2 * j + 2, :].rearrange("p k q -> p (k q)")
                            if n == 0:
                                parts = [(0, 0, CH)]
                            elif n % 2:
                                parts = [(0, (n - 1) * CH, P)]
                            else:
                                parts = [(0, n * CH, CH), (CH, (n - 1) * CH, CH)]
                            for off, key, width in parts:
                                last = pe.matmul(banks[4 + r][:, col + off:col + off + width], lhsT,
                                                 kT[rows, g, key:key + width], start=True, stop=True,
                                                 skip_group_check=True)
                last.then_inc(ev("s_done"), 1)

            def probs_T(n):
                keys = CH if n == 0 else P
                pe.wait_ge(ev("p_norm"), n + 1)
                for r in range(2):
                    name = f"p{n}{r}"
                    bank = t_open(name)
                    for g in range(4):
                        last = pe.transpose(bank[0:keys, g * P:(g + 1) * P], probs[:, r, g, 0:keys], ident[:, :])
                    t_put(last, name)

            def attend(n):
                keys = CH if n == 0 else P
                for r in range(2):
                    t_gone(pe, f"p{n}{r}")
                if n % 2 == 0 and n:
                    pe.wait_ge(ev("vp_ready"), 1)
                name = f"o{n}"
                bank = t_open(name)
                for g in range(NKV):
                    for r in range(2):
                        cols = slice(g * CH, (g + 1) * CH)
                        v = vp[0:keys, cols] if n % 2 == 0 and n else kv[0:keys, n // 2, P + g * CH:P + (g + 1) * CH]
                        last = pe.matmul(bank[r * CH:(r + 1) * CH, g * 256:(g + 1) * 256], v,
                                         probsT[0:keys, r, 2 * g:2 * g + 2, :].rearrange("p g n -> p (g n)"),
                                         start=True, stop=True, skip_group_check=True)
                t_put(last, name)

            scores(0)
            rows_times("ga1", 0, h_parts)
            ada(11)
            probs_T(0)
            scores(1)
            rows_times("ga1", 1, h_parts)
            late_rows(11)
            attend(0)
            rows_times("gb0", 0, h_parts)
            probs_T(1)
            scores(2)
            rows_times("gb0", 1, h_parts)
            attend(1)
            rows_times("gb1", 0, h_parts)
            probs_T(2)
            scores(3)
            rows_times("gb1", 1, h_parts)
            attend(2)
            pe.wait_ge(ev("yaT_parts"), 1)
            rows_times("oa0", 0, ya_parts)
            probs_T(3)
            rows_times("oa0", 1, ya_parts)
            attend(3)
            for t in range(TILES):
                rows_times("oa1", t, ya_parts)
            pe.wait_ge(ev("ybT_parts"), 1)
            for item in ("ob0", "ob1"):
                for t in range(TILES):
                    rows_times(item, t, yb_parts)
            z_gone(pe, "am11")

            def to_all(segments):
                for s in segments:
                    for h in range(2):
                        name = f"bc{s}{h}"
                        bank = z_open(name)
                        for q in range(NQT):
                            last = pe.matmul(bank[:, q * P:(q + 1) * P], row_sel[:, q, :], mod[:, 2 * s + h, :],
                                             start=True, stop=True, skip_group_check=True)
                        z_put(last, name)
            to_all((2, 3))
            pe.wait_ge(ev("merged_ready"), 2 * TILES)
            transposes(merged, "m")
            to_all((4, 5))
            for t in range(TILES):
                pe.wait_ge(ev("mT_parts"), t + 1)
                for item in ("out0", "out1"):
                    rows_times(item, t, m_parts)

            for t in range(TILES):
                pe.wait_ge(ev("h2_ready"), t + 1)
                transposes(h2, "h", [t])
            pe.wait_ge(route_in, 32)
            for t in range(TILES):
                for h in range(2):
                    t_gone(pe, f"h{t}{h}")
            bank = z_open("logit_parts")
            for a in range(2):
                for q in range(NQT):
                    last = pe.matmul(bank[q * QR:(q + 1) * QR, 0:S], wr[:, 4 * a + q, :], h2T[:, 4 * a + q, :],
                                     start=(a == 0), stop=(a == 1), skip_group_check=True)
            z_put(last, "logit_parts")
            z_gone(pe, "logit_parts")
            bank = z_open("logits")
            for t in range(TILES):
                last = pe.matmul(bank[:, t * E:(t + 1) * E], logit_parts[:, t * P:(t + 1) * P], quarter_ident[:, :],
                                 start=True, stop=True, skip_group_check=True)
            z_put(last, "logits")
            pe.wait_ge(ev("mask_ready"), 1)
            bank = z_open("rank")
            pe.matmul(bank[:, 0:E], tri, mask[:, 0, :], start=True, stop=True, skip_group_check=True)
            pe.matmul(bank[:, E:2 * E], tri, mask[:, 1, :], start=True, stop=False, skip_group_check=True)
            pe.matmul(bank[:, E:2 * E], ones, mask[:, 0, :], start=False, stop=True, skip_group_check=True)
            for t in range(TILES):
                pe.matmul(bank[:, 2 * E:3 * E], ones, mask[:, t, :], start=(t == 0), stop=(t == 1), skip_group_check=True)
            for t in range(TILES):
                last = pe.matmul(bank[0:E, 2 * P:3 * P], mask[:, t, :], ones, start=(t == 0), stop=(t == 1),
                                 skip_group_check=True)
            z_put(last, "rank")
            pe.wait_ge(ev("gates_ready"), 1)
            bank = t_open("gT")
            for t in range(TILES):
                last = pe.transpose(bank[0:E, t * P:(t + 1) * P], gates[:, t, :], ident[:, :])
            t_put(last, "gT")
            pe.wait_ge(ev("counts_ready"), 1)
            pe.wait_ge(ev("counters"), 5)
            bank = z_open("starts")
            pe.matmul(bank[:, 0:E], nbT, tri_exc[:, 0:E], start=True, stop=True, skip_group_check=True)
            pe.matmul(bank[:, 2 * E:2 * E + 2], tri_exc, nbT[:, 0:2], start=True, stop=True, skip_group_check=True)
            last = pe.matmul(bank[:, 2 * E + 2:2 * E + 4], tri_inc, nbT[:, 0:2], start=True, stop=True,
                             skip_group_check=True)
            z_put(last, "starts")
            pe.wait_ge(ev("cmp_ready"), 1)
            bank = z_open("etab")
            last = pe.matmul(bank[:, 0:GMAX], ones[0:E, :], cmp[0:E, :], start=True, stop=True)
            z_put(last, "etab")

            t_gone(pe, "gT")
            def gather():
                for t in range(TILES):
                    for h in range(NH):
                        last = pe.matmul(banks[6][h * BM:(h + 1) * BM, :], sel[:, t, :], h2[:, t, h * HW:(h + 1) * HW],
                                         start=(t == 0), stop=(t == 1), skip_group_check=True)
                last.then_inc(ev("xg_done"), 1)

            def gather_T():
                for i in range(4):
                    last = pe.transpose(banks[6][:, i * P:(i + 1) * P], xe[:, i * P:(i + 1) * P], ident[:, :])
                last.then_inc(ev("xt_done"), 1)

            def times_down(loaded):
                for k in range(KC):
                    if k % 2 == 0:
                        pe.wait_ge(dn_in[k // 2], loaded)
                    for h in range(NH):
                        last = pe.matmul(banks[7][h * BM:(h + 1) * BM, :], hidT[:, k % 4, k // 4, :],
                                         down[:, k, h * HW:(h + 1) * HW],
                                         start=(k == 0), stop=(k == KC - 1), skip_group_check=True)
                    if k % 2:
                        last.then_inc(ev("down_used"), 1)

            def combine(tiles=range(TILES)):
                for t in tiles:
                    for h in range(NH):
                        rows = slice(h * BM, (h + 1) * BM)
                        for y in (y_upper, y_lower):
                            last = pe.matmul(banks[2 * h + t][:, :], gT[rows, t * P:(t + 1) * P], y[rows, :],
                                             start=False, stop=True, skip_group_check=True)
                last.then_inc(ev("comb_done"), 1)

            pe.wait_ge(ev("sel_ready"), 1)
            gather()
            pe.wait_ge(ev("table_ready"), 1)
            pe.wait_ge(bd_in, 16)
            for h in range(NH):
                for t in range(TILES):
                    last = pe.matmul(banks[2 * h + t][:, :], gatesT[:, t, :], b_down_sb[:, h * HW:(h + 1) * HW],
                                     start=True, stop=True, skip_group_check=True)
            last.then_inc(ev("acc_init"), 1)
            pe.wait_ge(ev("bias_part_ready"), 4)
            pe.wait_ge(ev("xe_ready"), 1)
            gather_T()
            with pe.Fori(0, E // 2) as p:
                for s in range(2):
                    first = pe.value_load(table[0:1, bass.ds(p * 2 + (s + GMAX + E), 1)], min_val=0, max_val=GMAX - 1)
                    blocks = pe.value_load(table[0:1, bass.ds(p * 2 + (s + GMAX), 1)], min_val=1, max_val=S // BM)
                    with pe.Fori(0, blocks) as b:
                        g = first + b
                        pe.wait_ge(ev("xT_ready"), g + 1)
                        pe.wait_ge(ev("hot_ready"), g + 1)
                        for k in range(KC):
                            if k % 2 == 0:
                                pe.wait_ge(gu_in[s][k // 2], p * 16 + 16)
                            for a in range(2):
                                if k == 0 and a == 1:
                                    pe.wait_ge(ev("gT_ready"), g + 1)
                                for h in range(NH):
                                    last = pe.matmul(banks[4 + a][h * BM:(h + 1) * BM, :], xT[:, k % 4, k // 4, :],
                                                     gate_up[s][:, k, a * FF + h * HW:a * FF + (h + 1) * HW],
                                                     start=(k == 0), stop=(k == KC - 1), skip_group_check=True)
                            if k % 2:
                                last.then_inc(ev("gu_used"), 1)
                            if k == 0:
                                for a in range(2):
                                    for h in range(NH):
                                        pe.matmul(banks[4 + a][h * BM:(h + 1) * BM, :], onehot,
                                                  bias_parts[a][:, h * HW:(h + 1) * HW], start=False, stop=False,
                                                  skip_group_check=True)
                        pe.wait_ge(ev("hidT_ready"), g + 1)
                        loaded = pe.value_load(table[0:1, bass.ds(g + DOWN_AT, 1)], min_val=16, max_val=16 * E)
                        times_down(loaded)
                        pe.wait_ge(ev("sel_ready"), g + 2)
                        gather()
                        pe.wait_ge(ev("y_out"), g * 2 + 2)
                        pe.wait_ge(ev("hid_ready"), g + 1)
                        for i in range(4):
                            last = pe.transpose(banks[7][:, i * P:(i + 1) * P], hid[:, i * P:(i + 1) * P], ident[:, :])
                        last.then_inc(ev("ht_done"), 1)
                        pe.wait_ge(ev("xe_ready"), g + 2)
                        gather_T()
                        pe.wait_ge(ev("y_ready"), g + 1)
                        combine()
                        pe.wait_ge(ev("selg_ready"), g + 1)
                        for t in range(TILES):
                            last = pe.transpose(banks[5][:, t * P:(t + 1) * P], selg[:, t, :], ident[:, :])
                        last.then_inc(ev("gt_done"), 1)
            total = pe.value_load(table[0:1, GMAX + 3 * E:GMAX + 3 * E + 1], min_val=1, max_val=GMAX - 1)
            pe.wait_ge(ev("hidT_ready"), total + 1)
            times_down(16 * E)
            pe.wait_ge(ev("gT_ready"), total + 1)
            pe.wait_ge(ev("y_ready"), total + 1)
            for t in range(TILES):
                combine([t])


_INS = ["x", "c", "positions", "w_ada", "b_ada", "g_norm1", "w_in", "b_in", "ln_v_g", "ln_v_b", "w_spatial",
        "b_spatial", "sinks", "w_o_a", "w_o_b", "w_out", "g_norm2", "w_router", "b_router", "w_gate_up",
        "b_gate_up", "w_down", "b_down", "g_final"]


def kernel(**inputs):
    import numpy as _np
    import concourse.bacc as _bacc
    from concourse import mybir as _mybir
    from concourse.bass_utils import run_bass_kernel_spmd as _run

    nc = _bacc.Bacc("TRN2", target_bir_lowering=False, num_devices=1)
    arrays, args = {}, []
    for name in _INS:
        a = _np.ascontiguousarray(inputs[name])
        arrays[f"in_{name}_dram"] = a
        args.append(nc.dram_tensor(f"in_{name}_dram", a.shape, _mybir.dt.from_np(a.dtype), kind="ExternalInput").ap())
    args.append(nc.dram_tensor("out_dram", (1, S, D), F32, kind="ExternalOutput").ap())
    bass_hybrid_layer(nc, *args)
    r = _run(nc, [arrays], core_ids=[0])
    return r.results[0]["out_dram"]
```
